# Optimizing a Trainium2 kernel written in Bass

```python
import math, functools
import jax, jax.numpy as jnp
from jax import lax
import numpy as np

D_MODEL = 1024
BATCH = 1
SEQ = 1024
DEPTH = 1
DEC_BATCH = 8
DEC_SEQ = 4
PAST_LEN = 2048
PAGE_SIZE = 128

HEAD_DIM = 64
MIX_WIDTH = D_MODEL
DIFF_HEADS = MIX_WIDTH // (4 * HEAD_DIM)
DIFF_WIDTH = DIFF_HEADS * 2 * HEAD_DIM
DIL_WIDTH = MIX_WIDTH - DIFF_WIDTH
DIL_HEADS = DIL_WIDTH // HEAD_DIM
DIL_CONFIGS = ((128, 1), (512, 4), (2048, 16))
MAX_WINDOW = max(w for w, _ in DIL_CONFIGS)
PROJ_WIDTH = 3 * DIFF_WIDTH + 3 * DIL_WIDTH
ROPE_THETA = 10000.0
ATTN_SCALE = HEAD_DIM ** -0.5
Q_BLOCK = 128
N_KEYS = 128
N_EXPERTS = N_KEYS * N_KEYS
PEER_HEADS = 8
PEER_QDIM = 256
PEER_TOPK = 16
PEER_BLOCK = 128
NORM_EPS = 1e-6
SUBLN_EPS = 1e-5
NEG_INF = -1e30

kernel_name = "hymba_diffattn_dilated_peer_adaln_step"

def _rmsnorm(x, g, eps=NORM_EPS):
    xf = x.astype(jnp.float32)
    y = xf * lax.rsqrt(jnp.mean(xf * xf, axis=-1, keepdims=True) + eps) * g.astype(jnp.float32)
    return y.astype(x.dtype)

def _rope(x, pos):
    half = x.shape[-1] // 2
    inv = ROPE_THETA ** (-jnp.arange(half, dtype=jnp.float32) / half)
    ang = pos.astype(jnp.float32)[:, None] * inv[None, :]
    shape = (1, ang.shape[0]) + (1,) * (x.ndim - 3) + (half,)
    cos = jnp.cos(ang).reshape(shape)
    sin = jnp.sin(ang).reshape(shape)
    xf = x.astype(jnp.float32)
    x1, x2 = xf[..., :half], xf[..., half:]
    return jnp.concatenate([x1 * cos - x2 * sin, x2 * cos + x1 * sin], axis=-1).astype(x.dtype)

def _modulation(c, w, b):
    m = jax.nn.silu(c) @ w + b
    return [t[:, None, :] for t in jnp.split(m, 6, axis=-1)]

def _modulate(h, shift, scale):
    return h * (1.0 + scale) + shift

def _project(h, w_in, pos):
    B, S, _ = h.shape
    p = h @ w_in
    cuts = [DIFF_WIDTH, 2 * DIFF_WIDTH, 3 * DIFF_WIDTH, 3 * DIFF_WIDTH + DIL_WIDTH, 3 * DIFF_WIDTH + 2 * DIL_WIDTH]
    qa, ka, va, qb, kb, vb = jnp.split(p, cuts, axis=-1)
    qa = _rope(qa.reshape(B, S, DIFF_HEADS, 2, HEAD_DIM), pos)
    ka = _rope(ka.reshape(B, S, DIFF_HEADS, 2, HEAD_DIM), pos)
    va = va.reshape(B, S, DIFF_HEADS, 2 * HEAD_DIM)
    qb = _rope(qb.reshape(B, S, DIL_HEADS, HEAD_DIM), pos)
    kb = _rope(kb.reshape(B, S, DIL_HEADS, HEAD_DIM), pos)
    vb = vb.reshape(B, S, DIL_HEADS, HEAD_DIM)
    return qa, ka, va, qb, kb, vb

def _diff_lambda(lam, layer):
    lam_init = 0.8 - 0.6 * math.exp(-0.3 * layer)
    lf = lam.astype(jnp.float32)
    lam_full = jnp.exp(jnp.sum(lf[0] * lf[1])) - jnp.exp(jnp.sum(lf[2] * lf[3])) + lam_init
    return lam_full, lam_init

def _diff_combine(s, mask, v, lam):
    p = jax.nn.softmax(jnp.where(mask, s, NEG_INF), axis=-1)
    a = p[:, :, 0] - lam * p[:, :, 1]
    return jnp.einsum('bhqk,bkhe->bqhe', a, v.astype(jnp.float32))

def _diff_attn_prompt(q, k, v, lam):
    B, S, H, _, Dh = q.shape
    nb = S // Q_BLOCK
    qblocks = q.reshape(B, nb, Q_BLOCK, H, 2, Dh).swapaxes(0, 1)
    kpos = jnp.arange(S)

    def one(args):
        qblk, start = args
        s = jnp.einsum('bqhcd,bkhcd->bhcqk', qblk, k).astype(jnp.float32) * ATTN_SCALE
        qpos = start + jnp.arange(Q_BLOCK)
        return _diff_combine(s, kpos[None, :] <= qpos[:, None], v, lam)

    o = lax.map(one, (qblocks, jnp.arange(nb) * Q_BLOCK))
    return o.swapaxes(0, 1).reshape(B, S, H, 2 * Dh)

def _diff_attn_sample(q, k_new, v_new, k_pool, v_pool, page_table, lam):
    DB, DS, H, _, Dh = q.shape
    past = page_table.shape[1] * k_pool.shape[1]
    kp = k_pool[page_table].reshape(DB, past, H, 2, Dh)
    vp = v_pool[page_table].reshape(DB, past, H, 2 * Dh)
    k_all = jnp.concatenate([kp, k_new], axis=1)
    v_all = jnp.concatenate([vp, v_new], axis=1)
    s = jnp.einsum('bqhcd,bkhcd->bhcqk', q, k_all).astype(jnp.float32) * ATTN_SCALE
    mask = jnp.arange(past + DS)[None, :] <= past + jnp.arange(DS)[:, None]
    return _diff_combine(s, mask, v_all, lam)

def _dilated_prompt(q, k, v, window, dil):
    B, S, H, Dh = q.shape
    span = window // dil
    L = S // dil
    nb = -(-L // span)
    Lp = nb * span

    def split(a):
        return a.reshape(B, L, dil, H, Dh).transpose(0, 2, 1, 3, 4)

    qs = jnp.pad(split(q), ((0, 0), (0, 0), (0, Lp - L), (0, 0), (0, 0))).reshape(B, dil, nb, span, H, Dh)
    pad_k = ((0, 0), (0, 0), (span, Lp - L), (0, 0), (0, 0))
    kr = jnp.pad(split(k), pad_k).reshape(B, dil, nb + 1, span, H, Dh)
    vr = jnp.pad(split(v), pad_k).reshape(B, dil, nb + 1, span, H, Dh)
    kb = jnp.concatenate([kr[:, :, :-1], kr[:, :, 1:]], axis=3)
    vb = jnp.concatenate([vr[:, :, :-1], vr[:, :, 1:]], axis=3)
    s = jnp.einsum('brnqhd,brnkhd->brnqhk', qs, kb).astype(jnp.float32) * ATTN_SCALE
    qi = jnp.arange(span)[:, None]
    kk = jnp.arange(2 * span)[None, :]
    rel = kk - qi
    blk = jnp.arange(nb)[:, None, None]
    valid = (rel >= 0) & (rel <= span) & (blk * span + kk - span >= 0)
    s = jnp.where(valid[None, None, :, :, None, :], s, NEG_INF)
    m = jnp.max(s, axis=-1)
    p = jnp.exp(s - m[..., None])
    l = jnp.sum(p, axis=-1)
    o = jnp.einsum('brnqhk,brnkhd->brnqhd', p, vb.astype(jnp.float32)) / l[..., None]

    def merge(a):
        a = a.reshape((B, dil, Lp) + a.shape[4:])[:, :, :L]
        a = jnp.moveaxis(a, 1, 2)
        return a.reshape((B, S) + a.shape[3:])

    return merge(o), merge(m), merge(l)

def _dilated_sample(q, k_all, v_all, buf_len, window, dil):
    DS = q.shape[1]
    span = window // dil
    idx = buf_len + jnp.arange(DS)[:, None] - dil * jnp.arange(span + 1)[None, :]
    valid = idx >= 0
    idx = jnp.maximum(idx, 0)
    kg = k_all[:, idx]
    vg = v_all[:, idx]
    s = jnp.einsum('bqhd,bqjhd->bqhj', q, kg).astype(jnp.float32) * ATTN_SCALE
    s = jnp.where(valid[None, :, None, :], s, NEG_INF)
    m = jnp.max(s, axis=-1)
    p = jnp.exp(s - m[..., None])
    l = jnp.sum(p, axis=-1)
    o = jnp.einsum('bqhj,bqjhd->bqhd', p, vg.astype(jnp.float32)) / l[..., None]
    return o, m, l

def _combine_branches(branches):
    M = functools.reduce(jnp.maximum, [m for _, m, _ in branches])
    ws = [l * jnp.exp(m - M) for _, m, l in branches]
    den = functools.reduce(jnp.add, ws)
    num = functools.reduce(jnp.add, [w[..., None] * o for (o, _, _), w in zip(branches, ws)])
    return num / den[..., None]

def _mix_out(oa, ob, subln_g, lam_init, w_o, dtype):
    B, S = oa.shape[:2]
    oa = _rmsnorm(oa, subln_g, SUBLN_EPS) * (1.0 - lam_init)
    o = jnp.concatenate([oa.reshape(B, S, DIFF_WIDTH), ob.reshape(B, S, DIL_WIDTH)], axis=-1).astype(dtype)
    return o @ w_o

def _peer(h, wq, keys, u_tab, v_tab):
    B, S, D = h.shape
    t = h.reshape(B * S, D)
    T = t.shape[0]
    Tp = -(-T // PEER_BLOCK) * PEER_BLOCK
    t = jnp.pad(t, ((0, Tp - T), (0, 0)))

    def one(tb):
        q = (tb @ wq).reshape(PEER_BLOCK, PEER_HEADS, 2, PEER_QDIM // 2)
        s = jnp.einsum('thcd,hcnd->thcn', q, keys).astype(jnp.float32)
        sv, si = lax.top_k(s, PEER_TOPK)
        cand = sv[:, :, 0, :, None] + sv[:, :, 1, None, :]
        cv, ci = lax.top_k(cand.reshape(PEER_BLOCK, PEER_HEADS, PEER_TOPK * PEER_TOPK), PEER_TOPK)
        i1 = jnp.take_along_axis(si[:, :, 0], ci // PEER_TOPK, axis=-1)
        i2 = jnp.take_along_axis(si[:, :, 1], ci % PEER_TOPK, axis=-1)
        e = i1 * N_KEYS + i2
        g = jax.nn.softmax(cv, axis=-1)
        a = jax.nn.gelu(jnp.einsum('td,thkd->thk', tb, u_tab[e]).astype(jnp.float32), approximate=False)
        return jnp.einsum('thk,thkd->td', (g * a).astype(tb.dtype), v_tab[e])

    out = lax.map(one, t.reshape(Tp // PEER_BLOCK, PEER_BLOCK, D))
    return out.reshape(Tp, D)[:T].reshape(B, S, D)

def setup_inputs(seed: int = 0) -> dict:
    key = jax.random.key(seed)
    ks = jax.random.split(key, 24)
    f32 = jnp.float32
    n_pages = PAST_LEN // PAGE_SIZE
    n_used = DEC_BATCH * n_pages
    n_pool = n_used + max(1, n_used // 4)
    win_buf = min(MAX_WINDOW, PAST_LEN)

    def nrm(k, shape, s=1.0):
        return jax.random.normal(k, shape, f32) * s

    page_table = jax.random.permutation(ks[6], n_pool)[:n_used].reshape(DEC_BATCH, n_pages).astype(jnp.int32)
    return {
        "x_prompt": nrm(ks[0], (BATCH, SEQ, D_MODEL)),
        "x_sample": nrm(ks[1], (DEC_BATCH, DEC_SEQ, D_MODEL)),
        "cache_k_diff": nrm(ks[2], (DEPTH, n_pool, PAGE_SIZE, DIFF_HEADS, 2 * HEAD_DIM)),
        "cache_v_diff": nrm(ks[3], (DEPTH, n_pool, PAGE_SIZE, DIFF_HEADS, 2 * HEAD_DIM)),
        "state_k_win": nrm(ks[4], (DEPTH, DEC_BATCH, win_buf, DIL_HEADS, HEAD_DIM)),
        "state_v_win": nrm(ks[5], (DEPTH, DEC_BATCH, win_buf, DIL_HEADS, HEAD_DIM)),
        "page_table": page_table,
        "c_prompt": nrm(ks[7], (BATCH, D_MODEL)),
        "c_sample": nrm(ks[8], (DEC_BATCH, D_MODEL)),
        "ada_w": nrm(ks[9], (DEPTH, D_MODEL, 6 * D_MODEL), D_MODEL ** -0.5),
        "ada_b": nrm(ks[10], (DEPTH, 6 * D_MODEL), 0.01),
        "norm_attn_g": 1.0 + nrm(ks[11], (DEPTH, D_MODEL), 0.01),
        "norm_ffn_g": 1.0 + nrm(ks[12], (DEPTH, D_MODEL), 0.01),
        "w_in": nrm(ks[13], (DEPTH, D_MODEL, PROJ_WIDTH), D_MODEL ** -0.5),
        "w_o": nrm(ks[14], (DEPTH, MIX_WIDTH, D_MODEL), MIX_WIDTH ** -0.5),
        "diff_lambda": nrm(ks[15], (DEPTH, 4, HEAD_DIM), 0.1),
        "diff_subln_g": 1.0 + nrm(ks[16], (DEPTH, 2 * HEAD_DIM), 0.01),
        "peer_wq": nrm(ks[17], (DEPTH, D_MODEL, PEER_HEADS * PEER_QDIM), D_MODEL ** -0.5),
        "peer_keys": nrm(ks[18], (DEPTH, PEER_HEADS, 2, N_KEYS, PEER_QDIM // 2), (PEER_QDIM // 2) ** -0.5),
        "peer_u": nrm(ks[19], (DEPTH, N_EXPERTS, D_MODEL), D_MODEL ** -0.5),
        "peer_v": nrm(ks[20], (DEPTH, N_EXPERTS, D_MODEL), PEER_HEADS ** -0.5),
        "final_norm_g": 1.0 + nrm(ks[21], (D_MODEL,), 0.01),
    }

def reference(x_prompt, x_sample, cache_k_diff, cache_v_diff, state_k_win, state_v_win, page_table,
              c_prompt, c_sample, ada_w, ada_b, norm_attn_g, norm_ffn_g, w_in, w_o, diff_lambda,
              diff_subln_g, peer_wq, peer_keys, peer_u, peer_v, final_norm_g):
    B, S, _ = x_prompt.shape
    DB, DS, _ = x_sample.shape
    past = page_table.shape[1] * cache_k_diff.shape[2]
    buf_len = state_k_win.shape[2]
    pos_p = jnp.arange(S)
    pos_s = past + jnp.arange(DS)
    xp, xs = x_prompt, x_sample
    kdp, vdp, kwp, vwp, kds, vds, kws, vws = [], [], [], [], [], [], [], []
    for l in range(DEPTH):
        lam, lam_init = _diff_lambda(diff_lambda[l], l)
        mp = _modulation(c_prompt, ada_w[l], ada_b[l])
        ms = _modulation(c_sample, ada_w[l], ada_b[l])

        hp = _modulate(_rmsnorm(xp, norm_attn_g[l]), mp[0], mp[1])
        qa, ka, va, qb, kb, vb = _project(hp, w_in[l], pos_p)
        oa = _diff_attn_prompt(qa, ka, va, lam)
        ob = _combine_branches([_dilated_prompt(qb, kb, vb, w, d) for w, d in DIL_CONFIGS])
        xp = xp + mp[2] * _mix_out(oa, ob, diff_subln_g[l], lam_init, w_o[l], xp.dtype)
        wlen = min(MAX_WINDOW, S)
        kdp.append(ka.reshape(B, S, DIFF_HEADS, 2 * HEAD_DIM))
        vdp.append(va)
        kwp.append(kb[:, S - wlen:])
        vwp.append(vb[:, S - wlen:])

        hs = _modulate(_rmsnorm(xs, norm_attn_g[l]), ms[0], ms[1])
        qa, ka, va, qb, kb, vb = _project(hs, w_in[l], pos_s)
        oa = _diff_attn_sample(qa, ka, va, cache_k_diff[l], cache_v_diff[l], page_table, lam)
        k_all = jnp.concatenate([state_k_win[l], kb], axis=1)
        v_all = jnp.concatenate([state_v_win[l], vb], axis=1)
        ob = _combine_branches([_dilated_sample(qb, k_all, v_all, buf_len, w, d) for w, d in DIL_CONFIGS])
        xs = xs + ms[2] * _mix_out(oa, ob, diff_subln_g[l], lam_init, w_o[l], xs.dtype)
        keep = min(MAX_WINDOW, buf_len + DS)
        kds.append(ka.reshape(DB, DS, DIFF_HEADS, 2 * HEAD_DIM))
        vds.append(va)
        kws.append(k_all[:, buf_len + DS - keep:])
        vws.append(v_all[:, buf_len + DS - keep:])

        xp = xp + mp[5] * _peer(_modulate(_rmsnorm(xp, norm_ffn_g[l]), mp[3], mp[4]),
                                peer_wq[l], peer_keys[l], peer_u[l], peer_v[l])
        xs = xs + ms[5] * _peer(_modulate(_rmsnorm(xs, norm_ffn_g[l]), ms[3], ms[4]),
                                peer_wq[l], peer_keys[l], peer_u[l], peer_v[l])

    y_prompt = _rmsnorm(xp, final_norm_g)
    y_sample = _rmsnorm(xs, final_norm_g)
    return (y_prompt, y_sample, jnp.stack(kdp), jnp.stack(vdp), jnp.stack(kwp), jnp.stack(vwp),
            jnp.stack(kds), jnp.stack(vds), jnp.stack(kws), jnp.stack(vws))


_drawn_inputs = setup_inputs


def setup_inputs(seed=0):
    import zlib

    import numpy as np

    out = dict(_drawn_inputs(seed))
    spreads = {}
    factors = {'ada_b': 3.217,
     'norm_attn_g': 6.442,
     'norm_ffn_g': 23.991,
     'diff_subln_g': 38.915,
     'final_norm_g': 29.862}
    for name, (base, spread) in spreads.items():
        noise = np.random.default_rng([zlib.crc32(name.encode()), seed]).standard_normal(out[name].shape)
        drawn = base * np.exp(spread * noise) if base else spread * noise
        out[name] = __import__('jax').numpy.asarray(drawn.astype(out[name].dtype))
    for name, factor in factors.items():
        out[name] = (out[name] * factor).astype(out[name].dtype)
    return out
```

```python
import math
from contextlib import ExitStack

import concourse.bass as bass
import numpy as np
from concourse import mybir

ACT = mybir.ActivationFunctionType
ALU = mybir.AluOpType
AX = mybir.AxisListType
F32 = mybir.dt.float32
F32R = mybir.dt.float32r
U32 = mybir.dt.uint32
I32 = mybir.dt.int32
ds = bass.ds

P = 128
D = 1024
KC = D // P
TP = 1024
NT = TP // P
NSEQ, SQ = 8, 4
TS = NSEQ * SQ
T = TP + TS
GROUP = 512
PROJ = 6 * GROUP
HD = 64
CH = GROUP // P
PAST = 2048
PAGES = PAST // P
NCOND = 1 + NSEQ
NMOD = 6 * KC
SCALE = HD ** -0.5
NEG = -1e30
LAM_INIT = 0.8 - 0.6 * math.exp(-0.3 * 0)
EPS, SUBLN_EPS = 1e-6, 1e-5
NK = 128
PH = 8
TOPK = 16
NHC = 2 * PH
SHIFT1, SCALE1, GATE1, SHIFT2, SCALE2, GATE2 = range(6)


class Steps:

    def __init__(self, nc, name):
        self.sem, self.base, self.n, self.per = nc.alloc_semaphore(name), 0, 0, 0

    def now(self):
        return self.base + self.n

    def turn(self, i, per):
        self.start, self.n, self.per = self.now(), 0, per
        self.base = self.start + i * per

    def turned(self, turns):
        assert self.n == self.per, (self.n, self.per)
        self.base, self.n = self.start + turns * self.per, 0


def step(eng, steps, instruction):
    instruction.then_inc(steps.sem, 1)
    steps.n += 1
    eng.wait_ge(steps.sem, steps.now())


def hold(eng, passed):
    eng.sem_inc(passed, 1)


def host_tables():
    half = HD // 2
    inv = (np.float32(10000.0) ** (-np.arange(half, dtype=np.float32) / np.float32(half))).astype(np.float32)
    pos = np.concatenate([np.arange(TP), np.tile(PAST + np.arange(SQ), NSEQ)]).astype(np.float32)
    ang = (pos[:, None] * inv[None, :]).astype(np.float32)
    cos, sin = np.cos(ang), np.sin(ang)
    rope = np.concatenate([cos, cos, -sin, sin], axis=1).astype(np.float32)

    def count(back):
        n = sum(((back % d == 0) & (back <= w)).astype(np.float64) for w, d in ((128, 1), (512, 4), (2048, 16)))
        return np.where((back >= 0) & (n > 0), np.log(np.maximum(n, 1)), NEG)

    def causal(back):
        return np.where(back >= 0, 0.0, NEG)

    back = np.arange(P)[:, None] + (TP - P) - np.arange(TP)[None, :]
    prompt_bias = np.stack([f(back) / SCALE for f in (causal, count)], axis=1).astype(np.float32)
    row = np.arange(2 * CH * SQ) % SQ
    back = PAST + row[:, None] - np.arange(PAST + SQ)[None, :]
    sample_bias = np.stack([f(back) / SCALE for f in (causal, count)], axis=1).astype(np.float32)
    second = (np.arange(2 * CH * SQ) // SQ % 2).astype(np.float32)
    halves = np.stack([1 - second, second], axis=1).astype(np.float32)
    return {
        "t_ident": np.eye(P, dtype=np.float32),
        "t_rope": rope,
        "t_prompt_bias": prompt_bias,
        "t_sample_bias": sample_bias,
        "t_halves": halves,
        "t_iota": np.broadcast_to(np.arange(NK, dtype=np.float32), (P, NK)).copy(),
    }


def modulation(nc, io, keep):
    NB = NMOD // CH
    with ExitStack() as ctx:
        def sb(name, shape, dt=F32):
            return ctx.enter_context(nc.sbuf_tensor(name, shape, dt))

        crow = sb("m_crow", [NCOND, D])
        csilu = sb("m_csilu", [NCOND, D])
        cT = sb("m_cT", [P, KC, NCOND])
        rows = sb("m_rows", [P, P])
        wada = sb("m_wada", [P, 2, KC, GROUP])
        lam = sb("m_lam", [1, 4, HD])
        lprod = sb("m_lprod", [1, HD])
        lsum = sb("m_lsum", [1, 2])
        lexp = sb("m_lexp", [1, 2])
        ldiff = sb("m_ldiff", [1, 1])
        pT = ctx.enter_context(nc.psum_tensor("m_pT", [P, 512], F32))
        pL = ctx.enter_context(nc.psum_tensor("m_pL", [P, 512], F32))
        pM = ctx.enter_context(nc.psum_tensor("m_pM", [P, 2, 512], F32))

        small_in = nc.alloc_semaphore("m_small_in")
        w_in = [nc.alloc_semaphore(f"m_w_in{u}") for u in range(2)]
        silu_done = nc.alloc_semaphore("m_silu_done")
        ones_done = nc.alloc_semaphore("m_ones_done")
        turned = nc.alloc_semaphore("m_turned")
        turned_out = nc.alloc_semaphore("m_turned_out")
        lam_exp = nc.alloc_semaphore("m_lam_exp")
        lam_sum = nc.alloc_semaphore("m_lam_sum")
        lam_one = nc.alloc_semaphore("m_lam_one")
        lam_all = nc.alloc_semaphore("m_lam_all")
        block_done = nc.alloc_semaphore("m_block_done")
        block_out = nc.alloc_semaphore("m_block_out")
        dve = Steps(nc, "m_dve")
        NSMALL = 11
        wview = io["ada_w"][0].rearrange("(k p) n -> p k n", p=P)

        with nc.Block() as block:
            @block.sync
            def _(sp):
                sp.dma_start(crow[0:1, :], io["c_prompt"]).then_inc(small_in, 16)
                sp.dma_start(crow[1:NCOND, :], io["c_sample"]).then_inc(small_in, 16)
                sp.dma_start(rows[0:NMOD, :], io["ada_b"][0].rearrange("(k p) -> k p", p=P)).then_inc(small_in, 16)
                for n, g in enumerate(("norm_attn_g", "norm_ffn_g")):
                    sp.dma_start(rows[NMOD + n * KC:NMOD + (n + 1) * KC, :],
                                 io[g][0].rearrange("(k p) -> k p", p=P)).then_inc(small_in, 16)
                sp.dma_start(rows[NMOD + 2 * KC:NMOD + 3 * KC, :],
                             io["final_norm_g"].rearrange("(k p) -> k p", p=P)).then_inc(small_in, 16)
                sp.dma_start(rows[NMOD + 3 * KC:NMOD + 3 * KC + 1, :], io["diff_subln_g"]).then_inc(small_in, 16)
                sp.dma_start(lam[:], io["diff_lambda"]).then_inc(small_in, 16)
                sp.dma_start(keep.ident[:], io["t_ident"]).then_inc(small_in, 16)
                sp.dma_start(keep.iota[:], io["t_iota"]).then_inc(small_in, 16)
                sp.dma_start(keep.halves[:], io["t_halves"]).then_inc(small_in, 16)
                for u in range(2):
                    sp.dma_start(wada[:, u], wview[:, :, u * GROUP:(u + 1) * GROUP]).then_inc(w_in[u], 16)
                with sp.Fori(1, NB // 2) as i:
                    for u in range(2):
                        sp.wait_ge(block_done, 2 * i + u - 1)
                        sp.dma_start(wada[:, u], wview[:, :, ds((2 * i + u) * GROUP, GROUP)]).then_inc(w_in[u], 16)

            @block.scalar
            def _(act):
                act.wait_ge(small_in, 16 * NSMALL)
                nc.scalar.activation(csilu[:], crow[:], ACT.Silu).then_inc(silu_done, 1)
                act.wait_ge(lam_sum, 2)
                nc.scalar.activation(lexp[:], lsum[:], ACT.Exp).then_inc(lam_exp, 1)

            @block.tensor
            def _(pe):
                pe.wait_ge(silu_done, 1)
                NR = NMOD + 3 * KC + 1
                for k in range(KC):
                    nc.tensor.transpose(pT[:, k * NCOND:(k + 1) * NCOND], csilu[:, k * P:(k + 1) * P],
                                        keep.ident[0:NCOND, 0:NCOND])
                nc.tensor.transpose(pT[:, 128:128 + NR], rows[0:NR, :], keep.ident[0:NR, 0:NR]).then_inc(turned, 1)
                pe.wait_ge(lam_one, 1)
                pe.wait_ge(ones_done, 1)
                nc.tensor.matmul(pL[:, 0:1], keep.ones[0:1, :], ldiff[:], start=True, stop=True).then_inc(lam_all, 1)
                pe.wait_ge(turned_out, 2)
                with pe.Fori(0, NB // 2) as i:
                    for u in range(2):
                        pe.wait_ge(w_in[u], 16 * i + 16)
                        pe.wait_ge(block_out, 2 * i + u + 1)
                        for c in range(CH):
                            for k in range(KC):
                                mm = nc.tensor.matmul(pM[:, u, c * NCOND:(c + 1) * NCOND],
                                                      wada[:, u, k, c * P:(c + 1) * P], cT[:, k, :],
                                                      start=(k == 0), stop=(k == KC - 1))
                        mm.then_inc(block_done, 1)

            @block.vector
            def _(v):
                nc.vector.memset(keep.ones[:], 1.0).then_inc(ones_done, 1)
                v.sem_inc(block_out, 2)
                v.wait_ge(small_in, 16 * NSMALL)
                for n in range(2):
                    nc.vector.tensor_tensor_reduce(lprod[:], lam[:, 2 * n, :], lam[:, 2 * n + 1, :], 1.0, 0.0,
                                                   ALU.mult, ALU.add, lsum[:, n:n + 1]).then_inc(lam_sum, 1)
                    v.wait_ge(lam_sum, n + 1)
                v.wait_ge(lam_exp, 1)
                step(v, dve, nc.vector.tensor_tensor(ldiff[:], lexp[:, 1:2], lexp[:, 0:1], ALU.subtract))
                nc.vector.tensor_scalar(ldiff[:], ldiff[:], -LAM_INIT, None, ALU.add).then_inc(lam_one, 1)
                v.wait_ge(turned, 1)
                nc.vector.tensor_copy(cT[:], pT[:, 0:KC * NCOND].rearrange("p (k s) -> p k s", k=KC)).then_inc(turned_out, 1)
                nc.vector.tensor_copy(keep.param[:], pT[:, 128:128 + NMOD + 3 * KC + 1]).then_inc(turned_out, 1)
                v.wait_ge(lam_all, 1)
                nc.vector.tensor_copy(keep.neglam[:], pL[:, 0:1])
                v.wait_ge(turned_out, 2)
                with v.Fori(0, NB // 2) as i:
                    for u in range(2):
                        v.wait_ge(block_done, 2 * i + u + 1)
                        nc.vector.tensor_tensor(
                            keep.mod[:, ds((2 * i + u) * CH, CH), :],
                            pM[:, u, 0:CH * NCOND].rearrange("p (c s) -> p c s", c=CH),
                            keep.param[:, ds((2 * i + u) * CH, CH)].unsqueeze(2).to_broadcast([P, CH, NCOND]),
                            ALU.add).then_inc(block_out, 1)
                v.wait_ge(block_out, NB + 2)
                for m, out, g in ((SCALE1, keep.gs1, NMOD), (SCALE2, keep.gs2, NMOD + KC)):
                    step(v, dve, nc.vector.tensor_scalar(out[:], keep.mod[:, m * KC:(m + 1) * KC, :], 1.0, None, ALU.add))
                    nc.vector.tensor_tensor(out[:], out[:], keep.param[:, g:g + KC].unsqueeze(2)
                                            .to_broadcast([P, KC, NCOND]), ALU.mult)
                nc.vector.memset(keep.sign[:, 1:2], 1.0)
                step(v, dve, nc.vector.tensor_tensor(keep.sign[:, 0:1], keep.halves[:, 1:2], keep.neglam[0:2 * CH * SQ, :],
                                                     ALU.mult))
                nc.vector.tensor_tensor(keep.sign[:, 0:1], keep.sign[:, 0:1], keep.halves[:, 0:1], ALU.add)


def seq_bcast(vec, k=None):
    return vec.unsqueeze(2).to_broadcast([P, NSEQ, SQ])


def project(nc, io, keep):
    ORDER = (2, 5, 0, 1, 3, 4)
    ROPE = (0, 1, 3, 4)
    with ExitStack() as ctx:
        def sb(name, shape, dt=F32):
            return ctx.enter_context(nc.sbuf_tensor(name, shape, dt))

        win = sb("p_win", [P, KC, PROJ])
        x = sb("p_x", [P, D])
        xn = sb("p_xn", [P, D])
        square = sb("p_square", [P, D])
        ss = sb("p_ss", [P, 1])
        ms = sb("p_ms", [P, 1])
        rms = sb("p_rms", [P, 1])
        rstd = sb("p_rstd", [P, 1])
        hT = sb("p_hT", [P, KC, P])
        rope = sb("p_rope", [P, 2, 2 * HD])
        rows = sb("p_rows", [P, 6, GROUP])
        tA = sb("p_tA", [P, GROUP])
        tB = sb("p_tB", [P, GROUP])
        tp = ctx.enter_context(nc.psum_tensor("p_tp", [P, KC, P], F32))
        pj = ctx.enter_context(nc.psum_tensor("p_pj", [P, 6, GROUP], F32))

        win_in = nc.alloc_semaphore("p_win_in")
        x_in = nc.alloc_semaphore("p_x_in")
        rope_in = nc.alloc_semaphore("p_rope_in")
        squared = nc.alloc_semaphore("p_squared")
        mean_done = nc.alloc_semaphore("p_mean_done")
        root_done = nc.alloc_semaphore("p_root_done")
        rstd_done = nc.alloc_semaphore("p_rstd_done")
        xn_done = nc.alloc_semaphore("p_xn_done")
        turned = nc.alloc_semaphore("p_turned")
        h_done = nc.alloc_semaphore("p_h_done")
        proj_done = nc.alloc_semaphore("p_proj_done")
        rope_rows = nc.alloc_semaphore("p_rope_rows")
        v_rows = nc.alloc_semaphore("p_v_rows")
        stored = nc.alloc_semaphore("p_stored")
        tail = nc.alloc_semaphore("p_tail")
        dve = Steps(nc, "p_dve")
        xp = io["x_prompt"][0]
        xs = io["x_sample"].rearrange("b q d -> (b q) d")
        ks = {1: "k_diff", 2: "v_diff", 4: "k_win", 5: "v_win"}

        def flat(name):
            return io[name].rearrange("l b s h e -> (l b s) (h e)")

        with nc.Block() as block:
            @block.sync
            def _(sp):
                for k in range(KC):
                    sp.dma_start(win[:, k, :], io["w_in"][0, k * P:(k + 1) * P, :]).then_inc(win_in, 16)
                sp.sem_inc(stored, 80)

                def store(i, w, r0):
                    sp.wait_ge(rope_rows, 4 * i + 8)
                    sp.wait_ge(v_rows, 2 * i + 4)
                    sp.dma_start(io["s_proj"][ds(r0, w), :], rows[:w].rearrange("p g n -> p (g n)")).then_inc(stored, 16)

                with sp.Fori(0, NT) as i:
                    store(i, P, i * P)
                    for g, name in ks.items():
                        sp.dma_start(flat(name + "_prompt")[ds(i * P, P), :], rows[:, g]).then_inc(stored, 16)
                store(NT, TS, TP)
                sp.dma_start(flat("k_diff_sample"), rows[:TS, 1]).then_inc(stored, 16)
                sp.dma_start(flat("v_diff_sample"), rows[:TS, 2]).then_inc(stored, 16)
                sp.wait_ge(stored, 80 * (NT + 1) + 48)
                for g, name in ((4, "k_win_sample"), (5, "v_win_sample")):
                    sp.dma_start(io[name][0, :, PAST - SQ:PAST].rearrange("b q h e -> b q (h e)"),
                                 io["s_proj"][TP:T, g * GROUP:(g + 1) * GROUP]
                                 .rearrange("(b q) n -> b q n", b=NSEQ)).then_inc(tail, 16)
                sp.wait_ge(tail, 32)

            @block.gpsimd
            def _(pool):
                pool.dma_start(x[:], xp[0:P, :]).then_inc(x_in, 16)
                pool.dma_start(rope[:, 0], io["t_rope"][0:P, :]).then_inc(rope_in, 16)
                with pool.Fori(1, NT) as i:
                    pool.wait_ge(xn_done, i)
                    pool.dma_start(x[:], xp[ds(i * P, P), :]).then_inc(x_in, 16)
                    pool.wait_ge(rope_rows, 4 * i + 4)
                    pool.dma_start(rope[:, 0], io["t_rope"][ds(i * P, P), :]).then_inc(rope_in, 16)
                pool.wait_ge(xn_done, NT)
                pool.dma_start(x[:TS], xs).then_inc(x_in, 16)
                pool.wait_ge(rope_rows, 4 * NT + 4)
                pool.dma_start(rope[:TS, 0], io["t_rope"][TP:T, :]).then_inc(rope_in, 16)

            @block.scalar
            def _(act):
                act.sem_inc(v_rows, 2)

                def tile(i, w):
                    act.wait_ge(x_in, 16 * i + 16)
                    nc.scalar.activation(square[:w], x[:w], ACT.Square, accum_out=ss[:w]).then_inc(squared, 1)
                    act.wait_ge(mean_done, i + 1)
                    nc.scalar.activation(rms[:w], ms[:w], ACT.Sqrt).then_inc(root_done, 1)
                    act.wait_ge(rstd_done, i + 1)
                    nc.scalar.activation(xn[:w], x[:w], ACT.Copy, scale=rstd[:w]).then_inc(xn_done, 1)
                    for n in range(2):
                        act.wait_ge(turned, 2 * i + n + 1)
                        if w == P:
                            for k in range(4 * n, 4 * n + 4):
                                h = nc.scalar.activation(hT[:, k, :], tp[:, k, :], ACT.Identity,
                                                         bias=keep.mod[:, SHIFT1 * KC + k, 0:1],
                                                         scale=keep.gs1[:, k, 0:1])
                            h.then_inc(h_done, 1)
                    for n, g in enumerate((2, 5)):
                        act.wait_ge(proj_done, 6 * i + n + 1)
                        act.wait_ge(stored, 80 * i + 80)
                        nc.scalar.activation(rows[:w, g], pj[:w, g], ACT.Copy).then_inc(v_rows, 1)

                with act.Fori(0, NT) as i:
                    tile(i, P)
                tile(NT, TS)

            @block.tensor
            def _(pe):
                def tile(i, w):
                    pe.wait_ge(xn_done, i + 1)
                    for k in range(KC):
                        t = nc.tensor.transpose(tp[:, k, :w], xn[:w, k * P:(k + 1) * P], keep.ident[:w, :w])
                        if k % 4 == 3:
                            t.then_inc(turned, 1)
                    pe.wait_ge(h_done, 2 * i + 2)
                    for g in ORDER:
                        if g in ROPE:
                            pe.wait_ge(rope_rows, 4 * i + ROPE.index(g) + 1)
                        else:
                            pe.wait_ge(v_rows, 2 * i + (2, 5).index(g) + 1)
                        for k in range(KC):
                            mm = nc.tensor.matmul(pj[:w, g], hT[:, k, :w], win[:, k, g * GROUP:(g + 1) * GROUP],
                                                  start=(k == 0), stop=(k == KC - 1))
                        mm.then_inc(proj_done, 1)

                pe.wait_ge(win_in, 16 * KC)
                with pe.Fori(0, NT) as i:
                    tile(i, P)
                tile(NT, TS)

            @block.vector
            def _(v):
                v.sem_inc(rope_rows, 4)

                def norm(i, w):
                    v.wait_ge(squared, i + 1)
                    nc.vector.tensor_scalar(ms[:w], ss[:w], 1.0 / D, EPS, ALU.mult, ALU.add).then_inc(mean_done, 1)
                    v.wait_ge(root_done, i + 1)
                    nc.vector.reciprocal(rstd[:w], rms[:w]).then_inc(rstd_done, 1)

                def rotate(i, w):
                    v.wait_ge(rope_in, 16 * i + 16)
                    v.wait_ge(stored, 80 * i + 80)
                    for n, g in enumerate(ROPE):
                        v.wait_ge(proj_done, 6 * i + 3 + n)
                        src = pj[:w, g].rearrange("p (h t e) -> p h t e", t=2, e=HD // 2)
                        a = tA[:w].rearrange("p (h e) -> p h e", e=HD)
                        b = tB[:w].rearrange("p (h t e) -> p h t e", t=2, e=HD // 2)
                        cos = rope[:w, 0, 0:HD].unsqueeze(1).to_broadcast([w, 8, HD])
                        nsin = rope[:w, 0, HD:HD + 32].unsqueeze(1).to_broadcast([w, 8, HD // 2])
                        sin = rope[:w, 0, HD + 32:2 * HD].unsqueeze(1).to_broadcast([w, 8, HD // 2])
                        nc.vector.tensor_tensor(a, pj[:w, g].rearrange("p (h e) -> p h e", e=HD), cos, ALU.mult)
                        nc.vector.tensor_tensor(b[:, :, 0], src[:, :, 1], nsin, ALU.mult)
                        step(v, dve, nc.vector.tensor_tensor(b[:, :, 1], src[:, :, 0], sin, ALU.mult))
                        nc.vector.tensor_tensor(rows[:w, g], tA[:w], tB[:w], ALU.add).then_inc(rope_rows, 1)
                        v.wait_ge(rope_rows, 4 * i + 5 + n)

                with v.Fori(0, NT) as i:
                    dve.turn(i, 4)
                    norm(i, P)
                    rotate(i, P)
                dve.turned(NT)
                norm(NT, TS)
                for n in range(2):
                    v.wait_ge(turned, 2 * NT + n + 1)
                    for k in range(4 * n, 4 * n + 4):
                        hv = hT[:, k, 0:TS].rearrange("p (b q) -> p b q", b=NSEQ)
                        step(v, dve, nc.vector.tensor_tensor(hv, tp[:, k, 0:TS].rearrange("p (b q) -> p b q", b=NSEQ),
                                                             seq_bcast(keep.gs1[:, k, 1:NCOND]), ALU.mult))
                        h = nc.vector.tensor_tensor(hv, hv, seq_bcast(keep.mod[:, SHIFT1 * KC + k, 1:NCOND]), ALU.add)
                    h.then_inc(h_done, 1)
                rotate(NT, TS)


def prompt_attn(nc, io, keep):
    NB = NT
    with ExitStack() as ctx:
        def sb(name, shape, dt=F32):
            return ctx.enter_context(nc.sbuf_tensor(name, shape, dt))

        bias = sb("a_bias", [P, 2, TP])
        qk = sb("a_qk", [P, 2, 2, NB, P])
        vv = sb("a_vv", [P, 2, NB, P])
        qkT = sb("a_qkT", [P, 2, TP])
        S = sb("a_S", [P, 2, 2, TP])
        A = sb("a_A", [P, 2, TP])
        AT = sb("a_AT", [P, NB, P])
        mx = sb("a_mx", [P, 2, 2])
        nmx = sb("a_nmx", [P, 2, 2])
        sums = sb("a_sums", [P, 2, 2])
        rs = sb("a_rs", [P, 2, 2])
        pS = ctx.enter_context(nc.psum_tensor("a_pS", [P, 2, TP], F32))
        pT = ctx.enter_context(nc.psum_tensor("a_pT", [P, NB, P], F32))
        pO = ctx.enter_context(nc.psum_tensor("a_pO", [P, 2, 512], F32))

        bias_in = nc.alloc_semaphore("a_bias_in")
        qk_in = [nc.alloc_semaphore(f"a_qk_in{u}") for u in range(2)]
        v_in = [nc.alloc_semaphore(f"a_v_in{u}") for u in range(2)]
        turned = nc.alloc_semaphore("a_turned")
        turned_out = nc.alloc_semaphore("a_turned_out")
        scored = nc.alloc_semaphore("a_scored")
        max_done = nc.alloc_semaphore("a_max_done")
        exp_done = nc.alloc_semaphore("a_exp_done")
        probs = nc.alloc_semaphore("a_probs")
        probs_turned = nc.alloc_semaphore("a_probs_turned")
        probs_out = nc.alloc_semaphore("a_probs_out")
        mixed = nc.alloc_semaphore("a_mixed")
        mixed_out = nc.alloc_semaphore("a_mixed_out")
        dve = Steps(nc, "a_dve")
        held = nc.alloc_semaphore("a_held")
        NCH = D // P
        view = io["s_proj"][0:TP, :].rearrange("(i p) (g n) -> p i g n", p=P, g=6)

        def units(g):
            return 1 + g

        def each(eng, body, turn=None):
            for g in range(2):
                with eng.Fori(0, CH // 2) as i:
                    if turn:
                        turn(g, i)
                    for u in range(2):
                        c = 2 * i + u
                        body(g, u, c, 2 * g + i, CH * g + c, NB * CH * g + c * (NB * units(g)))
                if turn:
                    turn(g, None)

        with nc.Block() as block:
            @block.sync
            def _(sp):
                sp.dma_start(bias[:], io["t_prompt_bias"]).then_inc(bias_in, 16)

                def load(g, u, c, r, j, m0):
                    sp.wait_ge(turned, 4 * j + 4)
                    for t in range(2):
                        sp.dma_start(qk[:, u, t], view[:, :, 3 * g + t, ds(c * P, P)]).then_inc(qk_in[u], 16)
                    sp.wait_ge(mixed_out, NB * j + 2)
                    sp.dma_start(vv[:, u], view[:, :, 3 * g + 2, ds(c * P, P)]).then_inc(v_in[u], 16)
                each(sp, load)

            @block.tensor
            def _(pe):
                pe.sem_inc(turned, 8)
                pe.sem_inc(probs_turned, 1)

                def scores(i, j):
                    w = (i + 1) * P
                    for s in range(2):
                        pe.wait_ge(max_done, 2 * NB * j + 2 * i + s + 1)
                        for c0 in range(0, w, 512):
                            c1 = min(w, c0 + 512)
                            mm = nc.tensor.matmul(pS[:, s, c0:c1], qkT[HD * s:HD * s + HD, 0, i * P:(i + 1) * P],
                                                  qkT[HD * s:HD * s + HD, 1, c0:c1], start=True, stop=True)
                        mm.then_inc(scored, 1)

                def chunk(g, u, c, r, j, m0):
                    pe.wait_ge(qk_in[u], 32 * r + 32)
                    for n in range(4):
                        if n >= 2:
                            pe.wait_ge(turned_out, 4 * j + n - 1)
                        for k in range(4 * (n % 2), 4 * (n % 2) + 4):
                            tr = nc.tensor.transpose(pT[:, k, :], qk[:, u, n // 2, k, :], keep.ident[:])
                        tr.then_inc(turned, 1)
                    pe.wait_ge(turned_out, 4 * j + 4)
                    scores(0, j)
                    pe.wait_ge(v_in[u], 16 * r + 16)
                    for i in range(NB):
                        for s in range(units(g)):
                            m = m0 + i * units(g) + s
                            pe.wait_ge(probs, m + 1)
                            pe.wait_ge(probs_out, m + 1)
                            for k in range(i + 1):
                                tr = nc.tensor.transpose(pT[:, k, :], A[:, s, k * P:(k + 1) * P], keep.ident[:])
                            tr.then_inc(probs_turned, 1)
                            if i + 1 < NB and s == 0:
                                scores(i + 1, j)
                            pe.wait_ge(probs_out, m + 2)
                            pe.wait_ge(mixed_out, NB * j + i + 9)
                            for k in range(i + 1):
                                mm = nc.tensor.matmul(pO[:, i % 2, s * P:(s + 1) * P], vv[:, u, k, :], AT[:, k, :],
                                                      start=(k == 0), stop=(k == i))
                            mm.then_inc(mixed, 1)
                each(pe, chunk)

            @block.vector
            def _(v):
                v.sem_inc(max_done, 2)
                v.sem_inc(mixed_out, 10)
                v.wait_ge(bias_in, 16)

                def maxima(i, g, j):
                    w, e = (i + 1) * P, i % 2
                    for s in range(2):
                        v.wait_ge(scored, 2 * NB * j + 2 * i + s + 1)
                        hold(v, held)
                        step(v, dve, nc.vector.tensor_tensor_reduce(
                            S[:, e, s, 0:w], pS[:, s, 0:w], bias[:, g, TP - w:TP], SCALE, -3e38,
                            ALU.add, ALU.max, mx[:, e, s:s + 1]))
                        nc.vector.tensor_scalar(nmx[:, e, s:s + 1], mx[:, e, s:s + 1], -1.0, None,
                                                ALU.mult).then_inc(max_done, 1)

                def chunk(g, u, c, r, j, m0):
                    for n in range(4):
                        v.wait_ge(turned, 4 * j + n + 9)
                        b = 4 * (n % 2)
                        nc.vector.tensor_copy(qkT[:, n // 2, b * P:(b + 4) * P],
                                              pT[:, b:b + 4, :].rearrange("p k q -> p (k q)")).then_inc(turned_out, 1)
                    maxima(0, g, j)
                    for i in range(NB):
                        w, e = (i + 1) * P, i % 2
                        for s in range(2):
                            v.wait_ge(exp_done, 2 * NB * j + 2 * i + s + 1)
                            step(v, dve, nc.vector.reciprocal(rs[:, e, s:s + 1], sums[:, e, s:s + 1]))
                        if g == 0:
                            step(v, dve, nc.vector.tensor_scalar(rs[:, e, 1:2], rs[:, e, 1:2], keep.neglam[:, 0:1],
                                                                 None, ALU.mult))
                            v.wait_ge(probs_turned, m0 + i + 1)
                            step(v, dve, nc.vector.tensor_scalar(A[:, 0, 0:w], S[:, e, 0, 0:w], rs[:, e, 0:1], None,
                                                                 ALU.mult))
                            nc.vector.scalar_tensor_tensor(out=A[:, 0, 0:w], in0=S[:, e, 1, 0:w],
                                                           scalar=rs[:, e, 1:2], in1=A[:, 0, 0:w], op0=ALU.mult,
                                                           op1=ALU.add).then_inc(probs, 1)
                        else:
                            for s in range(2):
                                v.wait_ge(probs_turned, m0 + 2 * i + 1)
                                nc.vector.tensor_scalar(A[:, s, 0:w], S[:, e, s, 0:w], rs[:, e, s:s + 1], None,
                                                        ALU.mult).then_inc(probs, 1)
                        if i + 1 < NB:
                            maxima(i + 1, g, j)
                        v.wait_ge(mixed, m0 + (i + 1) * units(g))
                        dst = keep.OT[:, ds(j, 1), i * P:(i + 1) * P]
                        if g == 0:
                            nc.vector.tensor_copy(dst, pO[:, e, 0:P].unsqueeze(1)).then_inc(mixed_out, 1)
                        else:
                            nc.vector.tensor_copy(dst[0:HD], pO[0:HD, e, 0:P].unsqueeze(1))
                            nc.vector.tensor_copy(dst[HD:P], pO[HD:P, e, P:2 * P].unsqueeze(1)).then_inc(mixed_out, 1)

                def turn(g, i):
                    if i is None:
                        dve.turned(CH // 2)
                    else:
                        dve.turn(i, 2 * NB * (6 - 2 * g))
                each(v, chunk, turn)

            @block.scalar
            def _(act):
                act.sem_inc(probs_out, 1)

                def exps(i, j):
                    w, e = (i + 1) * P, i % 2
                    for s in range(2):
                        act.wait_ge(max_done, 2 * NB * j + 2 * i + s + 3)
                        nc.scalar.activation(S[:, e, s, 0:w], S[:, e, s, 0:w], ACT.Exp, bias=nmx[:, e, s:s + 1],
                                             accum_out=sums[:, e, s:s + 1]).then_inc(exp_done, 1)

                def chunk(g, u, c, r, j, m0):
                    exps(0, j)
                    for i in range(NB):
                        for s in range(units(g)):
                            act.wait_ge(probs_turned, m0 + i * units(g) + s + 2)
                            nc.scalar.activation(AT[:, 0:i + 1, :], pT[:, 0:i + 1, :], ACT.Copy).then_inc(probs_out, 1)
                            if i + 1 < NB and s == 0:
                                exps(i + 1, j)
                each(act, chunk)


def sample_attn(nc, io, keep):
    R = 2 * CH * SQ
    PG = 4
    NG = PAGES // PG
    ITEMS = NG * CH
    with ExitStack() as ctx:
        def sb(name, shape, dt=F32):
            return ctx.enter_context(nc.sbuf_tensor(name, shape, dt))

        bias = sb("s_bias", [R, 2, PAST + SQ])
        pages = sb("s_pages", [1, NSEQ * PAGES], I32)
        new = sb("s_new", [TS, PROJ])
        vnew = sb("s_vnew", [SQ, 2, GROUP])
        newT = sb("s_newT", [P, 2, 2 * CH, TS])
        kk = sb("s_kk", [P, 2, PG, GROUP])
        vv = sb("s_vv", [P, 2, PAGES, GROUP])
        kT = sb("s_kT", [P, 2, GROUP])
        qd = sb("s_qd", [P, 2, CH * (R + 2 * SQ)])
        S = sb("s_S", [R, 2, PAST + SQ])
        AT = sb("s_AT", [P, PAGES, R])
        ATn = sb("s_ATn", [SQ, R])
        mx = sb("s_mx", [R, 2])
        nmx = sb("s_nmx", [R, 1])
        sums = sb("s_sums", [R, 1])
        rs = sb("s_rs", [R, 1])
        pK = ctx.enter_context(nc.psum_tensor("s_pK", [P, 2, 512], F32))
        pS = ctx.enter_context(nc.psum_tensor("s_pS", [P, PAST], F32))
        pN = ctx.enter_context(nc.psum_tensor("s_pN", [P, 512], F32))
        pA = ctx.enter_context(nc.psum_tensor("s_pA", [P, 512], F32))

        small_in = nc.alloc_semaphore("s_small_in")
        new_turned = nc.alloc_semaphore("s_new_turned")
        new_out = nc.alloc_semaphore("s_new_out")
        k_in = [nc.alloc_semaphore(f"s_k_in{n}") for n in range(2)]
        v_in = [nc.alloc_semaphore(f"s_v_in{g}") for g in range(2)]
        k_turned = nc.alloc_semaphore("s_k_turned")
        k_out = [nc.alloc_semaphore(f"s_k_out{n}") for n in range(2)]
        scored = nc.alloc_semaphore("s_scored")
        zeroed = nc.alloc_semaphore("s_zeroed")
        qd_done = nc.alloc_semaphore("s_qd_done")
        max_done = nc.alloc_semaphore("s_max_done")
        exp_done = nc.alloc_semaphore("s_exp_done")
        rs_done = nc.alloc_semaphore("s_rs_done")
        probs = nc.alloc_semaphore("s_probs")
        probs_turned = nc.alloc_semaphore("s_probs_turned")
        probs_out = nc.alloc_semaphore("s_probs_out")
        mixed = nc.alloc_semaphore("s_mixed")
        mixed_out = nc.alloc_semaphore("s_mixed_out")
        dve = Steps(nc, "s_dve")
        held = [nc.alloc_semaphore(f"s_held{n}") for n in range(3)]
        pools = [io[n][0].rearrange("n r h e -> n r (h e)") for n in ("cache_k_diff", "cache_v_diff")]
        states = [io[n][0].rearrange("b r h e -> b r (h e)") for n in ("state_k_win", "state_v_win")]
        NPOOL = pools[0].shape[0]

        def piped(front, back):
            front(0, 0)

            def turn_of(b, more):
                front(b, 1)
                back(b, 0)
                if more:
                    front(b + 1, 0)
                back(b, 1)
            return turn_of

        with nc.Block() as block:
            @block.sync
            def _(sp):
                sp.dma_start(pages[:], io["page_table"].rearrange("b g -> (b g)").unsqueeze(0)).then_inc(small_in, 16)
                sp.dma_start(bias[:], io["t_sample_bias"]).then_inc(small_in, 16)
                sp.dma_start(new[:], io["s_proj"][TP:T, :]).then_inc(small_in, 16)
                sp.wait_ge(small_in, 48)

                def source(t, b, g, p):
                    if g:
                        return states[t][ds(b, 1), p * P:(p + 1) * P].rearrange("a r n -> (a r) n")
                    page = sp.value_load(pages[0:1, ds(b * PAGES + p, 1)], min_val=0, max_val=NPOOL - 1)
                    return pools[t][ds(page, 1)].rearrange("a r n -> (a r) n")

                with sp.Fori(0, NSEQ) as b:
                    for g in range(2):
                        for n in range(NG):
                            sp.wait_ge(k_turned, CH * (NG * (2 * b + g) + n) + CH)
                            hold(sp, held[2])
                            for p in range(PG):
                                sp.dma_start(kk[:, n % 2, p, :], source(0, b, g, PG * n + p)).then_inc(k_in[n % 2], 16)
                            if n == 1:
                                sp.wait_ge(mixed, 2 * b + g + 1)
                                hold(sp, held[2])
                                sp.dma_start(vnew[:, g], io["s_proj"][ds(TP + SQ * b, SQ),
                                                                      (2 + 3 * g) * GROUP:(3 + 3 * g) * GROUP]
                                             ).then_inc(v_in[g], 16)
                            for p in {0: (), 1: range(8), 2: range(8, 12), 3: range(12, PAGES)}[n]:
                                sp.dma_start(vv[:, g, p, :], source(1, b, g, p)).then_inc(v_in[g], 16)

            @block.gpsimd
            def _(pool):
                nc.gpsimd.memset(qd[:], 0.0).then_inc(zeroed, 1)

            @block.tensor
            def _(pe):
                pe.sem_inc(k_turned, 2 * CH)
                pe.sem_inc(mixed, 2)
                pe.wait_ge(small_in, 48)
                for t in range(2):
                    for c in range(2 * CH):
                        g, n = c // CH, c % CH
                        col = (3 * g + t) * GROUP + n * P
                        tr = nc.tensor.transpose(pA[:, (t * 2 * CH + c) * TS:(t * 2 * CH + c + 1) * TS],
                                                 new[:, col:col + P], keep.ident[0:TS, 0:TS])
                tr.then_inc(new_turned, 1)
                pe.wait_ge(new_out, 1)

                def front(b, g):
                    u = 2 * b + g
                    pe.wait_ge(qd_done, u + 1)
                    pe.wait_ge(max_done, u + 1)

                    def turn_keys(m):
                        n, c = m // CH, m % CH
                        if c == 0:
                            pe.wait_ge(k_in[n % 2], 16 * PG * (2 * u + n // 2) + 16 * PG)
                        pe.wait_ge(k_out[m % 2], ITEMS // 2 * u + m // 2 + 1)
                        for p in range(PG):
                            tr = nc.tensor.transpose(pK[:, m % 2, p * P:(p + 1) * P], kk[:, n % 2, p, c * P:(c + 1) * P],
                                                     keep.ident[:])
                        tr.then_inc(k_turned, 1)

                    def score(m):
                        n, c = m // CH, m % CH
                        pe.wait_ge(k_out[m % 2], ITEMS // 2 * u + m // 2 + 2)
                        nc.tensor.matmul(pS[0:R, n * GROUP:(n + 1) * GROUP], qd[:, g, c * R:(c + 1) * R], kT[:, m % 2, :],
                                         start=(c == 0), stop=(c == CH - 1))

                    turn_keys(0)
                    for m in range(1, ITEMS):
                        turn_keys(m)
                        score(m - 1)
                    score(ITEMS - 1)
                    for c in range(CH):
                        mm = nc.tensor.matmul(pK[0:R, 0, 0:SQ], qd[:, g, c * R:(c + 1) * R],
                                              newT[:, 1, CH * g + c, ds(SQ * b, SQ)], start=(c == 0), stop=(c == CH - 1))
                    mm.then_inc(scored, 1)

                def back(b, g):
                    u = 2 * b + g
                    pe.wait_ge(probs, u + 1)
                    pe.wait_ge(mixed_out, u + 1)
                    hold(pe, held[1])
                    for p in range(PAGES):
                        nc.tensor.transpose(pA[:, p * R:(p + 1) * R], S[:, g, p * P:(p + 1) * P], keep.ident[0:R, 0:R])
                    nc.tensor.transpose(pN[0:SQ, 0:R], S[:, g, PAST:PAST + SQ], keep.ident[0:R, 0:R]).then_inc(probs_turned, 1)
                    pe.wait_ge(v_in[g], 16 * (PAGES + 1) * b + 16 * (PAGES + 1))
                    pe.wait_ge(probs_out, u + 1)
                    w = SQ * (1 + g)
                    for c in range(CH):
                        out = pA[:, 2 * SQ * c:2 * SQ * c + w]
                        for p in range(PAGES):
                            nc.tensor.matmul(out, vv[:, g, p, c * P:(c + 1) * P], AT[:, p, w * c:w * (c + 1)],
                                             start=(p == 0), stop=False)
                        mm = nc.tensor.matmul(out, vnew[:, g, c * P:(c + 1) * P], ATn[:, w * c:w * (c + 1)],
                                              start=False, stop=True)
                    mm.then_inc(mixed, 1)

                turn_of = piped(front, back)
                with pe.Fori(0, NSEQ - 1) as b:
                    turn_of(b, True)
                turn_of(NSEQ - 1, False)

            @block.vector
            def _(v):
                v.sem_inc(k_out[1], 1)
                v.wait_ge(small_in, 48)
                v.sem_inc(max_done, 1)
                v.sem_inc(mixed_out, 1)
                v.wait_ge(new_turned, 1)
                nc.vector.tensor_copy(newT[:].rearrange("p t c q -> p (t c q)"), pA[:]).then_inc(new_out, 1)
                v.wait_ge(new_out, 1)
                v.wait_ge(zeroed, 1)

                def front(b, g):
                    u = 2 * b + g
                    for s in range(2):
                        h = nc.vector.tensor_copy(
                            qd[HD * s:HD * s + HD, g].rearrange("p (c r) -> p c r", c=CH)[:, :, SQ * s:SQ * s + SQ],
                            newT[HD * s:HD * s + HD, 0, CH * g:CH * g + CH, ds(SQ * b, SQ)])
                    h.then_inc(qd_done, 1)
                    for m in range(1, ITEMS, 2):
                        v.wait_ge(k_turned, ITEMS * u + m + 1 + 2 * CH)
                        nc.vector.tensor_copy(kT[:, 1, :], pK[:, 1, :]).then_inc(k_out[1], 1)
                    v.wait_ge(scored, u + 1)
                    hold(v, held[0])
                    nc.vector.tensor_tensor_reduce(S[:, g, 0:PAST], pS[0:R, :], bias[:, g, 0:PAST], SCALE, -3e38,
                                                   ALU.add, ALU.max, mx[:, 0:1])
                    step(v, dve, nc.vector.tensor_tensor_reduce(S[:, g, PAST:PAST + SQ], pK[0:R, 0, 0:SQ],
                                                                bias[:, g, PAST:PAST + SQ], SCALE, -3e38,
                                                                ALU.add, ALU.max, mx[:, 1:2]))
                    nc.vector.tensor_scalar(nmx[:], mx[:, 0:1], mx[:, 1:2], -1.0, ALU.max, ALU.mult).then_inc(max_done, 1)
                    v.wait_ge(exp_done, u + 1)
                    step(v, dve, nc.vector.reciprocal(rs[:], sums[:]))
                    nc.vector.tensor_tensor(rs[:], rs[:], keep.sign[:, g:g + 1], ALU.mult).then_inc(rs_done, 1)

                def back(b, g):
                    u = 2 * b + g
                    v.wait_ge(probs_turned, u + 1)
                    if g == 0:
                        for dst, src in ((AT[:, :, 0:R // 2], pA[:]), (ATn[:, 0:R // 2], pN[0:SQ, 0:R])):
                            if src.shape[0] == P:
                                d4 = dst.rearrange("p a (c q) -> p a c q", c=CH)
                                s4 = src.rearrange("p (a c s q) -> p a c s q", a=PAGES, c=CH, s=2)
                                for c in range(CH):
                                    step(v, dve, nc.vector.tensor_copy(d4[:, :, c], s4[:, :, c, 0]))
                                    nc.vector.tensor_tensor(d4[:, :, c], d4[:, :, c], s4[:, :, c, 1], ALU.add)
                            else:
                                d4 = dst.rearrange("p (c q) -> p c q", c=CH)
                                s4 = src.rearrange("p (c s q) -> p c s q", c=CH, s=2)
                                step(v, dve, nc.vector.tensor_copy(d4, s4[:, :, 0]))
                                nc.vector.tensor_tensor(d4, d4, s4[:, :, 1], ALU.add).then_inc(probs_out, 1)
                    else:
                        nc.vector.tensor_copy(AT[:].rearrange("p a r -> p (a r)"), pA[:])
                        nc.vector.tensor_copy(ATn[:], pN[0:SQ, 0:R]).then_inc(probs_out, 1)
                    v.wait_ge(mixed, u + 3)
                    got = pA[:, 0:2 * SQ * CH].rearrange("p (c s q) -> p c s q", c=CH, s=2)
                    dst = keep.OT[:, CH * g:CH * g + CH, ds(TP + SQ * b, SQ)]
                    if g == 0:
                        nc.vector.tensor_copy(dst, got[:, :, 0]).then_inc(mixed_out, 1)
                    else:
                        nc.vector.tensor_copy(dst[0:HD], got[0:HD, :, 0])
                        nc.vector.tensor_copy(dst[HD:P], got[HD:P, :, 1]).then_inc(mixed_out, 1)

                turn_of = piped(front, back)
                with v.Fori(0, NSEQ - 1) as b:
                    dve.turn(b, 2 * 2 + CH + 1)
                    turn_of(b, True)
                dve.turned(NSEQ - 1)
                turn_of(NSEQ - 1, False)

            @block.scalar
            def _(act):
                act.sem_inc(k_out[0], 1)

                def front(b, g):
                    u = 2 * b + g
                    for m in range(0, ITEMS, 2):
                        act.wait_ge(k_turned, ITEMS * u + m + 1 + 2 * CH)
                        nc.scalar.activation(kT[:, 0, :], pK[:, 0, :], ACT.Copy).then_inc(k_out[0], 1)
                    act.wait_ge(max_done, u + 2)
                    nc.scalar.activation(S[:, g, :], S[:, g, :], ACT.Exp, bias=nmx[:], accum_out=sums[:]).then_inc(exp_done, 1)
                    act.wait_ge(rs_done, u + 1)
                    nc.scalar.activation(S[:, g, :], S[:, g, :], ACT.Copy, scale=rs[:]).then_inc(probs, 1)

                with act.Fori(0, NSEQ) as b:
                    for g in range(2):
                        front(b, g)


NBK = 3
W = T // NBK
WP = TP - 2 * W


def by_seq(ap):
    return ap.rearrange("p (b q) -> p b q", b=NSEQ)


def mix_out(nc, io, keep):
    with ExitStack() as ctx:
        def sb(name, shape, dt=F32):
            return ctx.enter_context(nc.sbuf_tensor(name, shape, dt))

        xT = sb("o_xT", [P, KC, T])
        x = sb("o_x", [P, 2, D])
        wo = sb("o_wo", [P, 2, KC, P])
        sq = sb("o_sq", [P, 2, T])
        rstd = sb("o_rstd", [P, T])
        sub = sb("o_sub", [P, 1])
        small = sb("o_small", [P, 2, TS])
        ps = ctx.enter_context(nc.psum_tensor("o_ps", [P, 6, 512], F32))
        pt = ctx.enter_context(nc.psum_tensor("o_pt", [P, KC, P], F32))

        squared = nc.alloc_semaphore("o_squared")
        summed = nc.alloc_semaphore("o_summed")
        mean_done = nc.alloc_semaphore("o_mean_done")
        rooted = nc.alloc_semaphore("o_rooted")
        normed = nc.alloc_semaphore("o_normed")
        x_in = [nc.alloc_semaphore(f"o_x_in{u}") for u in range(2)]
        x_turned = nc.alloc_semaphore("o_x_turned")
        x_out = nc.alloc_semaphore("o_x_out")
        wo_in = [nc.alloc_semaphore(f"o_wo_in{u}") for u in range(2)]
        mixed = nc.alloc_semaphore("o_mixed")
        added = nc.alloc_semaphore("o_added")
        x_squared = nc.alloc_semaphore("o_x_squared")
        x_summed = nc.alloc_semaphore("o_x_summed")
        shifted = nc.alloc_semaphore("o_shifted")
        hi_done = nc.alloc_semaphore("o_hi_done")
        lo_done = nc.alloc_semaphore("o_lo_done")
        stored = nc.alloc_semaphore("o_stored")
        dve = Steps(nc, "o_dve")
        wview = io["w_o"][0].rearrange("(k p) n -> p k n", p=P)
        GSUB = NMOD + 3 * KC

        def x_rows(i):
            return io["x_prompt"][0, i * P:(i + 1) * P, :] if i < NT else io["x_sample"].rearrange("b q d -> (b q) d")

        with nc.Block() as block:
            @block.sync
            def _(sp):
                for u in range(2):
                    sp.dma_start(wo[:, u], wview[:, :, u * P:(u + 1) * P]).then_inc(wo_in[u], 16)
                for i in range(NT + 1):
                    if i >= 2:
                        sp.wait_ge(x_turned, 2 * (i - 1))
                    sp.dma_start(x[0:(P if i < NT else TS), i % 2], x_rows(i)).then_inc(x_in[i % 2], 16)
                with sp.Fori(1, KC // 2) as i:
                    for u in range(2):
                        sp.wait_ge(mixed, 2 * i + u - 1)
                        sp.dma_start(wo[:, u], wview[:, :, ds((2 * i + u) * P, P)]).then_inc(wo_in[u], 16)
                sp.wait_ge(added, KC + 2)
                sp.dma_start(io["s_x"], xT[:]).then_inc(stored, 16)
                sp.wait_ge(stored, 16)

            @block.scalar
            def _(act):
                with act.Fori(0, CH) as c:
                    act.wait_ge(normed, c + 1)
                    nc.scalar.activation(sq[:, 0:1, :], keep.OT[:, ds(c, 1), :], ACT.Square).then_inc(squared, 1)
                    act.wait_ge(mean_done, c + 1)
                    nc.scalar.activation(rstd[:], rstd[:], ACT.Sqrt).then_inc(rooted, 1)
                for i in range(NT + 1):
                    w = P if i < NT else TS
                    for n in range(2):
                        act.wait_ge(x_turned, 2 * i + n + 1)
                        nc.scalar.activation(xT[:, 4 * n:4 * n + 4, i * P:i * P + w], pt[:, 4 * n:4 * n + 4, 0:w],
                                             ACT.Copy).then_inc(x_out, 1)
                for k in range(KC):
                    act.wait_ge(added, k + 3)
                    if k >= 2:
                        act.wait_ge(x_summed, k - 1)
                    nc.scalar.activation(sq[:, k % 2], xT[:, k], ACT.Square).then_inc(x_squared, 1)
                act.wait_ge(mean_done, CH + 1)
                nc.scalar.activation(rstd[:], rstd[:], ACT.Sqrt).then_inc(rooted, 1)
                for k in range(KC):
                    act.wait_ge(shifted, k + 1)
                    nc.scalar.activation(keep.hi[:, k], sq[:, k % 2], ACT.Copy).then_inc(hi_done, 1)

            @block.tensor
            def _(pe):
                with pe.Fori(0, CH) as c:
                    pe.wait_ge(squared, c + 1)
                    for b in range(NBK):
                        mm = nc.tensor.matmul(ps[:, b, 0:W], keep.ones[:], sq[:, 0, b * W:(b + 1) * W],
                                              start=True, stop=True)
                    mm.then_inc(summed, 1)
                for i in range(NT + 1):
                    w = P if i < NT else TS
                    pe.wait_ge(x_in[i % 2], 16 * (i // 2) + 16)
                    for n in range(2):
                        if i:
                            pe.wait_ge(x_out, 2 * i + n - 1)
                        for k in range(4 * n, 4 * n + 4):
                            tr = nc.tensor.transpose(pt[:, k, 0:w], x[0:w, i % 2, k * P:(k + 1) * P],
                                                     keep.ident[0:w, 0:w])
                        tr.then_inc(x_turned, 1)
                pe.wait_ge(normed, CH + 1)
                with pe.Fori(0, KC // 2) as i:
                    for u in range(2):
                        pe.wait_ge(wo_in[u], 16 * i + 16)
                        pe.wait_ge(added, 2 * i + u + 1)
                        for b in range(NBK):
                            for k in range(KC):
                                mm = nc.tensor.matmul(ps[:, 3 * u + b, 0:W], wo[:, u, k, :],
                                                      keep.OT[:, k, b * W:(b + 1) * W], start=(k == 0), stop=(k == KC - 1))
                        mm.then_inc(mixed, 1)
                pe.wait_ge(added, KC + 2)
                for k in range(KC):
                    pe.wait_ge(x_squared, k + 1)
                    for b in range(NBK):
                        mm = nc.tensor.matmul(ps[:, b, 0:W], keep.ones[:], sq[:, k % 2, b * W:(b + 1) * W],
                                              start=(k == 0), stop=(k == KC - 1), skip_group_check=True)
                    mm.then_inc(x_summed, 1)

            @block.vector
            def _(v):
                v.sem_inc(normed, 1)
                v.sem_inc(added, 2)
                step(v, dve, nc.vector.tensor_scalar(sub[:], keep.param[:, GSUB:GSUB + 1], 1.0 - LAM_INIT, None, ALU.mult))
                with v.Fori(0, CH) as c:
                    dve.turn(c, 1)
                    v.wait_ge(summed, c + 1)
                    nc.vector.tensor_scalar(rstd[:].rearrange("p (b w) -> p b w", b=NBK), ps[:, 0:NBK, 0:W], 1.0 / P,
                                            SUBLN_EPS, ALU.mult, ALU.add).then_inc(mean_done, 1)
                    v.wait_ge(rooted, c + 1)
                    step(v, dve, nc.vector.reciprocal(rstd[:], rstd[:]))
                    head = keep.OT[:, ds(c, 1), :].rearrange("p a t -> p (a t)")
                    nc.vector.scalar_tensor_tensor(out=head, in0=head, scalar=sub[:], in1=rstd[:], op0=ALU.mult,
                                                   op1=ALU.mult).then_inc(normed, 1)
                    v.wait_ge(normed, c + 2)
                dve.turned(CH)
                v.wait_ge(x_out, 2 * (NT + 1))
                with v.Fori(0, KC // 2) as i:
                    dve.turn(i, 2)
                    for u in range(2):
                        k = 2 * i + u
                        v.wait_ge(mixed, k + 1)
                        gate = keep.mod[:, ds(GATE1 * KC + k, 1), :].rearrange("p a s -> p (a s)")
                        row = xT[:, ds(k, 1), :].rearrange("p a t -> p (a t)")
                        step(v, dve, nc.vector.tensor_tensor(by_seq(small[:, u]), by_seq(ps[:, 3 * u + 2, WP:W]),
                                                             seq_bcast(gate[:, 1:NCOND]), ALU.mult))
                        nc.vector.tensor_tensor(row[:, TP:T], row[:, TP:T], small[:, u], ALU.add)
                        for b in range(NBK):
                            w = W if b < 2 else WP
                            cols = row[:, b * W:b * W + w]
                            h = nc.vector.scalar_tensor_tensor(out=cols, in0=ps[:, 3 * u + b, 0:w], scalar=gate[:, 0:1],
                                                               in1=cols, op0=ALU.mult, op1=ALU.add)
                        h.then_inc(added, 1)
                dve.turned(KC // 2)
                v.wait_ge(x_summed, KC)
                nc.vector.tensor_scalar(rstd[:].rearrange("p (b w) -> p b w", b=NBK), ps[:, 0:NBK, 0:W], 1.0 / D,
                                        EPS, ALU.mult, ALU.add).then_inc(mean_done, 1)
                v.wait_ge(rooted, CH + 1)
                step(v, dve, nc.vector.reciprocal(rstd[:], rstd[:]))
                for k in range(KC):
                    h = sq[:, k % 2]
                    if k >= 2:
                        v.wait_ge(lo_done, k - 1)
                    nc.vector.scalar_tensor_tensor(out=h[:, 0:TP], in0=xT[:, k, 0:TP], scalar=keep.gs2[:, k, 0:1],
                                                   in1=rstd[:, 0:TP], op0=ALU.mult, op1=ALU.mult)
                    step(v, dve, nc.vector.tensor_tensor(by_seq(h[:, TP:T]), by_seq(xT[:, k, TP:T]),
                                                         seq_bcast(keep.gs2[:, k, 1:NCOND]), ALU.mult))
                    step(v, dve, nc.vector.tensor_tensor(h[:, TP:T], h[:, TP:T], rstd[:, TP:T], ALU.mult))
                    shift = keep.mod[:, SHIFT2 * KC + k]
                    nc.vector.tensor_tensor(by_seq(h[:, TP:T]), by_seq(h[:, TP:T]), seq_bcast(shift[:, 1:NCOND]), ALU.add)
                    nc.vector.tensor_scalar(h[:, 0:TP], h[:, 0:TP], shift[:, 0:1], None, ALU.add).then_inc(shifted, 1)

            @block.gpsimd
            def _(pool):
                for k in range(KC):
                    pool.wait_ge(hi_done, k + 1)
                    nc.gpsimd.tensor_tensor(keep.lo[:, k], sq[:, k % 2], keep.hi[:, k], ALU.subtract).then_inc(lo_done, 1)


def split_product(nc, out, lhs_hi, lhs_lo, rhs_hi, rhs_lo, start, stop):
    nc.tensor.matmul(out, lhs_hi, rhs_hi, start=start, stop=False)
    nc.tensor.matmul(out, lhs_hi, rhs_lo, start=False, stop=False)
    return nc.tensor.matmul(out, lhs_lo, rhs_hi, start=False, stop=stop)


def peer_scores(nc, io, keep):
    with ExitStack() as ctx:
        def sb(name, shape, dt=F32):
            return ctx.enter_context(nc.sbuf_tensor(name, shape, dt))

        wq = sb("q_wq", [P, 2, KC, P])
        wh = sb("q_wh", [P, 2, KC, P], F32R)
        wl = sb("q_wl", [P, 2, KC, P], F32R)
        keys = sb("q_keys", [P, 2, P])
        keysT = sb("q_keysT", [P, 2, P])
        qT = sb("q_qT", [P, 2, T])
        S = sb("q_S", [P, 2, NT + 1, NK])
        pq = ctx.enter_context(nc.psum_tensor("q_pq", [P, NBK, 512], F32))
        pk = ctx.enter_context(nc.psum_tensor("q_pk", [P, 512], F32))
        pS = ctx.enter_context(nc.psum_tensor("q_pS", [P, NBK, 4, NK], F32))

        wq_in = [nc.alloc_semaphore(f"q_wq_in{u}") for u in range(2)]
        keys_in = [nc.alloc_semaphore(f"q_keys_in{u}") for u in range(2)]
        hi_done = nc.alloc_semaphore("q_hi_done")
        lo_done = nc.alloc_semaphore("q_lo_done")
        keys_turned = nc.alloc_semaphore("q_keys_turned")
        keys_out = nc.alloc_semaphore("q_keys_out")
        queried = nc.alloc_semaphore("q_queried")
        q_out = nc.alloc_semaphore("q_out")
        scored = nc.alloc_semaphore("q_scored")
        s_out = nc.alloc_semaphore("q_s_out")
        held = nc.alloc_semaphore("q_held")
        stored = [nc.alloc_semaphore(f"q_stored{u}") for u in range(2)]
        wview = io["peer_wq"][0].rearrange("(k p) n -> p k n", p=P)
        kview = io["peer_keys"][0].rearrange("h c n d -> (h c) n d")

        def each(eng, body):
            with eng.Fori(0, NHC // 2) as i:
                for u in range(2):
                    body(i, u, 2 * i + u)

        with nc.Block() as block:
            @block.sync
            def _(sp):
                for u in range(2):
                    sp.sem_inc(stored[u], 32)
                    sp.dma_start(wq[:, u], wview[:, :, u * P:(u + 1) * P]).then_inc(wq_in[u], 16)
                    sp.dma_start(keys[:, u], kview[u]).then_inc(keys_in[u], 16)

                def turn(i, u, c, more):
                    if more:
                        sp.wait_ge(lo_done, c + 1)
                        sp.dma_start(wq[:, u], wview[:, :, ds((c + 2) * P, P)]).then_inc(wq_in[u], 16)
                        sp.wait_ge(keys_turned, c + 1)
                        sp.dma_start(keys[:, u], kview[ds(c + 2, 1)].rearrange("a n d -> (a n) d")).then_inc(keys_in[u], 16)
                    sp.wait_ge(s_out, c + 2)
                    sp.dma_start(io["s_s"][0:TP, ds(c, 1), :].rearrange("(i p) a n -> p i (a n)", p=P),
                                 S[:, u, 0:NT]).then_inc(stored[u], 16)
                    sp.dma_start(io["s_s"][TP:T, ds(c, 1), :].rearrange("p a n -> p (a n)"),
                                 S[0:TS, u, NT]).then_inc(stored[u], 16)

                with sp.Fori(0, NHC // 2 - 1) as i:
                    for u in range(2):
                        turn(i, u, 2 * i + u, True)
                for u in range(2):
                    turn(None, u, NHC - 2 + u, False)
                for u in range(2):
                    sp.wait_ge(stored[u], 32 * (NHC // 2) + 32)

            @block.gpsimd
            def _(pool):
                def split(i, u, c):
                    pool.wait_ge(wq_in[u], 16 * i + 16)
                    pool.wait_ge(queried, c + 1)
                    hold(pool, held)
                    nc.gpsimd.tensor_copy(wh[:, u], wq[:, u]).then_inc(hi_done, 1)
                    pool.wait_ge(hi_done, c + 1)
                    nc.gpsimd.tensor_tensor(wl[:, u], wq[:, u], wh[:, u], ALU.subtract).then_inc(lo_done, 1)
                each(pool, split)

            @block.tensor
            def _(pe):
                pe.sem_inc(queried, 2)

                def turn(i, u, c):
                    pe.wait_ge(keys_in[u], 16 * i + 16)
                    pe.wait_ge(keys_out, c + 1)
                    nc.tensor.transpose(pk[:, 0:P], keys[:, u, :], keep.ident[:]).then_inc(keys_turned, 1)
                    pe.wait_ge(lo_done, c + 1)
                    pe.wait_ge(q_out, c + 1)
                    for b in range(NBK):
                        cols = slice(b * W, (b + 1) * W)
                        for k in range(KC):
                            mm = split_product(nc, pq[:, b, 0:W], wh[:, u, k, :], wl[:, u, k, :], keep.hi[:, k, cols],
                                               keep.lo[:, k, cols], k == 0, k == KC - 1)
                    mm.then_inc(queried, 1)
                    pe.wait_ge(keys_out, c + 2)
                    pe.wait_ge(q_out, c + 2)
                    pe.wait_ge(s_out, c + 1)
                    for i in range(NT + 1):
                        w = P if i < NT else TS
                        mm = nc.tensor.matmul(pS[0:w, i // 4, i % 4, :], qT[:, u, i * P:i * P + w], keysT[:, u, :],
                                              start=True, stop=True)
                    mm.then_inc(scored, 1)
                each(pe, turn)

            @block.scalar
            def _(act):
                act.sem_inc(q_out, 1)

                def turn(i, u, c):
                    act.wait_ge(queried, c + 3)
                    nc.scalar.activation(qT[:, u].rearrange("p (b w) -> p b w", b=NBK), pq[:, :, 0:W],
                                         ACT.Copy).then_inc(q_out, 1)
                each(act, turn)

            @block.vector
            def _(v):
                v.sem_inc(keys_out, 1)
                v.sem_inc(s_out, 1)

                def turn(i, u, c):
                    v.wait_ge(keys_turned, c + 1)
                    nc.vector.tensor_copy(keysT[:, u, :], pk[:, 0:P]).then_inc(keys_out, 1)
                    v.wait_ge(scored, c + 1)
                    v.wait_ge(stored[u], 32 * i + 32)
                    nc.vector.tensor_copy(S[:, u, 0:NT].rearrange("p (b i) n -> p b i n", b=2), pS[:, 0:2])
                    nc.vector.tensor_copy(S[0:TS, u, NT], pS[0:TS, 2, 0]).then_inc(s_out, 1)
                each(v, turn)


def peer_route(nc, io, keep):
    HALF = P // 2
    GT = 4
    BEST = 8
    with ExitStack() as ctx:
        def sb(name, shape, dt=F32):
            return ctx.enter_context(nc.sbuf_tensor(name, shape, dt))

        room = keep.OT[:].rearrange("p k t -> p (k t)")
        s, rest = (room[:, n * NHC * NK:(n + 1) * NHC * NK].rearrange("p (c n) -> p c n", n=NK) for n in range(2))
        top = sb("r_top", [P, NHC, TOPK])
        at = sb("r_at", [P, NHC, TOPK], U32)
        atf = sb("r_atf", [P, NHC, TOPK])
        sums = sb("r_sums", [P, PH, TOPK * TOPK])
        best = sb("r_best", [P, PH, TOPK])
        place = sb("r_place", [P, PH, TOPK], U32)
        part = sb("r_part", [P, 2, PH * TOPK], U32)
        partf = sb("r_partf", [P, 2, PH * TOPK])
        pick = sb("r_pick", [P, 3, PH * TOPK])
        den = sb("r_den", [P, PH])
        rden = sb("r_rden", [P, PH])
        pickT = sb("r_pickT", [P, 3, P])
        hot1 = sb("r_hot1", [P, 2, GT, NK])
        hot2 = sb("r_hot2", [P, 2, GT, NK])
        second = sb("r_second", [P, 2, GT])
        G = sb("r_G", [P, 2, NK, HALF])
        pp = ctx.enter_context(nc.psum_tensor("r_pp", [P, 512], F32))
        pG = ctx.enter_context(nc.psum_tensor("r_pG", [P, 2, GT, NK], F32))

        s_in = nc.alloc_semaphore("r_s_in")
        s_used = nc.alloc_semaphore("r_s_used")
        shifted = nc.alloc_semaphore("r_shifted")
        exp_done = nc.alloc_semaphore("r_exp_done")
        picked = nc.alloc_semaphore("r_picked")
        pick_turned = nc.alloc_semaphore("r_pick_turned")
        pick_out = nc.alloc_semaphore("r_pick_out")
        hot1_done = nc.alloc_semaphore("r_hot1_done")
        hot2_done = nc.alloc_semaphore("r_hot2_done")
        spread = nc.alloc_semaphore("r_spread")
        g_out = nc.alloc_semaphore("r_g_out")
        stored = [nc.alloc_semaphore(f"r_stored{n}") for n in range(2)]
        held = nc.alloc_semaphore("r_held")
        pool_held = nc.alloc_semaphore("r_pool_held")
        second_done = nc.alloc_semaphore("r_second_done")
        dve = Steps(nc, "r_dve")
        NGT = P // GT
        gview = io["s_g"].rearrange("i j t -> j i t")

        def halves(eng, i, w, body):
            for h in range(2 if w == P else 1):
                n = NGT // 2 if w == P else w // GT
                with eng.Fori(0, n // 2) as r:
                    for u in range(2):
                        body(h, u, n * h + 2 * r + u, 2 * r + u)

        def each(eng, body):
            with eng.Fori(0, NT) as i:
                body(i, P)
            body(NT, TS)

        with nc.Block() as block:
            @block.sync
            def _(sp):
                for n in range(2):
                    sp.sem_inc(stored[n], 16)

                def store(i, w, t0):
                    for h in range(2 if w == P else 1):
                        sp.wait_ge(g_out, NGT * i + (NGT // 2 * (h + 1) if w == P else w // GT) + 2)
                        m = min(w, HALF)
                        sp.dma_start(gview[:, :, ds(t0 + HALF * h, m)], G[:, h, :, 0:m]).then_inc(stored[h], 16)

                sp.dma_start(s, io["s_s"][0:P]).then_inc(s_in, 16)
                with sp.Fori(1, NT) as i:
                    sp.wait_ge(s_used, i)
                    sp.dma_start(s, io["s_s"][ds(i * P, P)]).then_inc(s_in, 16)
                    store(i - 1, P, (i - 1) * P)
                sp.wait_ge(s_used, NT)
                sp.dma_start(s[0:TS], io["s_s"][TP:T]).then_inc(s_in, 16)
                store(NT - 1, P, TP - P)
                store(NT, TS, TP)
                sp.wait_ge(stored[0], 16 * (NT + 1) + 16)
                sp.wait_ge(stored[1], 16 * NT + 16)

            @block.vector
            def _(v):
                def tile(i, w):
                    def two(ap, c):
                        return ap[0:w].rearrange("p (h c) k -> p h c k", c=2)[:, :, c]

                    v.wait_ge(s_in, 16 * i + 16)
                    hold(v, held)
                    for lo in (0, BEST):
                        src = s if lo == 0 else rest
                        for c in range(NHC):
                            x = nc.vector.max(top[0:w, c, lo:lo + BEST], src[0:w, c])
                        step(v, dve, x)
                        hold(v, held)
                        for c in range(NHC):
                            x = nc.vector.max_index(at[0:w, c, lo:lo + BEST], top[0:w, c, lo:lo + BEST], src[0:w, c])
                            if lo == 0:
                                x = nc.vector.match_replace(rest[0:w, c], top[0:w, c, 0:BEST], s[0:w, c], -3e38)
                        if lo == 0:
                            x.then_inc(s_used, 1)
                            v.wait_ge(s_used, i + 1)
                            hold(v, held)
                        else:
                            step(v, dve, x)
                    nc.vector.tensor_tensor(
                        sums[0:w].rearrange("p h (a b) -> p h a b", a=TOPK),
                        two(top, 0).unsqueeze(3).to_broadcast([w, PH, TOPK, TOPK]),
                        two(top, 1).unsqueeze(2).to_broadcast([w, PH, TOPK, TOPK]), ALU.add)
                    step(v, dve, nc.vector.tensor_copy(atf[0:w], at[0:w]))
                    hold(v, held)
                    other = rest.rearrange("p c n -> p (c n)").rearrange("p (h n) -> p h n", h=PH)
                    for lo in (0, BEST):
                        src = sums if lo == 0 else other
                        for h in range(PH):
                            x = nc.vector.max(best[0:w, h, lo:lo + BEST], src[0:w, h])
                        step(v, dve, x)
                        hold(v, held)
                        for h in range(PH):
                            x = nc.vector.max_index(place[0:w, h, lo:lo + BEST], best[0:w, h, lo:lo + BEST], src[0:w, h])
                            if lo == 0:
                                x = nc.vector.match_replace(other[0:w, h], best[0:w, h, 0:BEST], sums[0:w, h], -3e38)
                        step(v, dve, x)
                        hold(v, held)
                    flat = place[0:w].rearrange("p h k -> p (h k)")
                    wgt = pick[0:w, 2].rearrange("p (h k) -> p h k", h=PH)
                    nc.vector.tensor_tensor(wgt, best[0:w], best[0:w, :, 0:1].to_broadcast([w, PH, TOPK]),
                                            ALU.subtract).then_inc(shifted, 1)
                    nc.vector.tensor_scalar(part[0:w, 0], flat, 4, None, ALU.logical_shift_right)
                    step(v, dve, nc.vector.tensor_scalar(part[0:w, 1], flat, TOPK - 1, None, ALU.bitwise_and))
                    step(v, dve, nc.vector.tensor_copy(partf[0:w], part[0:w]))
                    for c in range(2):
                        eq = (sums if c == 0 else other)[0:w].rearrange("p h (k a) -> p h k a", k=TOPK)
                        step(v, dve, nc.vector.tensor_tensor(
                            eq, keep.iota[0:w, 0:TOPK].unsqueeze(1).unsqueeze(1).to_broadcast([w, PH, TOPK, TOPK]),
                            partf[0:w, c].rearrange("p (h k) -> p h k", h=PH).unsqueeze(3)
                            .to_broadcast([w, PH, TOPK, TOPK]), ALU.is_equal))
                        step(v, dve, nc.vector.tensor_tensor(
                            eq, eq, two(atf, c).unsqueeze(2).to_broadcast([w, PH, TOPK, TOPK]), ALU.mult))
                        nc.vector.tensor_reduce(pick[0:w, c].rearrange("p (h k) -> p h k", h=PH), eq, AX.X, ALU.add)
                    v.wait_ge(exp_done, i + 1)
                    step(v, dve, nc.vector.tensor_reduce(den[0:w], wgt, AX.X, ALU.add))
                    step(v, dve, nc.vector.reciprocal(rden[0:w], den[0:w]))
                    nc.vector.tensor_tensor(wgt, wgt, rden[0:w].unsqueeze(2).to_broadcast([w, PH, TOPK]),
                                            ALU.mult).then_inc(picked, 1)
                    v.wait_ge(pick_turned, i + 1)
                    nc.vector.tensor_copy(pickT[:, :, 0:w], pp[:, 0:3 * P].rearrange("p (n t) -> p n t", n=3)[:, :, 0:w]
                                          ).then_inc(pick_out, 1)
                    v.wait_ge(pick_out, i + 1)
                    hold(v, held)

                    def rows(h, u, g, r):
                        v.wait_ge(spread, NGT * i + g + 1)
                        for t in range(GT):
                            col = ds(GT * g + t, 1)
                            x = nc.vector.tensor_scalar(hot1[:, u, t], keep.iota[:], pickT[:, 0, col], pickT[:, 2, col],
                                                        ALU.is_equal, ALU.mult)
                        x.then_inc(hot1_done, 1)
                    halves(v, i, w, rows)

                PER = 16
                with v.Fori(0, NT) as i:
                    dve.turn(i, PER)
                    tile(i, P)
                dve.turned(NT)
                tile(NT, TS)

            @block.scalar
            def _(act):
                act.sem_inc(g_out, 2)

                def tile(i, w):
                    act.wait_ge(shifted, i + 1)
                    nc.scalar.activation(pick[0:w, 2], pick[0:w, 2], ACT.Exp).then_inc(exp_done, 1)

                    def leave(h, u, g, r):
                        act.wait_ge(spread, NGT * i + g + 3)
                        act.wait_ge(stored[h], 16 * i + 16)
                        nc.scalar.activation(G[:, h, :, ds(GT * r, GT)], pG[:, u].rearrange("p t i -> p i t"), ACT.Copy).then_inc(g_out, 1)
                    halves(act, i, w, leave)
                each(act, tile)

            @block.gpsimd
            def _(pool):
                def tile(i, w):
                    pool.wait_ge(pick_out, i + 1)
                    hold(pool, pool_held)

                    def rows(h, u, g, r):
                        pool.wait_ge(spread, NGT * i + g + 1)
                        hold(pool, pool_held)
                        nc.gpsimd.tensor_copy(second[:, u], pickT[:, 1, ds(GT * g, GT)]).then_inc(second_done, 1)
                        pool.wait_ge(second_done, NGT * i + g + 1)
                        hold(pool, pool_held)
                        for t in range(GT):
                            x = nc.gpsimd.tensor_scalar(hot2[:, u, t], keep.iota[:], second[:, u, t:t + 1], None,
                                                        ALU.is_equal)
                        x.then_inc(hot2_done, 1)
                    halves(pool, i, w, rows)
                each(pool, tile)

            @block.tensor
            def _(pe):
                pe.sem_inc(spread, 2)

                def tile(i, w):
                    pe.wait_ge(picked, i + 1)
                    for n in range(3):
                        x = nc.tensor.transpose(pp[:, n * P:n * P + w], pick[0:w, n], keep.ident[0:w, 0:w])
                    x.then_inc(pick_turned, 1)

                    def products(h, u, g, r):
                        pe.wait_ge(hot1_done, NGT * i + g + 1)
                        pe.wait_ge(hot2_done, NGT * i + g + 1)
                        pe.wait_ge(g_out, NGT * i + g + 1)
                        for t in range(GT):
                            x = nc.tensor.matmul(pG[:, u, t], hot2[:, u, t], hot1[:, u, t], start=True, stop=True)
                        x.then_inc(spread, 1)
                    halves(pe, i, w, products)
                each(pe, tile)


def peer_experts(nc, io, keep):
    with ExitStack() as ctx:
        def sb(name, shape, dt=F32):
            return ctx.enter_context(nc.sbuf_tensor(name, shape, dt))

        uu = sb("e_u", [P, 2, D])
        vv = sb("e_v", [P, 2, D])
        G = sb("e_G", [P, 2, T])
        uh = sb("e_uh", [P, 2, KC, P], F32R)
        ul = sb("e_ul", [P, 2, KC, P], F32R)
        vh = sb("e_vh", [P, 2, D], F32R)
        vl = sb("e_vl", [P, 2, D], F32R)
        act_out = sb("e_act", [P, NBK, W])
        ph = sb("e_ph", [P, 2, T], F32R)
        pl = sb("e_pl", [P, 2, T], F32R)
        pu = ctx.enter_context(nc.psum_tensor("e_pu", [P, 512], F32))
        pa = ctx.enter_context(nc.psum_tensor("e_pa", [P, NBK, 512], F32))
        po = ctx.enter_context(nc.psum_tensor("e_po", [P, 4, 512], F32))
        acc = keep.OT

        u_in = [nc.alloc_semaphore(f"e_u_in{u}") for u in range(2)]
        v_in = [nc.alloc_semaphore(f"e_v_in{u}") for u in range(2)]
        g_in = [nc.alloc_semaphore(f"e_g_in{u}") for u in range(2)]
        u_turned = nc.alloc_semaphore("e_u_turned")
        uh_done = nc.alloc_semaphore("e_uh_done")
        ul_done = nc.alloc_semaphore("e_ul_done")
        vh_done = nc.alloc_semaphore("e_vh_done")
        vl_done = nc.alloc_semaphore("e_vl_done")
        dotted = nc.alloc_semaphore("e_dotted")
        gelu_done = nc.alloc_semaphore("e_gelu_done")
        p_done = nc.alloc_semaphore("e_p_done")
        ph_done = nc.alloc_semaphore("e_ph_done")
        pl_done = nc.alloc_semaphore("e_pl_done")
        summed = nc.alloc_semaphore("e_summed")
        added = nc.alloc_semaphore("e_added")
        held = nc.alloc_semaphore("e_held")
        zeroed = nc.alloc_semaphore("e_zeroed")
        win_out = nc.alloc_semaphore("e_win_out")
        NP = NK // 2
        OUTS = KC * NBK
        SHARES = 28
        SHARE = (PAST - SQ) // SHARES
        assert SHARES * SHARE == PAST - SQ and 2 * SHARES < NP
        states = [io[n][0].rearrange("b r h e -> b r (h e)") for n in ("state_k_win", "state_v_win")]
        wins = [io[n][0].rearrange("b r h e -> b r (h e)") for n in ("k_win_sample", "v_win_sample")]
        uview = io["peer_u"][0].rearrange("(c e) d -> c e d", e=NK)
        vview = io["peer_v"][0].rearrange("(c e) d -> c e d", e=NK)

        def row(view, c):
            return view[ds(c, 1)].rearrange("a e d -> (a e) d")

        with nc.Block() as block:
            @block.sync
            def _(sp):
                for u in range(2):
                    sp.dma_start(uu[:, u], uview[u]).then_inc(u_in[u], 16)
                    sp.dma_start(G[:, u], io["s_g"][u]).then_inc(g_in[u], 16)
                    sp.dma_start(vv[:, u], vview[u]).then_inc(v_in[u], 16)

                def next_pair(i):
                    for u in range(2):
                        c = 2 * i + u
                        sp.wait_ge(u_turned, 2 * c + 2)
                        sp.dma_start(uu[:, u], row(uview, c + 2)).then_inc(u_in[u], 16)
                        sp.wait_ge(vl_done, c + 1)
                        sp.dma_start(vv[:, u], row(vview, c + 2)).then_inc(v_in[u], 16)
                    for u in range(2):
                        c = 2 * i + u
                        sp.wait_ge(p_done, NBK * c + NBK)
                        sp.dma_start(G[:, u], row(io["s_g"], c + 2)).then_inc(g_in[u], 16)

                with sp.Fori(0, SHARES) as j:
                    for t in range(2):
                        sp.dma_start(wins[t][:, ds(j * SHARE, SHARE)], states[t][:, ds(j * SHARE + SQ, SHARE)]
                                     ).then_inc(win_out, 16)
                        next_pair(2 * j + t)
                with sp.Fori(2 * SHARES, NP - 1) as i:
                    next_pair(i)
                sp.wait_ge(win_out, 16 * 2 * SHARES)

            @block.tensor
            def _(pe):
                pe.sem_inc(summed, 1)

                def turn_u(i, u, n):
                    c = 2 * i + u
                    pe.wait_ge(u_in[u], 16 * i + 16)
                    pe.wait_ge(ul_done, 2 * c + n + 1)
                    for k in range(4):
                        x = nc.tensor.transpose(pu[:, k * P:(k + 1) * P], uu[:, u, (4 * n + k) * P:(4 * n + k + 1) * P],
                                                keep.ident[:])
                    x.then_inc(u_turned, 1)

                def dot(i, u, blocks):
                    c = 2 * i + u
                    pe.wait_ge(ul_done, 2 * c + 3)
                    for b in blocks:
                        pe.wait_ge(gelu_done, NBK * c + b + 1)
                        cols = slice(b * W, (b + 1) * W)
                        for k in range(KC):
                            x = split_product(nc, pa[:, b, 0:W], uh[:, u, k], ul[:, u, k], keep.hi[:, k, cols],
                                              keep.lo[:, k, cols], k == 0, k == KC - 1)
                        x.then_inc(dotted, 1)

                def out(i, blocks):
                    pe.wait_ge(vl_done, 2 * i + 2)
                    n = KC * blocks[0]
                    for b in blocks:
                        cols = slice(b * W, (b + 1) * W)
                        pe.wait_ge(pl_done, NBK * (2 * i + 1) + b + 1 + NBK)
                        for k in range(KC):
                            pe.wait_ge(added, OUTS * i + n + 1)
                            for u in range(2):
                                x = split_product(nc, po[:, n % 4, 0:W], vh[:, u, k * P:(k + 1) * P],
                                                  vl[:, u, k * P:(k + 1) * P], ph[:, u, cols], pl[:, u, cols],
                                                  u == 0, u == 1)
                            x.then_inc(summed, 1)
                            n += 1

                ALL = range(NBK)
                for u in range(2):
                    for n in range(2):
                        turn_u(0, u, n)
                with pe.Fori(0, NP - 1) as i:
                    dot(i, 0, ALL)
                    turn_u(i + 1, 0, 0)
                    dot(i, 1, ALL[:1])
                    turn_u(i + 1, 0, 1)
                    dot(i, 1, ALL[1:])
                    turn_u(i + 1, 1, 0)
                    out(i, ALL[:1])
                    turn_u(i + 1, 1, 1)
                    out(i, ALL[1:])
                for u in range(2):
                    dot(NP - 1, u, ALL)
                out(NP - 1, ALL)

            @block.scalar
            def _(act):
                act.sem_inc(gelu_done, NBK)

                def copy_u(i, u, n):
                    act.wait_ge(u_turned, 2 * (2 * i + u) + n + 1)
                    nc.scalar.activation(uh[:, u, 4 * n:4 * n + 4], pu[:].rearrange("p (k e) -> p k e", k=4),
                                         ACT.Copy).then_inc(uh_done, 1)

                def gelus(i, u, blocks):
                    c = 2 * i + u
                    for b in blocks:
                        act.wait_ge(dotted, NBK * c + b + 1)
                        act.wait_ge(pl_done, NBK * c + b + 1)
                        nc.scalar.activation(act_out[:, b], pa[:, b, 0:W], ACT.Gelu).then_inc(gelu_done, 1)
                        act.wait_ge(p_done, NBK * c + b + 1)
                        nc.scalar.activation(ph[:, u, b * W:(b + 1) * W], act_out[:, b], ACT.Copy).then_inc(ph_done, 1)

                ALL = range(NBK)
                for u in range(2):
                    for n in range(2):
                        copy_u(0, u, n)
                with act.Fori(0, NP - 1) as i:
                    gelus(i, 0, ALL)
                    copy_u(i + 1, 0, 0)
                    gelus(i, 1, ALL[:1])
                    copy_u(i + 1, 0, 1)
                    gelus(i, 1, ALL[1:])
                    for n in range(2):
                        copy_u(i + 1, 1, n)
                for u in range(2):
                    gelus(NP - 1, u, ALL)

            @block.vector
            def _(v):
                v.sem_inc(ul_done, 1)
                v.sem_inc(pl_done, NBK)
                v.sem_inc(added, 4)

                def low_u(i, u, n):
                    v.wait_ge(uh_done, 2 * (2 * i + u) + n + 1)
                    part = slice(4 * n, 4 * n + 4)
                    nc.vector.tensor_tensor(ul[:, u, part], pu[:].rearrange("p (k e) -> p k e", k=4), uh[:, u, part],
                                            ALU.subtract).then_inc(ul_done, 1)

                def weigh(i, u, blocks):
                    c = 2 * i + u
                    v.wait_ge(g_in[u], 16 * i + 16)
                    for b in blocks:
                        cols = slice(b * W, (b + 1) * W)
                        v.wait_ge(gelu_done, NBK * c + b + 4)
                        nc.vector.tensor_tensor(act_out[:, b], act_out[:, b], G[:, u, cols], ALU.mult).then_inc(p_done, 1)
                        v.wait_ge(ph_done, NBK * c + b + 1)
                        nc.vector.tensor_tensor(pl[:, u, cols], act_out[:, b], ph[:, u, cols],
                                                ALU.subtract).then_inc(pl_done, 1)

                def add(i, blocks):
                    v.wait_ge(added, OUTS * i + 4)
                    n = KC * blocks[0]
                    for b in blocks:
                        cols = slice(b * W, (b + 1) * W)
                        for k in range(KC):
                            v.wait_ge(summed, OUTS * i + n + 2)
                            nc.vector.tensor_tensor(acc[:, k, cols], po[:, n % 4, 0:W], acc[:, k, cols],
                                                    ALU.add).then_inc(added, 1)
                            n += 1

                ALL = range(NBK)
                for u in range(2):
                    for n in range(2):
                        low_u(0, u, n)
                v.wait_ge(zeroed, 1)
                with v.Fori(0, NP - 1) as i:
                    weigh(i, 0, ALL)
                    low_u(i + 1, 0, 0)
                    weigh(i, 1, ALL[:1])
                    low_u(i + 1, 0, 1)
                    weigh(i, 1, ALL[1:])
                    low_u(i + 1, 1, 0)
                    add(i, ALL[:1])
                    low_u(i + 1, 1, 1)
                    add(i, ALL[1:])
                for u in range(2):
                    weigh(NP - 1, u, ALL)
                add(NP - 1, ALL)

            @block.gpsimd
            def _(pool):
                nc.gpsimd.memset(acc[:], 0.0).then_inc(zeroed, 1)
                with pool.Fori(0, NP) as i:
                    for u in range(2):
                        c = 2 * i + u
                        pool.wait_ge(v_in[u], 16 * i + 16)
                        pool.wait_ge(summed, OUTS * i + 1)
                        hold(pool, held)
                        nc.gpsimd.tensor_copy(vh[:, u], vv[:, u]).then_inc(vh_done, 1)
                        pool.wait_ge(vh_done, c + 1)
                        nc.gpsimd.tensor_tensor(vl[:, u], vv[:, u], vh[:, u], ALU.subtract).then_inc(vl_done, 1)


def finish(nc, io, keep):
    with ExitStack() as ctx:
        def sb(name, shape, dt=F32):
            return ctx.enter_context(nc.sbuf_tensor(name, shape, dt))

        xT = sb("f_xT", [P, KC, T])
        sq = sb("f_sq", [P, 2, T])
        rstd = sb("f_rstd", [P, T])
        y = sb("f_y", [P, 2, D])
        small = sb("f_small", [P, KC, TS])
        ps = ctx.enter_context(nc.psum_tensor("f_ps", [P, NBK, 512], F32))
        pt = ctx.enter_context(nc.psum_tensor("f_pt", [P, 2, 512], F32))
        x_in = nc.alloc_semaphore("f_x_in")
        added = nc.alloc_semaphore("f_added")
        squared = nc.alloc_semaphore("f_squared")
        summed = nc.alloc_semaphore("f_summed")
        mean_done = nc.alloc_semaphore("f_mean_done")
        rooted = nc.alloc_semaphore("f_rooted")
        normed = nc.alloc_semaphore("f_normed")
        turned = nc.alloc_semaphore("f_turned")
        y_out = [nc.alloc_semaphore(f"f_y_out{n}") for n in range(2)]
        stored = [nc.alloc_semaphore(f"f_stored{n}") for n in range(2)]
        dve = Steps(nc, "f_dve")
        GF = NMOD + 2 * KC

        def y_rows(i):
            return io["y_prompt"][0, i * P:(i + 1) * P, :] if i < NT else io["y_sample"].rearrange("b q d -> (b q) d")

        with nc.Block() as block:
            @block.sync
            def _(sp):
                sp.dma_start(xT[:], io["s_x"]).then_inc(x_in, 16)
                for i in range(NT + 1):
                    for n in range(2):
                        sp.wait_ge(y_out[n], i + 1)
                    sp.dma_start(y_rows(i), y[0:(P if i < NT else TS), i % 2]).then_inc(stored[i % 2], 16)
                for n in range(2):
                    sp.wait_ge(stored[n], 16 * ((NT + 2 - n) // 2))

            @block.vector
            def _(v):
                v.wait_ge(x_in, 16)
                for k in range(KC):
                    step(v, dve, nc.vector.tensor_tensor(by_seq(small[:, k]), by_seq(keep.OT[:, k, TP:T]),
                                                         seq_bcast(keep.mod[:, GATE2 * KC + k, 1:NCOND]), ALU.mult))
                    nc.vector.tensor_tensor(xT[:, k, TP:T], xT[:, k, TP:T], small[:, k], ALU.add)
                    nc.vector.scalar_tensor_tensor(out=xT[:, k, 0:TP], in0=keep.OT[:, k, 0:TP],
                                                   scalar=keep.mod[:, GATE2 * KC + k, 0:1], in1=xT[:, k, 0:TP],
                                                   op0=ALU.mult, op1=ALU.add).then_inc(added, 1)
                v.wait_ge(summed, KC)
                nc.vector.tensor_scalar(rstd[:].rearrange("p (b w) -> p b w", b=NBK), ps[:, :, 0:W], 1.0 / D, EPS,
                                        ALU.mult, ALU.add).then_inc(mean_done, 1)
                v.wait_ge(rooted, 1)
                step(v, dve, nc.vector.reciprocal(rstd[:], rstd[:]))
                for k in range(KC):
                    x = nc.vector.scalar_tensor_tensor(out=xT[:, k], in0=xT[:, k], scalar=keep.param[:, GF + k:GF + k + 1],
                                                       in1=rstd[:], op0=ALU.mult, op1=ALU.mult)
                    if k % 4 == 3:
                        x.then_inc(normed, 1)
                for i in range(NT + 1):
                    w = P if i < NT else TS
                    v.wait_ge(turned, 2 * i + 2)
                    if i >= 2:
                        v.wait_ge(stored[i % 2], 16 * (i // 2))
                    nc.vector.tensor_copy(y[0:w, i % 2, 512:D], pt[0:w, 1]).then_inc(y_out[1], 1)

            @block.scalar
            def _(act):
                for k in range(KC):
                    act.wait_ge(added, k + 1)
                    if k >= 2:
                        act.wait_ge(summed, k - 1)
                    nc.scalar.activation(sq[:, k % 2], xT[:, k], ACT.Square).then_inc(squared, 1)
                act.wait_ge(mean_done, 1)
                nc.scalar.activation(rstd[:], rstd[:], ACT.Sqrt).then_inc(rooted, 1)
                for i in range(NT + 1):
                    w = P if i < NT else TS
                    act.wait_ge(turned, 2 * i + 1)
                    if i >= 2:
                        act.wait_ge(stored[i % 2], 16 * (i // 2))
                    nc.scalar.activation(y[0:w, i % 2, 0:512], pt[0:w, 0], ACT.Copy).then_inc(y_out[0], 1)

            @block.tensor
            def _(pe):
                for k in range(KC):
                    pe.wait_ge(squared, k + 1)
                    for b in range(NBK):
                        x = nc.tensor.matmul(ps[:, b, 0:W], keep.ones[:], sq[:, k % 2, b * W:(b + 1) * W],
                                             start=(k == 0), stop=(k == KC - 1), skip_group_check=True)
                    x.then_inc(summed, 1)
                for i in range(NT + 1):
                    w = P if i < NT else TS
                    for n in range(2):
                        if i == 0:
                            pe.wait_ge(normed, n + 1)
                        else:
                            pe.wait_ge(y_out[n], i)
                        for k in range(4):
                            x = nc.tensor.transpose(pt[0:w, n, k * P:(k + 1) * P], xT[:, 4 * n + k, i * P:i * P + w],
                                                    keep.ident[:])
                        x.then_inc(turned, 1)


class Keep:
    pass


def run_stage(nc, io, keep, stage):
    before = nc.snapshot_sems()
    stage(nc, io, keep)
    nc.clear_and_free_semaphores(nc.allocated_since(before))
    nc.all_engine_barrier()


def build(nc, io):
    keep = Keep()
    with ExitStack() as ctx:
        def sb(name, shape, dt=F32):
            return ctx.enter_context(nc.sbuf_tensor(name, shape, dt))

        keep.ident = sb("k_ident", [P, P])
        keep.ones = sb("k_ones", [P, P])
        keep.iota = sb("k_iota", [P, NK])
        keep.param = sb("k_param", [P, NMOD + 3 * KC + 1])
        keep.mod = sb("k_mod", [P, NMOD, NCOND])
        keep.gs1 = sb("k_gs1", [P, KC, NCOND])
        keep.gs2 = sb("k_gs2", [P, KC, NCOND])
        keep.neglam = sb("k_neglam", [P, 1])
        keep.halves = sb("k_halves", [2 * CH * SQ, 2])
        keep.sign = sb("k_sign", [2 * CH * SQ, 2])
        for stage in (modulation, project):
            run_stage(nc, io, keep, stage)
        keep.OT = sb("k_OT", [P, KC, T])
        for stage in (prompt_attn, sample_attn):
            run_stage(nc, io, keep, stage)
        keep.hi = sb("k_hi", [P, KC, T], F32R)
        keep.lo = sb("k_lo", [P, KC, T], F32R)
        for stage in (mix_out, peer_scores, peer_route, peer_experts, finish):
            run_stage(nc, io, keep, stage)


INPUTS = ["x_prompt", "x_sample", "cache_k_diff", "cache_v_diff", "state_k_win", "state_v_win", "page_table",
          "c_prompt", "c_sample", "ada_w", "ada_b", "norm_attn_g", "norm_ffn_g", "w_in", "w_o", "diff_lambda",
          "diff_subln_g", "peer_wq", "peer_keys", "peer_u", "peer_v", "final_norm_g"]
OUTPUTS = {
    "y_prompt": (1, TP, D), "y_sample": (NSEQ, SQ, D),
    "k_diff_prompt": (1, 1, TP, 4, 128), "v_diff_prompt": (1, 1, TP, 4, 128),
    "k_win_prompt": (1, 1, TP, 8, 64), "v_win_prompt": (1, 1, TP, 8, 64),
    "k_diff_sample": (1, NSEQ, SQ, 4, 128), "v_diff_sample": (1, NSEQ, SQ, 4, 128),
    "k_win_sample": (1, NSEQ, PAST, 8, 64), "v_win_sample": (1, NSEQ, PAST, 8, 64),
}
SCRATCH = {"s_proj": (T, PROJ), "s_x": (P, KC, T), "s_s": (T, NHC, NK), "s_g": (NK, NK, T)}


def kernel(**inputs):
    import concourse.bacc as bacc
    from concourse.bass_utils import run_bass_kernel_spmd

    nc = bacc.Bacc("TRN2", target_bir_lowering=False, num_devices=1)
    arrays = {name: np.ascontiguousarray(inputs[name]) for name in INPUTS} | host_tables()
    io = {name: nc.dram_tensor(name, a.shape, mybir.dt.from_np(a.dtype), kind="ExternalInput").ap()
          for name, a in arrays.items()}
    for name, shape in OUTPUTS.items():
        io[name] = nc.dram_tensor(name, shape, F32, kind="ExternalOutput").ap()
    for name, shape in SCRATCH.items():
        io[name] = nc.dram_tensor(name, shape, F32).ap()
    build(nc, io)
    got = run_bass_kernel_spmd(nc, [arrays], core_ids=[0]).results[0]
    return tuple(got[name] for name in OUTPUTS)
```

```python
import math
from contextlib import ExitStack

import concourse.bass as bass
import numpy as np
from concourse import mybir

ACT = mybir.ActivationFunctionType
ALU = mybir.AluOpType
AX = mybir.AxisListType
F32 = mybir.dt.float32
F32R = mybir.dt.float32r
U32 = mybir.dt.uint32
I32 = mybir.dt.int32
ds = bass.ds

P = 128
D = 1024
KC = D // P
TP = 1024
NT = TP // P
NSEQ, SQ = 8, 4
TS = NSEQ * SQ
T = TP + TS
GROUP = 512
PROJ = 6 * GROUP
HD = 64
CH = GROUP // P
PAST = 2048
PAGES = PAST // P
NCOND = 1 + NSEQ
NMOD = 6 * KC
SCALE = HD ** -0.5
NEG = -1e30
LAM_INIT = 0.8 - 0.6 * math.exp(-0.3 * 0)
EPS, SUBLN_EPS = 1e-6, 1e-5
NK = 128
PH = 8
TOPK = 16
NHC = 2 * PH
SHIFT1, SCALE1, GATE1, SHIFT2, SCALE2, GATE2 = range(6)


class Steps:

    def __init__(self, nc, name):
        self.sem, self.base, self.n, self.per = nc.alloc_semaphore(name), 0, 0, 0

    def now(self):
        return self.base + self.n

    def turn(self, i, per):
        self.start, self.n, self.per = self.now(), 0, per
        self.base = self.start + i * per

    def turned(self, turns):
        assert self.n == self.per, (self.n, self.per)
        self.base, self.n = self.start + turns * self.per, 0


def step(eng, steps, instruction):
    instruction.then_inc(steps.sem, 1)
    steps.n += 1
    eng.wait_ge(steps.sem, steps.now())


def hold(eng, passed):
    eng.sem_inc(passed, 1)


def host_tables():
    half = HD // 2
    inv = (np.float32(10000.0) ** (-np.arange(half, dtype=np.float32) / np.float32(half))).astype(np.float32)
    pos = np.concatenate([np.arange(TP), np.tile(PAST + np.arange(SQ), NSEQ)]).astype(np.float32)
    ang = (pos[:, None] * inv[None, :]).astype(np.float32)
    cos, sin = np.cos(ang), np.sin(ang)
    rope = np.concatenate([cos, cos, -sin, sin], axis=1).astype(np.float32)

    def count(back):
        n = sum(((back % d == 0) & (back <= w)).astype(np.float64) for w, d in ((128, 1), (512, 4), (2048, 16)))
        return np.where((back >= 0) & (n > 0), np.log(np.maximum(n, 1)), NEG)

    def causal(back):
        return np.where(back >= 0, 0.0, NEG)

    back = np.arange(P)[:, None] + (TP - P) - np.arange(TP)[None, :]
    prompt_bias = np.stack([f(back) / SCALE for f in (causal, count)], axis=1).astype(np.float32)
    row = np.arange(2 * CH * SQ) % SQ
    back = PAST + row[:, None] - np.arange(PAST + SQ)[None, :]
    sample_bias = np.stack([f(back) / SCALE for f in (causal, count)], axis=1).astype(np.float32)
    second = (np.arange(2 * CH * SQ) // SQ % 2).astype(np.float32)
    halves = np.stack([1 - second, second], axis=1).astype(np.float32)
    return {
        "t_ident": np.eye(P, dtype=np.float32),
        "t_rope": rope,
        "t_prompt_bias": prompt_bias,
        "t_sample_bias": sample_bias,
        "t_halves": halves,
        "t_iota": np.broadcast_to(np.arange(NK, dtype=np.float32), (P, NK)).copy(),
    }


def modulation(nc, io, keep):
    NB = NMOD // CH
    SLOTS = 4
    with ExitStack() as ctx:
        def sb(name, shape, dt=F32):
            return ctx.enter_context(nc.sbuf_tensor(name, shape, dt))

        crow = sb("m_crow", [NCOND, D])
        csilu = sb("m_csilu", [NCOND, D])
        cT = sb("m_cT", [P, KC, NCOND])
        rows = sb("m_rows", [P, P])
        wada = sb("m_wada", [P, SLOTS, KC, GROUP])
        mrow = sb("m_mrow", [NCOND, SLOTS, GROUP])
        lam = sb("m_lam", [1, 4, HD])
        lprod = sb("m_lprod", [1, HD])
        lsum = sb("m_lsum", [1, 2])
        lexp = sb("m_lexp", [1, 2])
        ldiff = sb("m_ldiff", [1, 1])
        pT = ctx.enter_context(nc.psum_tensor("m_pT", [P, 512], F32))
        pL = ctx.enter_context(nc.psum_tensor("m_pL", [P, 512], F32))
        pX = ctx.enter_context(nc.psum_tensor("m_pX", [P, 2, 512], F32))
        pM = ctx.enter_context(nc.psum_tensor("m_pM", [P, SLOTS, 512], F32))

        small_in = nc.alloc_semaphore("m_small_in")
        w_in = [nc.alloc_semaphore(f"m_w_in{u}") for u in range(SLOTS)]
        win_in = nc.alloc_semaphore("m_win_in")
        silu_done = nc.alloc_semaphore("m_silu_done")
        ones_done = nc.alloc_semaphore("m_ones_done")
        turned = nc.alloc_semaphore("m_turned")
        turned_out = nc.alloc_semaphore("m_turned_out")
        lam_exp = nc.alloc_semaphore("m_lam_exp")
        lam_sum = nc.alloc_semaphore("m_lam_sum")
        lam_one = nc.alloc_semaphore("m_lam_one")
        lam_all = nc.alloc_semaphore("m_lam_all")
        block_done = nc.alloc_semaphore("m_block_done")
        row_out = nc.alloc_semaphore("m_row_out")
        row_turned = nc.alloc_semaphore("m_row_turned")
        block_out = nc.alloc_semaphore("m_block_out")
        held = nc.alloc_semaphore("m_held")
        dve = Steps(nc, "m_dve")
        NSMALL = 11
        wview = io["ada_w"][0].rearrange("(k p) n -> p k n", p=P)

        with nc.Block() as block:
            @block.sync
            def _(sp):
                sp.dma_start(crow[0:1, :], io["c_prompt"]).then_inc(small_in, 16)
                sp.dma_start(crow[1:NCOND, :], io["c_sample"]).then_inc(small_in, 16)
                sp.dma_start(rows[0:NMOD, :], io["ada_b"][0].rearrange("(k p) -> k p", p=P)).then_inc(small_in, 16)
                for n, g in enumerate(("norm_attn_g", "norm_ffn_g")):
                    sp.dma_start(rows[NMOD + n * KC:NMOD + (n + 1) * KC, :],
                                 io[g][0].rearrange("(k p) -> k p", p=P)).then_inc(small_in, 16)
                sp.dma_start(rows[NMOD + 2 * KC:NMOD + 3 * KC, :],
                             io["final_norm_g"].rearrange("(k p) -> k p", p=P)).then_inc(small_in, 16)
                sp.dma_start(rows[NMOD + 3 * KC:NMOD + 3 * KC + 1, :], io["diff_subln_g"]).then_inc(small_in, 16)
                sp.dma_start(lam[:], io["diff_lambda"]).then_inc(small_in, 16)
                sp.dma_start(keep.ident[:], io["t_ident"]).then_inc(small_in, 16)
                sp.dma_start(keep.iota[:], io["t_iota"]).then_inc(small_in, 16)
                sp.dma_start(keep.halves[:], io["t_halves"]).then_inc(small_in, 16)
                for u in range(SLOTS):
                    sp.dma_start(wada[:, u], wview[:, :, u * GROUP:(u + 1) * GROUP]).then_inc(w_in[u], 16)
                for k in range(KC):
                    sp.dma_start(keep.win[:, k, :], io["w_in"][0, k * P:(k + 1) * P, :]).then_inc(win_in, 16)
                with sp.Fori(1, NB // SLOTS) as i:
                    for u in range(SLOTS):
                        sp.wait_ge(block_done, SLOTS * (i - 1) + u + 1)
                        sp.dma_start(wada[:, u], wview[:, :, ds((SLOTS * i + u) * GROUP, GROUP)]).then_inc(w_in[u], 16)
                sp.wait_ge(win_in, 16 * KC)

            @block.scalar
            def _(act):
                act.wait_ge(small_in, 16 * NSMALL)
                nc.scalar.activation(csilu[:], crow[:], ACT.Silu).then_inc(silu_done, 1)
                act.wait_ge(lam_sum, 2)
                nc.scalar.activation(lexp[:], lsum[:], ACT.Exp).then_inc(lam_exp, 1)
                with act.Fori(0, NB // SLOTS) as i:
                    for u in range(SLOTS):
                        act.wait_ge(block_done, SLOTS * i + u + 1)
                        nc.scalar.activation(mrow[:, u], pM[0:NCOND, u], ACT.Copy).then_inc(row_out, 1)

            @block.tensor
            def _(pe):
                pe.wait_ge(silu_done, 1)
                NR = NMOD + 3 * KC + 1
                for k in range(KC):
                    nc.tensor.transpose(pT[:, k * NCOND:(k + 1) * NCOND], csilu[:, k * P:(k + 1) * P],
                                        keep.ident[0:NCOND, 0:NCOND])
                nc.tensor.transpose(pT[:, 128:128 + NR], rows[0:NR, :], keep.ident[0:NR, 0:NR]).then_inc(turned, 1)
                pe.wait_ge(lam_one, 1)
                pe.wait_ge(ones_done, 1)
                nc.tensor.matmul(pL[:, 0:1], keep.ones[0:1, :], ldiff[:], start=True, stop=True).then_inc(lam_all, 1)
                pe.wait_ge(turned_out, 2)
                with pe.Fori(0, NB // SLOTS) as i:
                    for u in range(SLOTS):
                        pe.wait_ge(w_in[u], 16 * i + 16)
                        for k in range(KC):
                            mm = nc.tensor.matmul(pM[0:NCOND, u, :], cT[:, k, :], wada[:, u, k, :],
                                                  start=(k == 0), stop=(k == KC - 1))
                        mm.then_inc(block_done, 1)
                        pe.wait_ge(row_out, SLOTS * i + u + 1)
                        pe.wait_ge(block_out, SLOTS * i + u + 1)
                        hold(pe, held)
                        for c in range(CH):
                            tr = nc.tensor.transpose(pX[:, u % 2, c * NCOND:(c + 1) * NCOND],
                                                     mrow[:, u, c * P:(c + 1) * P], keep.ident[0:NCOND, 0:NCOND])
                        tr.then_inc(row_turned, 1)

            @block.vector
            def _(v):
                nc.vector.memset(keep.ones[:], 1.0).then_inc(ones_done, 1)
                v.sem_inc(block_out, 2)
                v.wait_ge(small_in, 16 * NSMALL)
                for n in range(2):
                    nc.vector.tensor_tensor_reduce(lprod[:], lam[:, 2 * n, :], lam[:, 2 * n + 1, :], 1.0, 0.0,
                                                   ALU.mult, ALU.add, lsum[:, n:n + 1]).then_inc(lam_sum, 1)
                    v.wait_ge(lam_sum, n + 1)
                v.wait_ge(lam_exp, 1)
                step(v, dve, nc.vector.tensor_tensor(ldiff[:], lexp[:, 1:2], lexp[:, 0:1], ALU.subtract))
                nc.vector.tensor_scalar(ldiff[:], ldiff[:], -LAM_INIT, None, ALU.add).then_inc(lam_one, 1)
                v.wait_ge(turned, 1)
                nc.vector.tensor_copy(cT[:], pT[:, 0:KC * NCOND].rearrange("p (k s) -> p k s", k=KC)).then_inc(turned_out, 1)
                nc.vector.tensor_copy(keep.param[:], pT[:, 128:128 + NMOD + 3 * KC + 1]).then_inc(turned_out, 1)
                v.wait_ge(lam_all, 1)
                nc.vector.tensor_copy(keep.neglam[:], pL[:, 0:1])
                v.wait_ge(turned_out, 2)
                with v.Fori(0, NB // SLOTS) as i:
                    for u in range(SLOTS):
                        v.wait_ge(row_turned, SLOTS * i + u + 1)
                        nc.vector.tensor_tensor(
                            keep.mod[:, ds((SLOTS * i + u) * CH, CH), :],
                            pX[:, u % 2, 0:CH * NCOND].rearrange("p (c s) -> p c s", c=CH),
                            keep.param[:, ds((SLOTS * i + u) * CH, CH)].unsqueeze(2).to_broadcast([P, CH, NCOND]),
                            ALU.add).then_inc(block_out, 1)
                v.wait_ge(block_out, NB + 2)
                for m, out, g in ((SCALE1, keep.gs1, NMOD), (SCALE2, keep.gs2, NMOD + KC)):
                    step(v, dve, nc.vector.tensor_scalar(out[:], keep.mod[:, m * KC:(m + 1) * KC, :], 1.0, None, ALU.add))
                    nc.vector.tensor_tensor(out[:], out[:], keep.param[:, g:g + KC].unsqueeze(2)
                                            .to_broadcast([P, KC, NCOND]), ALU.mult)
                nc.vector.memset(keep.sign[:, 1:2], 1.0)
                step(v, dve, nc.vector.tensor_tensor(keep.sign[:, 0:1], keep.halves[:, 1:2], keep.neglam[0:2 * CH * SQ, :],
                                                     ALU.mult))
                nc.vector.tensor_tensor(keep.sign[:, 0:1], keep.sign[:, 0:1], keep.halves[:, 0:1], ALU.add)


def seq_bcast(vec, k=None):
    return vec.unsqueeze(2).to_broadcast([P, NSEQ, SQ])


def project(nc, io, keep):
    ORDER = (2, 5, 0, 1, 3, 4)
    ROPE = (0, 1, 3, 4)
    with ExitStack() as ctx:
        def sb(name, shape, dt=F32):
            return ctx.enter_context(nc.sbuf_tensor(name, shape, dt))

        win = keep.win
        x = sb("p_x", [P, D])
        xn = sb("p_xn", [P, D])
        square = sb("p_square", [P, D])
        ss = sb("p_ss", [P, 1])
        ms = sb("p_ms", [P, 1])
        rms = sb("p_rms", [P, 1])
        rstd = sb("p_rstd", [P, 1])
        hT = sb("p_hT", [P, KC, P])
        rope = sb("p_rope", [P, 2, 2 * HD])
        rows = sb("p_rows", [P, 6, GROUP])
        tA = sb("p_tA", [P, GROUP])
        tB = sb("p_tB", [P, GROUP])
        tp = ctx.enter_context(nc.psum_tensor("p_tp", [P, KC, P], F32))
        pj = ctx.enter_context(nc.psum_tensor("p_pj", [P, 6, GROUP], F32))

        x_in = nc.alloc_semaphore("p_x_in")
        rope_in = nc.alloc_semaphore("p_rope_in")
        squared = nc.alloc_semaphore("p_squared")
        mean_done = nc.alloc_semaphore("p_mean_done")
        root_done = nc.alloc_semaphore("p_root_done")
        rstd_done = nc.alloc_semaphore("p_rstd_done")
        xn_done = nc.alloc_semaphore("p_xn_done")
        turned = nc.alloc_semaphore("p_turned")
        h_done = nc.alloc_semaphore("p_h_done")
        proj_done = nc.alloc_semaphore("p_proj_done")
        rope_rows = nc.alloc_semaphore("p_rope_rows")
        v_rows = nc.alloc_semaphore("p_v_rows")
        stored = nc.alloc_semaphore("p_stored")
        tail = nc.alloc_semaphore("p_tail")
        dve = Steps(nc, "p_dve")
        xp = io["x_prompt"][0]
        xs = io["x_sample"].rearrange("b q d -> (b q) d")
        ks = {1: "k_diff", 2: "v_diff", 4: "k_win", 5: "v_win"}

        def flat(name):
            return io[name].rearrange("l b s h e -> (l b s) (h e)")

        with nc.Block() as block:
            @block.sync
            def _(sp):
                sp.sem_inc(stored, 80)

                def store(i, w, r0):
                    sp.wait_ge(rope_rows, 4 * i + 8)
                    sp.wait_ge(v_rows, 2 * i + 4)
                    sp.dma_start(io["s_proj"][ds(r0, w), :], rows[:w].rearrange("p g n -> p (g n)")).then_inc(stored, 16)

                with sp.Fori(0, NT) as i:
                    store(i, P, i * P)
                    for g, name in ks.items():
                        sp.dma_start(flat(name + "_prompt")[ds(i * P, P), :], rows[:, g]).then_inc(stored, 16)
                store(NT, TS, TP)
                sp.dma_start(flat("k_diff_sample"), rows[:TS, 1]).then_inc(stored, 16)
                sp.dma_start(flat("v_diff_sample"), rows[:TS, 2]).then_inc(stored, 16)
                sp.wait_ge(stored, 80 * (NT + 1) + 48)
                for g, name in ((4, "k_win_sample"), (5, "v_win_sample")):
                    sp.dma_start(io[name][0, :, PAST - SQ:PAST].rearrange("b q h e -> b q (h e)"),
                                 io["s_proj"][TP:T, g * GROUP:(g + 1) * GROUP]
                                 .rearrange("(b q) n -> b q n", b=NSEQ)).then_inc(tail, 16)
                sp.wait_ge(tail, 32)

            @block.gpsimd
            def _(pool):
                pool.dma_start(x[:], xp[0:P, :]).then_inc(x_in, 16)
                pool.dma_start(rope[:, 0], io["t_rope"][0:P, :]).then_inc(rope_in, 16)
                with pool.Fori(1, NT) as i:
                    pool.wait_ge(xn_done, i)
                    pool.dma_start(x[:], xp[ds(i * P, P), :]).then_inc(x_in, 16)
                    pool.wait_ge(rope_rows, 4 * i + 4)
                    pool.dma_start(rope[:, 0], io["t_rope"][ds(i * P, P), :]).then_inc(rope_in, 16)
                pool.wait_ge(xn_done, NT)
                pool.dma_start(x[:TS], xs).then_inc(x_in, 16)
                pool.wait_ge(rope_rows, 4 * NT + 4)
                pool.dma_start(rope[:TS, 0], io["t_rope"][TP:T, :]).then_inc(rope_in, 16)

            @block.scalar
            def _(act):
                act.sem_inc(v_rows, 2)

                def prepare(i, w):
                    act.wait_ge(x_in, 16 * i + 16)
                    nc.scalar.activation(square[:w], x[:w], ACT.Square, accum_out=ss[:w]).then_inc(squared, 1)
                    act.wait_ge(mean_done, i + 1)
                    nc.scalar.activation(rms[:w], ms[:w], ACT.Sqrt).then_inc(root_done, 1)
                    act.wait_ge(rstd_done, i + 1)
                    nc.scalar.activation(xn[:w], x[:w], ACT.Copy, scale=rstd[:w]).then_inc(xn_done, 1)

                def tile(i, w, ahead):
                    act.wait_ge(proj_done, 6 * i + 6)
                    for n in range(2):
                        act.wait_ge(turned, 2 * i + n + 1)
                        if w == P:
                            for k in range(4 * n, 4 * n + 4):
                                h = nc.scalar.activation(hT[:, k, :], tp[:, k, :], ACT.Identity,
                                                         bias=keep.mod[:, SHIFT1 * KC + k, 0:1],
                                                         scale=keep.gs1[:, k, 0:1])
                            h.then_inc(h_done, 1)
                    if ahead:
                        prepare(i + 1, ahead)
                    for n, g in enumerate((2, 5)):
                        act.wait_ge(proj_done, 6 * i + n + 7)
                        act.wait_ge(stored, 80 * i + 80)
                        nc.scalar.activation(rows[:w, g], pj[:w, g], ACT.Copy).then_inc(v_rows, 1)

                prepare(0, P)
                with act.Fori(0, NT - 1) as i:
                    tile(i, P, P)
                tile(NT - 1, P, TS)
                tile(NT, TS, 0)

            @block.tensor
            def _(pe):
                pe.sem_inc(proj_done, 6)

                def turn_rows(i, w):
                    pe.wait_ge(xn_done, i + 1)
                    for k in range(KC):
                        t = nc.tensor.transpose(tp[:, k, :w], xn[:w, k * P:(k + 1) * P], keep.ident[:w, :w])
                        if k % 4 == 3:
                            t.then_inc(turned, 1)

                def tile(i, w, ahead):
                    pe.wait_ge(h_done, 2 * i + 2)
                    for n, g in enumerate(ORDER):
                        if n == 4 and ahead:
                            turn_rows(i + 1, ahead)
                        if g in ROPE:
                            pe.wait_ge(rope_rows, 4 * i + ROPE.index(g) + 1)
                        else:
                            pe.wait_ge(v_rows, 2 * i + (2, 5).index(g) + 1)
                        for k in range(KC):
                            mm = nc.tensor.matmul(pj[:w, g], hT[:, k, :w], win[:, k, g * GROUP:(g + 1) * GROUP],
                                                  start=(k == 0), stop=(k == KC - 1))
                        mm.then_inc(proj_done, 1)

                turn_rows(0, P)
                with pe.Fori(0, NT - 1) as i:
                    tile(i, P, P)
                tile(NT - 1, P, TS)
                tile(NT, TS, 0)

            @block.vector
            def _(v):
                v.sem_inc(rope_rows, 4)

                def norm(i, w):
                    v.wait_ge(squared, i + 1)
                    nc.vector.tensor_scalar(ms[:w], ss[:w], 1.0 / D, EPS, ALU.mult, ALU.add).then_inc(mean_done, 1)
                    v.wait_ge(root_done, i + 1)
                    nc.vector.reciprocal(rstd[:w], rms[:w]).then_inc(rstd_done, 1)

                def rotate(i, w):
                    v.wait_ge(rope_in, 16 * i + 16)
                    v.wait_ge(stored, 80 * i + 80)
                    for n, g in enumerate(ROPE):
                        v.wait_ge(proj_done, 6 * i + 9 + n)
                        src = pj[:w, g].rearrange("p (h t e) -> p h t e", t=2, e=HD // 2)
                        a = tA[:w].rearrange("p (h e) -> p h e", e=HD)
                        b = tB[:w].rearrange("p (h t e) -> p h t e", t=2, e=HD // 2)
                        cos = rope[:w, 0, 0:HD].unsqueeze(1).to_broadcast([w, 8, HD])
                        nsin = rope[:w, 0, HD:HD + 32].unsqueeze(1).to_broadcast([w, 8, HD // 2])
                        sin = rope[:w, 0, HD + 32:2 * HD].unsqueeze(1).to_broadcast([w, 8, HD // 2])
                        nc.vector.tensor_tensor(a, pj[:w, g].rearrange("p (h e) -> p h e", e=HD), cos, ALU.mult)
                        nc.vector.tensor_tensor(b[:, :, 0], src[:, :, 1], nsin, ALU.mult)
                        step(v, dve, nc.vector.tensor_tensor(b[:, :, 1], src[:, :, 0], sin, ALU.mult))
                        nc.vector.tensor_tensor(rows[:w, g], tA[:w], tB[:w], ALU.add).then_inc(rope_rows, 1)
                        v.wait_ge(rope_rows, 4 * i + 5 + n)

                norm(0, P)
                with v.Fori(0, NT - 1) as i:
                    dve.turn(i, 4)
                    norm(i + 1, P)
                    rotate(i, P)
                dve.turned(NT - 1)
                norm(NT, TS)
                rotate(NT - 1, P)
                for n in range(2):
                    v.wait_ge(turned, 2 * NT + n + 1)
                    for k in range(4 * n, 4 * n + 4):
                        hv = hT[:, k, 0:TS].rearrange("p (b q) -> p b q", b=NSEQ)
                        step(v, dve, nc.vector.tensor_tensor(hv, tp[:, k, 0:TS].rearrange("p (b q) -> p b q", b=NSEQ),
                                                             seq_bcast(keep.gs1[:, k, 1:NCOND]), ALU.mult))
                        h = nc.vector.tensor_tensor(hv, hv, seq_bcast(keep.mod[:, SHIFT1 * KC + k, 1:NCOND]), ALU.add)
                    h.then_inc(h_done, 1)
                rotate(NT, TS)


def prompt_attn(nc, io, keep):
    NB = NT
    with ExitStack() as ctx:
        def sb(name, shape, dt=F32):
            return ctx.enter_context(nc.sbuf_tensor(name, shape, dt))

        bias = sb("a_bias", [P, 2, TP])
        qk = sb("a_qk", [P, 2, 2, NB, P])
        vv = sb("a_vv", [P, 2, NB, P])
        qkT = sb("a_qkT", [P, 2, TP])
        S = sb("a_S", [P, 2, 2, TP])
        A = sb("a_A", [P, 2, TP])
        AT = sb("a_AT", [P, NB, P])
        mx = sb("a_mx", [P, 2, 2])
        nmx = sb("a_nmx", [P, 2, 2])
        sums = sb("a_sums", [P, 2, 2])
        rs = sb("a_rs", [P, 2, 2])
        pS = ctx.enter_context(nc.psum_tensor("a_pS", [P, 2, TP], F32))
        pT = ctx.enter_context(nc.psum_tensor("a_pT", [P, NB, P], F32))
        pO = ctx.enter_context(nc.psum_tensor("a_pO", [P, 2, 512], F32))

        bias_in = nc.alloc_semaphore("a_bias_in")
        qk_in = [nc.alloc_semaphore(f"a_qk_in{u}") for u in range(2)]
        v_in = [nc.alloc_semaphore(f"a_v_in{u}") for u in range(2)]
        turned = nc.alloc_semaphore("a_turned")
        turned_out = nc.alloc_semaphore("a_turned_out")
        scored = nc.alloc_semaphore("a_scored")
        max_done = nc.alloc_semaphore("a_max_done")
        exp_done = nc.alloc_semaphore("a_exp_done")
        probs = nc.alloc_semaphore("a_probs")
        probs_turned = nc.alloc_semaphore("a_probs_turned")
        probs_out = nc.alloc_semaphore("a_probs_out")
        mixed = nc.alloc_semaphore("a_mixed")
        mixed_out = nc.alloc_semaphore("a_mixed_out")
        dve = Steps(nc, "a_dve")
        held = nc.alloc_semaphore("a_held")
        NCH = D // P
        view = io["s_proj"][0:TP, :].rearrange("(i p) (g n) -> p i g n", p=P, g=6)

        def units(g):
            return 1 + g

        def each(eng, body, turn=None):
            for g in range(2):
                with eng.Fori(0, CH // 2) as i:
                    if turn:
                        turn(g, i)
                    for u in range(2):
                        c = 2 * i + u
                        body(g, u, c, 2 * g + i, CH * g + c, NB * CH * g + c * (NB * units(g)))
                if turn:
                    turn(g, None)

        with nc.Block() as block:
            @block.sync
            def _(sp):
                sp.dma_start(bias[:], io["t_prompt_bias"]).then_inc(bias_in, 16)

                def load(g, u, c, r, j, m0):
                    sp.wait_ge(turned, 4 * j + 4)
                    for t in range(2):
                        sp.dma_start(qk[:, u, t], view[:, :, 3 * g + t, ds(c * P, P)]).then_inc(qk_in[u], 16)
                    sp.wait_ge(mixed_out, NB * j + 2)
                    sp.dma_start(vv[:, u], view[:, :, 3 * g + 2, ds(c * P, P)]).then_inc(v_in[u], 16)
                each(sp, load)

            @block.tensor
            def _(pe):
                pe.sem_inc(turned, 8)
                pe.sem_inc(probs_turned, 1)

                def scores(i, j):
                    w = (i + 1) * P
                    for s in range(2):
                        pe.wait_ge(max_done, 2 * NB * j + 2 * i + s + 1)
                        for c0 in range(0, w, 512):
                            c1 = min(w, c0 + 512)
                            mm = nc.tensor.matmul(pS[:, s, c0:c1], qkT[HD * s:HD * s + HD, 0, i * P:(i + 1) * P],
                                                  qkT[HD * s:HD * s + HD, 1, c0:c1], start=True, stop=True)
                        mm.then_inc(scored, 1)

                def chunk(g, u, c, r, j, m0):
                    pe.wait_ge(qk_in[u], 32 * r + 32)
                    for n in range(4):
                        if n >= 2:
                            pe.wait_ge(turned_out, 4 * j + n - 1)
                        for k in range(4 * (n % 2), 4 * (n % 2) + 4):
                            tr = nc.tensor.transpose(pT[:, k, :], qk[:, u, n // 2, k, :], keep.ident[:])
                        tr.then_inc(turned, 1)
                    pe.wait_ge(turned_out, 4 * j + 4)
                    scores(0, j)
                    scores(1, j)
                    pe.wait_ge(v_in[u], 16 * r + 16)
                    for i in range(NB):
                        for s in range(units(g)):
                            m = m0 + i * units(g) + s
                            pe.wait_ge(probs, m + 1)
                            pe.wait_ge(probs_out, m + 1)
                            for k in range(i + 1):
                                tr = nc.tensor.transpose(pT[:, k, :], A[:, s, k * P:(k + 1) * P], keep.ident[:])
                            tr.then_inc(probs_turned, 1)
                            if i + 2 < NB and s == 0:
                                scores(i + 2, j)
                            pe.wait_ge(probs_out, m + 2)
                            pe.wait_ge(mixed_out, NB * j + i + 9)
                            for k in range(i + 1):
                                mm = nc.tensor.matmul(pO[:, i % 2, s * P:(s + 1) * P], vv[:, u, k, :], AT[:, k, :],
                                                      start=(k == 0), stop=(k == i))
                            mm.then_inc(mixed, 1)
                each(pe, chunk)

            @block.vector
            def _(v):
                v.sem_inc(max_done, 2)
                v.sem_inc(mixed_out, 10)
                v.wait_ge(bias_in, 16)

                def maxima(i, g, j):
                    w, e = (i + 1) * P, i % 2
                    for s in range(2):
                        v.wait_ge(scored, 2 * NB * j + 2 * i + s + 1)
                        hold(v, held)
                        step(v, dve, nc.vector.tensor_tensor_reduce(
                            S[:, e, s, 0:w], pS[:, s, 0:w], bias[:, g, TP - w:TP], SCALE, -3e38,
                            ALU.add, ALU.max, mx[:, e, s:s + 1]))
                        nc.vector.tensor_scalar(nmx[:, e, s:s + 1], mx[:, e, s:s + 1], -1.0, None,
                                                ALU.mult).then_inc(max_done, 1)

                def combine(i, g, j, m0):
                    w, e = (i + 1) * P, i % 2
                    for s in range(2):
                        v.wait_ge(exp_done, 2 * NB * j + 2 * i + s + 1)
                        step(v, dve, nc.vector.reciprocal(rs[:, e, s:s + 1], sums[:, e, s:s + 1]))
                    if g == 0:
                        step(v, dve, nc.vector.tensor_scalar(rs[:, e, 1:2], rs[:, e, 1:2], keep.neglam[:, 0:1],
                                                             None, ALU.mult))
                        v.wait_ge(probs_turned, m0 + i + 1)
                        step(v, dve, nc.vector.tensor_scalar(A[:, 0, 0:w], S[:, e, 0, 0:w], rs[:, e, 0:1], None,
                                                             ALU.mult))
                        nc.vector.scalar_tensor_tensor(out=A[:, 0, 0:w], in0=S[:, e, 1, 0:w],
                                                       scalar=rs[:, e, 1:2], in1=A[:, 0, 0:w], op0=ALU.mult,
                                                       op1=ALU.add).then_inc(probs, 1)
                    else:
                        for s in range(2):
                            v.wait_ge(probs_turned, m0 + 2 * i + (s if i else 1))
                            nc.vector.tensor_scalar(A[:, s, 0:w], S[:, e, s, 0:w], rs[:, e, s:s + 1], None,
                                                    ALU.mult).then_inc(probs, 1)

                def chunk(g, u, c, r, j, m0):
                    for n in range(4):
                        v.wait_ge(turned, 4 * j + n + 9)
                        b = 4 * (n % 2)
                        nc.vector.tensor_copy(qkT[:, n // 2, b * P:(b + 4) * P],
                                              pT[:, b:b + 4, :].rearrange("p k q -> p (k q)")).then_inc(turned_out, 1)
                    maxima(0, g, j)
                    maxima(1, g, j)
                    combine(0, g, j, m0)
                    for i in range(NB):
                        if i + 1 < NB:
                            combine(i + 1, g, j, m0)
                        if i + 2 < NB:
                            maxima(i + 2, g, j)
                        v.wait_ge(mixed, m0 + (i + 1) * units(g))
                        dst, e = keep.OT[:, ds(j, 1), i * P:(i + 1) * P], i % 2
                        if g == 0:
                            nc.vector.tensor_copy(dst, pO[:, e, 0:P].unsqueeze(1)).then_inc(mixed_out, 1)
                        else:
                            nc.vector.tensor_copy(dst[0:HD], pO[0:HD, e, 0:P].unsqueeze(1))
                            nc.vector.tensor_copy(dst[HD:P], pO[HD:P, e, P:2 * P].unsqueeze(1)).then_inc(mixed_out, 1)

                def turn(g, i):
                    if i is None:
                        dve.turned(CH // 2)
                    else:
                        dve.turn(i, 2 * NB * (6 - 2 * g))
                each(v, chunk, turn)

            @block.scalar
            def _(act):
                act.sem_inc(probs_out, 1)

                def exps(i, j):
                    w, e = (i + 1) * P, i % 2
                    for s in range(2):
                        act.wait_ge(max_done, 2 * NB * j + 2 * i + s + 3)
                        nc.scalar.activation(S[:, e, s, 0:w], S[:, e, s, 0:w], ACT.Exp, bias=nmx[:, e, s:s + 1],
                                             accum_out=sums[:, e, s:s + 1]).then_inc(exp_done, 1)

                def chunk(g, u, c, r, j, m0):
                    exps(0, j)
                    exps(1, j)
                    for i in range(NB):
                        for s in range(units(g)):
                            act.wait_ge(probs_turned, m0 + i * units(g) + s + 2)
                            nc.scalar.activation(AT[:, 0:i + 1, :], pT[:, 0:i + 1, :], ACT.Copy).then_inc(probs_out, 1)
                        if i + 2 < NB:
                            exps(i + 2, j)
                each(act, chunk)


def sample_attn(nc, io, keep):
    R = 2 * CH * SQ
    PG = 4
    NG = PAGES // PG
    ITEMS = NG * CH
    MEET = 9
    with ExitStack() as ctx:
        def sb(name, shape, dt=F32):
            return ctx.enter_context(nc.sbuf_tensor(name, shape, dt))

        bias = sb("s_bias", [R, 2, PAST + SQ])
        pages = sb("s_pages", [1, NSEQ * PAGES], I32)
        new = sb("s_new", [TS, PROJ])
        vnew = sb("s_vnew", [SQ, 2, GROUP])
        newT = sb("s_newT", [P, 2, 2 * CH, TS])
        kk = sb("s_kk", [P, 2, PG, GROUP])
        vv = sb("s_vv", [P, 2, PAGES, GROUP])
        kT = sb("s_kT", [P, 2, GROUP])
        qd = sb("s_qd", [P, 2, CH * (R + 2 * SQ)])
        S = sb("s_S", [R, 2, PAST + SQ])
        AT = sb("s_AT", [P, PAGES, R])
        ATn = sb("s_ATn", [SQ, R])
        mix = sb("s_mix", [R, GROUP])
        mx = sb("s_mx", [R, 2])
        nmx = sb("s_nmx", [R, 1])
        sums = sb("s_sums", [R, 1])
        rs = sb("s_rs", [R, 1])
        pK = ctx.enter_context(nc.psum_tensor("s_pK", [P, 2, 512], F32))
        pS = ctx.enter_context(nc.psum_tensor("s_pS", [P, PAST], F32))
        pN = ctx.enter_context(nc.psum_tensor("s_pN", [P, 512], F32))
        pA = ctx.enter_context(nc.psum_tensor("s_pA", [P, 512], F32))

        small_in = nc.alloc_semaphore("s_small_in")
        new_turned = nc.alloc_semaphore("s_new_turned")
        new_out = nc.alloc_semaphore("s_new_out")
        k_in = [nc.alloc_semaphore(f"s_k_in{n}") for n in range(2)]
        v_in = [nc.alloc_semaphore(f"s_v_in{g}") for g in range(2)]
        k_turned = nc.alloc_semaphore("s_k_turned")
        k_out = [nc.alloc_semaphore(f"s_k_out{n}") for n in range(2)]
        scored = nc.alloc_semaphore("s_scored")
        zeroed = nc.alloc_semaphore("s_zeroed")
        qd_done = nc.alloc_semaphore("s_qd_done")
        max_done = nc.alloc_semaphore("s_max_done")
        exp_done = nc.alloc_semaphore("s_exp_done")
        rs_done = nc.alloc_semaphore("s_rs_done")
        probs = nc.alloc_semaphore("s_probs")
        probs_turned = nc.alloc_semaphore("s_probs_turned")
        probs_out = nc.alloc_semaphore("s_probs_out")
        mixed = nc.alloc_semaphore("s_mixed")
        mixed_out = nc.alloc_semaphore("s_mixed_out")
        mix_rows = nc.alloc_semaphore("s_mix_rows")
        mix_turned = nc.alloc_semaphore("s_mix_turned")
        dve = Steps(nc, "s_dve")
        held = [nc.alloc_semaphore(f"s_held{n}") for n in range(3)]
        pools = [io[n][0].rearrange("n r h e -> n r (h e)") for n in ("cache_k_diff", "cache_v_diff")]
        states = [io[n][0].rearrange("b r h e -> b r (h e)") for n in ("state_k_win", "state_v_win")]
        NPOOL = pools[0].shape[0]

        def piped(front, back, meet):
            front(0, 0, None)

            def turn_of(b, more):
                front(b, 1, (b, 0))
                back(b, 0)
                if more:
                    front(b + 1, 0, (b, 1))
                else:
                    meet(b, 1)
                back(b, 1)
            return turn_of

        with nc.Block() as block:
            @block.sync
            def _(sp):
                sp.dma_start(pages[:], io["page_table"].rearrange("b g -> (b g)").unsqueeze(0)).then_inc(small_in, 16)
                sp.dma_start(bias[:], io["t_sample_bias"]).then_inc(small_in, 16)
                sp.dma_start(new[:], io["s_proj"][TP:T, :]).then_inc(small_in, 16)
                sp.wait_ge(small_in, 48)

                def source(t, b, g, p):
                    if g:
                        return states[t][ds(b, 1), p * P:(p + 1) * P].rearrange("a r n -> (a r) n")
                    page = sp.value_load(pages[0:1, ds(b * PAGES + p, 1)], min_val=0, max_val=NPOOL - 1)
                    return pools[t][ds(page, 1)].rearrange("a r n -> (a r) n")

                with sp.Fori(0, NSEQ) as b:
                    for g in range(2):
                        for n in range(NG):
                            sp.wait_ge(k_turned, CH * (NG * (2 * b + g) + n) + CH)
                            hold(sp, held[2])
                            for p in range(PG):
                                sp.dma_start(kk[:, n % 2, p, :], source(0, b, g, PG * n + p)).then_inc(k_in[n % 2], 16)
                            if n == 1:
                                sp.wait_ge(mixed, 2 * b + g + 1)
                                hold(sp, held[2])
                                sp.dma_start(vnew[:, g], io["s_proj"][ds(TP + SQ * b, SQ),
                                                                      (2 + 3 * g) * GROUP:(3 + 3 * g) * GROUP]
                                             ).then_inc(v_in[g], 16)
                            for p in {0: (), 1: range(8), 2: range(8, 12), 3: range(12, PAGES)}[n]:
                                sp.dma_start(vv[:, g, p, :], source(1, b, g, p)).then_inc(v_in[g], 16)

            @block.gpsimd
            def _(pool):
                nc.gpsimd.memset(qd[:], 0.0).then_inc(zeroed, 1)

            @block.tensor
            def _(pe):
                pe.sem_inc(k_turned, 2 * CH)
                pe.sem_inc(mixed, 2)
                pe.wait_ge(small_in, 48)
                for t in range(2):
                    for c in range(2 * CH):
                        g, n = c // CH, c % CH
                        col = (3 * g + t) * GROUP + n * P
                        tr = nc.tensor.transpose(pA[:, (t * 2 * CH + c) * TS:(t * 2 * CH + c + 1) * TS],
                                                 new[:, col:col + P], keep.ident[0:TS, 0:TS])
                tr.then_inc(new_turned, 1)
                pe.wait_ge(new_out, 1)

                def turn_probs(b, g):
                    u = 2 * b + g
                    pe.wait_ge(probs, u + 1)
                    pe.wait_ge(mixed_out, u + 1)
                    hold(pe, held[1])
                    for p in range(PAGES):
                        nc.tensor.transpose(pA[:, p * R:(p + 1) * R], S[:, g, p * P:(p + 1) * P], keep.ident[0:R, 0:R])
                    nc.tensor.transpose(pN[0:SQ, 0:R], S[:, g, PAST:PAST + SQ], keep.ident[0:R, 0:R]).then_inc(probs_turned, 1)

                def front(b, g, before):
                    u = 2 * b + g
                    pe.wait_ge(qd_done, u + 1)
                    pe.wait_ge(max_done, u + 1)

                    def turn_keys(m):
                        n, c = m // CH, m % CH
                        if c == 0:
                            pe.wait_ge(k_in[n % 2], 16 * PG * (2 * u + n // 2) + 16 * PG)
                        pe.wait_ge(k_out[m % 2], ITEMS // 2 * u + m // 2 + 1)
                        for p in range(PG):
                            tr = nc.tensor.transpose(pK[:, m % 2, p * P:(p + 1) * P], kk[:, n % 2, p, c * P:(c + 1) * P],
                                                     keep.ident[:])
                        tr.then_inc(k_turned, 1)

                    def score(m):
                        n, c = m // CH, m % CH
                        pe.wait_ge(k_out[m % 2], ITEMS // 2 * u + m // 2 + 2)
                        nc.tensor.matmul(pS[0:R, n * GROUP:(n + 1) * GROUP], qd[:, g, c * R:(c + 1) * R], kT[:, m % 2, :],
                                         start=(c == 0), stop=(c == CH - 1))

                    turn_keys(0)
                    for m in range(1, ITEMS):
                        turn_keys(m)
                        score(m - 1)
                        if m == MEET and before is not None:
                            turn_probs(*before)
                    score(ITEMS - 1)
                    for c in range(CH):
                        mm = nc.tensor.matmul(pK[0:R, 0, 0:SQ], qd[:, g, c * R:(c + 1) * R],
                                              newT[:, 1, CH * g + c, ds(SQ * b, SQ)], start=(c == 0), stop=(c == CH - 1))
                    mm.then_inc(scored, 1)

                def back(b, g):
                    u = 2 * b + g
                    pe.wait_ge(v_in[g], 16 * (PAGES + 1) * b + 16 * (PAGES + 1))
                    pe.wait_ge(probs_out, u + 1)
                    for p in range(PAGES):
                        nc.tensor.matmul(pA[0:R, :], AT[:, p, :], vv[:, g, p, :], start=(p == 0), stop=False)
                    nc.tensor.matmul(pA[0:R, :], ATn[:], vnew[:, g, :], start=False, stop=True).then_inc(mixed, 1)
                    pe.wait_ge(mix_rows, u + 1)
                    hold(pe, held[1])
                    for c in range(CH):
                        tr = nc.tensor.transpose(pN[:, c * R:(c + 1) * R], mix[:, c * P:(c + 1) * P], keep.ident[0:R, 0:R])
                    tr.then_inc(mix_turned, 1)

                turn_of = piped(front, back, turn_probs)
                with pe.Fori(0, NSEQ - 1) as b:
                    turn_of(b, True)
                turn_of(NSEQ - 1, False)

            @block.vector
            def _(v):
                v.sem_inc(k_out[1], 1)
                v.wait_ge(small_in, 48)
                v.sem_inc(max_done, 1)
                v.sem_inc(mixed_out, 1)
                v.wait_ge(new_turned, 1)
                nc.vector.tensor_copy(newT[:].rearrange("p t c q -> p (t c q)"), pA[:]).then_inc(new_out, 1)
                v.wait_ge(new_out, 1)
                v.wait_ge(zeroed, 1)

                def probs_away(b, g):
                    v.wait_ge(probs_turned, 2 * b + g + 1)
                    nc.vector.tensor_copy(AT[:].rearrange("p a r -> p (a r)"), pA[:])
                    nc.vector.tensor_copy(ATn[:], pN[0:SQ, 0:R]).then_inc(probs_out, 1)

                def front(b, g, before):
                    u = 2 * b + g
                    for s in range(2):
                        h = nc.vector.tensor_copy(
                            qd[HD * s:HD * s + HD, g].rearrange("p (c r) -> p c r", c=CH)[:, :, SQ * s:SQ * s + SQ],
                            newT[HD * s:HD * s + HD, 0, CH * g:CH * g + CH, ds(SQ * b, SQ)])
                    h.then_inc(qd_done, 1)
                    for m in range(1, ITEMS, 2):
                        v.wait_ge(k_turned, ITEMS * u + m + 1 + 2 * CH)
                        nc.vector.tensor_copy(kT[:, 1, :], pK[:, 1, :]).then_inc(k_out[1], 1)
                        if m == MEET and before is not None:
                            probs_away(*before)
                    v.wait_ge(scored, u + 1)
                    hold(v, held[0])
                    nc.vector.tensor_tensor_reduce(S[:, g, 0:PAST], pS[0:R, :], bias[:, g, 0:PAST], SCALE, -3e38,
                                                   ALU.add, ALU.max, mx[:, 0:1])
                    step(v, dve, nc.vector.tensor_tensor_reduce(S[:, g, PAST:PAST + SQ], pK[0:R, 0, 0:SQ],
                                                                bias[:, g, PAST:PAST + SQ], SCALE, -3e38,
                                                                ALU.add, ALU.max, mx[:, 1:2]))
                    nc.vector.tensor_scalar(nmx[:], mx[:, 0:1], mx[:, 1:2], -1.0, ALU.max, ALU.mult).then_inc(max_done, 1)
                    v.wait_ge(exp_done, u + 1)
                    step(v, dve, nc.vector.reciprocal(rs[:], sums[:]))
                    nc.vector.tensor_tensor(rs[:], rs[:], keep.sign[:, g:g + 1], ALU.mult).then_inc(rs_done, 1)

                def back(b, g):
                    u = 2 * b + g
                    v.wait_ge(mixed, u + 3)
                    nc.vector.tensor_copy(mix[:], pA[0:R, :]).then_inc(mix_rows, 1)
                    v.wait_ge(mix_turned, u + 1)
                    got = pN[:, 0:CH * R].rearrange("p (c d s q) -> p c d s q", c=CH, d=CH, s=2)
                    for c in range(CH):
                        dst = keep.OT[:, CH * g + c, ds(TP + SQ * b, SQ)]
                        if g == 0:
                            step(v, dve, nc.vector.tensor_copy(dst, got[:, c, c, 0]))
                            x = nc.vector.tensor_tensor(dst, dst, got[:, c, c, 1], ALU.add)
                        else:
                            nc.vector.tensor_copy(dst[0:HD], got[0:HD, c, c, 0])
                            x = nc.vector.tensor_copy(dst[HD:P], got[HD:P, c, c, 1])
                    x.then_inc(mixed_out, 1)

                turn_of = piped(front, back, probs_away)
                with v.Fori(0, NSEQ - 1) as b:
                    dve.turn(b, 2 * 2 + CH)
                    turn_of(b, True)
                dve.turned(NSEQ - 1)
                turn_of(NSEQ - 1, False)

            @block.scalar
            def _(act):
                act.sem_inc(k_out[0], 1)

                def front(b, g):
                    u = 2 * b + g
                    for m in range(0, ITEMS, 2):
                        act.wait_ge(k_turned, ITEMS * u + m + 1 + 2 * CH)
                        nc.scalar.activation(kT[:, 0, :], pK[:, 0, :], ACT.Copy).then_inc(k_out[0], 1)
                    act.wait_ge(max_done, u + 2)
                    nc.scalar.activation(S[:, g, :], S[:, g, :], ACT.Exp, bias=nmx[:], accum_out=sums[:]).then_inc(exp_done, 1)
                    act.wait_ge(rs_done, u + 1)
                    nc.scalar.activation(S[:, g, :], S[:, g, :], ACT.Copy, scale=rs[:]).then_inc(probs, 1)

                with act.Fori(0, NSEQ) as b:
                    for g in range(2):
                        front(b, g)


NBK = 3
W = T // NBK
WP = TP - 2 * W


def by_seq(ap):
    return ap.rearrange("p (b q) -> p b q", b=NSEQ)


def mix_out(nc, io, keep):
    with ExitStack() as ctx:
        def sb(name, shape, dt=F32):
            return ctx.enter_context(nc.sbuf_tensor(name, shape, dt))

        XS = 5
        xT = sb("o_xT", [P, KC, T])
        x = sb("o_x", [P, XS, D])
        wo = sb("o_wo", [P, 2, KC, P])
        sq = sb("o_sq", [P, 2, T])
        rstd = sb("o_rstd", [P, T])
        sub = sb("o_sub", [P, 1])
        small = sb("o_small", [P, 2, TS])
        ps = ctx.enter_context(nc.psum_tensor("o_ps", [P, 6, 512], F32))
        pt = ctx.enter_context(nc.psum_tensor("o_pt", [P, KC, P], F32))

        squared = nc.alloc_semaphore("o_squared")
        summed = nc.alloc_semaphore("o_summed")
        mean_done = nc.alloc_semaphore("o_mean_done")
        rooted = nc.alloc_semaphore("o_rooted")
        normed = nc.alloc_semaphore("o_normed")
        x_in = [nc.alloc_semaphore(f"o_x_in{u}") for u in range(XS)]
        x_turned = nc.alloc_semaphore("o_x_turned")
        x_out = nc.alloc_semaphore("o_x_out")
        wo_in = [nc.alloc_semaphore(f"o_wo_in{u}") for u in range(2)]
        mixed = nc.alloc_semaphore("o_mixed")
        added = nc.alloc_semaphore("o_added")
        x_squared = nc.alloc_semaphore("o_x_squared")
        x_summed = nc.alloc_semaphore("o_x_summed")
        shifted = nc.alloc_semaphore("o_shifted")
        hi_done = nc.alloc_semaphore("o_hi_done")
        lo_done = nc.alloc_semaphore("o_lo_done")
        stored = nc.alloc_semaphore("o_stored")
        dve = Steps(nc, "o_dve")
        wview = io["w_o"][0].rearrange("(k p) n -> p k n", p=P)
        GSUB = NMOD + 3 * KC

        def x_tiles(c):
            return range(2 * c, NT + 1 if c == CH - 1 else 2 * c + 2)

        def x_rows(i):
            return io["x_prompt"][0, i * P:(i + 1) * P, :] if i < NT else io["x_sample"].rearrange("b q d -> (b q) d")

        with nc.Block() as block:
            @block.sync
            def _(sp):
                for i in range(NT + 1):
                    if i >= XS:
                        sp.wait_ge(x_turned, 2 * (i - XS + 1))
                    sp.dma_start(x[0:(P if i < NT else TS), i % XS], x_rows(i)).then_inc(x_in[i % XS], 16)
                for u in range(2):
                    sp.dma_start(wo[:, u], wview[:, :, u * P:(u + 1) * P]).then_inc(wo_in[u], 16)
                with sp.Fori(1, KC // 2) as i:
                    for u in range(2):
                        sp.wait_ge(mixed, 2 * i + u - 1)
                        sp.dma_start(wo[:, u], wview[:, :, ds((2 * i + u) * P, P)]).then_inc(wo_in[u], 16)
                sp.wait_ge(added, KC + 2)
                sp.dma_start(io["s_x"], xT[:]).then_inc(stored, 16)
                sp.wait_ge(stored, 16)

            @block.scalar
            def _(act):
                for c in range(CH):
                    act.wait_ge(normed, c + 1)
                    nc.scalar.activation(sq[:, 0:1, :], keep.OT[:, ds(c, 1), :], ACT.Square).then_inc(squared, 1)
                    act.wait_ge(mean_done, c + 1)
                    nc.scalar.activation(rstd[:], rstd[:], ACT.Sqrt).then_inc(rooted, 1)
                    for i in x_tiles(c):
                        w = P if i < NT else TS
                        for n in range(2):
                            act.wait_ge(x_turned, 2 * i + n + 1)
                            nc.scalar.activation(xT[:, 4 * n:4 * n + 4, i * P:i * P + w], pt[:, 4 * n:4 * n + 4, 0:w],
                                                 ACT.Copy).then_inc(x_out, 1)
                for k in range(KC):
                    act.wait_ge(added, k + 3)
                    if k >= 2:
                        act.wait_ge(x_summed, k - 1)
                    nc.scalar.activation(sq[:, k % 2], xT[:, k], ACT.Square).then_inc(x_squared, 1)
                act.wait_ge(mean_done, CH + 1)
                nc.scalar.activation(rstd[:], rstd[:], ACT.Sqrt).then_inc(rooted, 1)
                for k in range(KC):
                    act.wait_ge(shifted, k + 1)
                    nc.scalar.activation(keep.hi[:, k], sq[:, k % 2], ACT.Copy).then_inc(hi_done, 1)

            @block.tensor
            def _(pe):
                for c in range(CH):
                    pe.wait_ge(squared, c + 1)
                    for b in range(NBK):
                        mm = nc.tensor.matmul(ps[:, b, 0:W], keep.ones[:], sq[:, 0, b * W:(b + 1) * W],
                                              start=True, stop=True)
                    mm.then_inc(summed, 1)
                    for i in x_tiles(c):
                        w = P if i < NT else TS
                        pe.wait_ge(x_in[i % XS], 16 * (i // XS) + 16)
                        for n in range(2):
                            if i:
                                pe.wait_ge(x_out, 2 * i + n - 1)
                            for k in range(4 * n, 4 * n + 4):
                                tr = nc.tensor.transpose(pt[:, k, 0:w], x[0:w, i % XS, k * P:(k + 1) * P],
                                                         keep.ident[0:w, 0:w])
                            tr.then_inc(x_turned, 1)
                pe.wait_ge(normed, CH + 1)
                with pe.Fori(0, KC // 2) as i:
                    for u in range(2):
                        pe.wait_ge(wo_in[u], 16 * i + 16)
                        pe.wait_ge(added, 2 * i + u + 1)
                        for b in range(NBK):
                            for k in range(KC):
                                mm = nc.tensor.matmul(ps[:, 3 * u + b, 0:W], wo[:, u, k, :],
                                                      keep.OT[:, k, b * W:(b + 1) * W], start=(k == 0), stop=(k == KC - 1))
                        mm.then_inc(mixed, 1)
                pe.wait_ge(added, KC + 2)
                for k in range(KC):
                    pe.wait_ge(x_squared, k + 1)
                    for b in range(NBK):
                        mm = nc.tensor.matmul(ps[:, b, 0:W], keep.ones[:], sq[:, k % 2, b * W:(b + 1) * W],
                                              start=(k == 0), stop=(k == KC - 1), skip_group_check=True)
                    mm.then_inc(x_summed, 1)

            @block.vector
            def _(v):
                v.sem_inc(normed, 1)
                v.sem_inc(added, 2)
                step(v, dve, nc.vector.tensor_scalar(sub[:], keep.param[:, GSUB:GSUB + 1], 1.0 - LAM_INIT, None, ALU.mult))
                with v.Fori(0, CH) as c:
                    dve.turn(c, 1)
                    v.wait_ge(summed, c + 1)
                    nc.vector.tensor_scalar(rstd[:].rearrange("p (b w) -> p b w", b=NBK), ps[:, 0:NBK, 0:W], 1.0 / P,
                                            SUBLN_EPS, ALU.mult, ALU.add).then_inc(mean_done, 1)
                    v.wait_ge(rooted, c + 1)
                    step(v, dve, nc.vector.reciprocal(rstd[:], rstd[:]))
                    head = keep.OT[:, ds(c, 1), :].rearrange("p a t -> p (a t)")
                    nc.vector.scalar_tensor_tensor(out=head, in0=head, scalar=sub[:], in1=rstd[:], op0=ALU.mult,
                                                   op1=ALU.mult).then_inc(normed, 1)
                    v.wait_ge(normed, c + 2)
                dve.turned(CH)
                v.wait_ge(x_out, 2 * (NT + 1))
                with v.Fori(0, KC // 2) as i:
                    dve.turn(i, 2)
                    for u in range(2):
                        k = 2 * i + u
                        v.wait_ge(mixed, k + 1)
                        gate = keep.mod[:, ds(GATE1 * KC + k, 1), :].rearrange("p a s -> p (a s)")
                        row = xT[:, ds(k, 1), :].rearrange("p a t -> p (a t)")
                        step(v, dve, nc.vector.tensor_tensor(by_seq(small[:, u]), by_seq(ps[:, 3 * u + 2, WP:W]),
                                                             seq_bcast(gate[:, 1:NCOND]), ALU.mult))
                        nc.vector.tensor_tensor(row[:, TP:T], row[:, TP:T], small[:, u], ALU.add)
                        for b in range(NBK):
                            w = W if b < 2 else WP
                            cols = row[:, b * W:b * W + w]
                            h = nc.vector.scalar_tensor_tensor(out=cols, in0=ps[:, 3 * u + b, 0:w], scalar=gate[:, 0:1],
                                                               in1=cols, op0=ALU.mult, op1=ALU.add)
                        h.then_inc(added, 1)
                dve.turned(KC // 2)
                v.wait_ge(x_summed, KC)
                nc.vector.tensor_scalar(rstd[:].rearrange("p (b w) -> p b w", b=NBK), ps[:, 0:NBK, 0:W], 1.0 / D,
                                        EPS, ALU.mult, ALU.add).then_inc(mean_done, 1)
                v.wait_ge(rooted, CH + 1)
                step(v, dve, nc.vector.reciprocal(rstd[:], rstd[:]))
                for k in range(KC):
                    h = sq[:, k % 2]
                    if k >= 2:
                        v.wait_ge(lo_done, k - 1)
                    nc.vector.scalar_tensor_tensor(out=h[:, 0:TP], in0=xT[:, k, 0:TP], scalar=keep.gs2[:, k, 0:1],
                                                   in1=rstd[:, 0:TP], op0=ALU.mult, op1=ALU.mult)
                    step(v, dve, nc.vector.tensor_tensor(by_seq(h[:, TP:T]), by_seq(xT[:, k, TP:T]),
                                                         seq_bcast(keep.gs2[:, k, 1:NCOND]), ALU.mult))
                    step(v, dve, nc.vector.tensor_tensor(h[:, TP:T], h[:, TP:T], rstd[:, TP:T], ALU.mult))
                    shift = keep.mod[:, SHIFT2 * KC + k]
                    nc.vector.tensor_tensor(by_seq(h[:, TP:T]), by_seq(h[:, TP:T]), seq_bcast(shift[:, 1:NCOND]), ALU.add)
                    nc.vector.tensor_scalar(h[:, 0:TP], h[:, 0:TP], shift[:, 0:1], None, ALU.add).then_inc(shifted, 1)

            @block.gpsimd
            def _(pool):
                for k in range(KC):
                    pool.wait_ge(hi_done, k + 1)
                    nc.gpsimd.tensor_tensor(keep.lo[:, k], sq[:, k % 2], keep.hi[:, k], ALU.subtract).then_inc(lo_done, 1)


def split_product(nc, out, lhs_hi, lhs_lo, rhs_hi, rhs_lo, start, stop):
    nc.tensor.matmul(out, lhs_hi, rhs_hi, start=start, stop=False)
    nc.tensor.matmul(out, lhs_hi, rhs_lo, start=False, stop=False)
    return nc.tensor.matmul(out, lhs_lo, rhs_hi, start=False, stop=stop)


def peer_scores(nc, io, keep):
    with ExitStack() as ctx:
        def sb(name, shape, dt=F32):
            return ctx.enter_context(nc.sbuf_tensor(name, shape, dt))

        wq = sb("q_wq", [P, 2, KC, P])
        wh = sb("q_wh", [P, 2, KC, P], F32R)
        wl = sb("q_wl", [P, 2, KC, P], F32R)
        keys = sb("q_keys", [P, 2, P])
        keysT = sb("q_keysT", [P, 2, P])
        qT = sb("q_qT", [P, 2, T])
        S = sb("q_S", [P, 2, NT + 1, NK])
        pq = ctx.enter_context(nc.psum_tensor("q_pq", [P, NBK, 512], F32))
        pk = ctx.enter_context(nc.psum_tensor("q_pk", [P, 512], F32))
        pS = ctx.enter_context(nc.psum_tensor("q_pS", [P, NBK, 4, NK], F32))

        wq_in = [nc.alloc_semaphore(f"q_wq_in{u}") for u in range(2)]
        keys_in = [nc.alloc_semaphore(f"q_keys_in{u}") for u in range(2)]
        hi_done = nc.alloc_semaphore("q_hi_done")
        lo_done = nc.alloc_semaphore("q_lo_done")
        keys_turned = nc.alloc_semaphore("q_keys_turned")
        keys_out = nc.alloc_semaphore("q_keys_out")
        queried = nc.alloc_semaphore("q_queried")
        q_out = nc.alloc_semaphore("q_out")
        scored = nc.alloc_semaphore("q_scored")
        s_out = nc.alloc_semaphore("q_s_out")
        held = nc.alloc_semaphore("q_held")
        stored = [nc.alloc_semaphore(f"q_stored{u}") for u in range(2)]
        wview = io["peer_wq"][0].rearrange("(k p) n -> p k n", p=P)
        kview = io["peer_keys"][0].rearrange("h c n d -> (h c) n d")

        def each(eng, body):
            with eng.Fori(0, NHC // 2) as i:
                for u in range(2):
                    body(i, u, 2 * i + u)

        with nc.Block() as block:
            @block.sync
            def _(sp):
                for u in range(2):
                    sp.sem_inc(stored[u], 32)
                    sp.dma_start(wq[:, u], wview[:, :, u * P:(u + 1) * P]).then_inc(wq_in[u], 16)
                    sp.dma_start(keys[:, u], kview[u]).then_inc(keys_in[u], 16)

                def turn(i, u, c, more):
                    if more:
                        sp.wait_ge(lo_done, c + 1)
                        sp.dma_start(wq[:, u], wview[:, :, ds((c + 2) * P, P)]).then_inc(wq_in[u], 16)
                        sp.wait_ge(keys_turned, c + 1)
                        sp.dma_start(keys[:, u], kview[ds(c + 2, 1)].rearrange("a n d -> (a n) d")).then_inc(keys_in[u], 16)
                    sp.wait_ge(s_out, c + 2)
                    sp.dma_start(io["s_s"][0:TP, ds(c, 1), :].rearrange("(i p) a n -> p i (a n)", p=P),
                                 S[:, u, 0:NT]).then_inc(stored[u], 16)
                    sp.dma_start(io["s_s"][TP:T, ds(c, 1), :].rearrange("p a n -> p (a n)"),
                                 S[0:TS, u, NT]).then_inc(stored[u], 16)

                with sp.Fori(0, NHC // 2 - 1) as i:
                    for u in range(2):
                        turn(i, u, 2 * i + u, True)
                for u in range(2):
                    turn(None, u, NHC - 2 + u, False)
                for u in range(2):
                    sp.wait_ge(stored[u], 32 * (NHC // 2) + 32)

            @block.gpsimd
            def _(pool):
                def split(i, u, c):
                    pool.wait_ge(wq_in[u], 16 * i + 16)
                    pool.wait_ge(queried, c + 1)
                    hold(pool, held)
                    nc.gpsimd.tensor_copy(wh[:, u], wq[:, u]).then_inc(hi_done, 1)
                    pool.wait_ge(hi_done, c + 1)
                    nc.gpsimd.tensor_tensor(wl[:, u], wq[:, u], wh[:, u], ALU.subtract).then_inc(lo_done, 1)
                each(pool, split)

            @block.tensor
            def _(pe):
                pe.sem_inc(queried, 2)

                def turn(i, u, c):
                    pe.wait_ge(keys_in[u], 16 * i + 16)
                    pe.wait_ge(keys_out, c + 1)
                    nc.tensor.transpose(pk[:, 0:P], keys[:, u, :], keep.ident[:]).then_inc(keys_turned, 1)
                    pe.wait_ge(lo_done, c + 1)
                    pe.wait_ge(q_out, c + 1)
                    for b in range(NBK):
                        cols = slice(b * W, (b + 1) * W)
                        for k in range(KC):
                            mm = split_product(nc, pq[:, b, 0:W], wh[:, u, k, :], wl[:, u, k, :], keep.hi[:, k, cols],
                                               keep.lo[:, k, cols], k == 0, k == KC - 1)
                    mm.then_inc(queried, 1)
                    pe.wait_ge(keys_out, c + 2)
                    pe.wait_ge(q_out, c + 2)
                    pe.wait_ge(s_out, c + 1)
                    for i in range(NT + 1):
                        w = P if i < NT else TS
                        mm = nc.tensor.matmul(pS[0:w, i // 4, i % 4, :], qT[:, u, i * P:i * P + w], keysT[:, u, :],
                                              start=True, stop=True)
                    mm.then_inc(scored, 1)
                each(pe, turn)

            @block.scalar
            def _(act):
                act.sem_inc(q_out, 1)

                def turn(i, u, c):
                    act.wait_ge(queried, c + 3)
                    nc.scalar.activation(qT[:, u].rearrange("p (b w) -> p b w", b=NBK), pq[:, :, 0:W],
                                         ACT.Copy).then_inc(q_out, 1)
                each(act, turn)

            @block.vector
            def _(v):
                v.sem_inc(keys_out, 1)
                v.sem_inc(s_out, 1)

                def turn(i, u, c):
                    v.wait_ge(keys_turned, c + 1)
                    nc.vector.tensor_copy(keysT[:, u, :], pk[:, 0:P]).then_inc(keys_out, 1)
                    v.wait_ge(scored, c + 1)
                    v.wait_ge(stored[u], 32 * i + 32)
                    nc.vector.tensor_copy(S[:, u, 0:NT].rearrange("p (b i) n -> p b i n", b=2), pS[:, 0:2])
                    nc.vector.tensor_copy(S[0:TS, u, NT], pS[0:TS, 2, 0]).then_inc(s_out, 1)
                each(v, turn)


def peer_route(nc, io, keep):
    HALF = P // 2
    GT = 4
    SLOTS = 4
    BEST = 8
    NEAR, FEW = 4, 4
    CAND = NEAR * TOPK + (TOPK - NEAR) * FEW
    with ExitStack() as ctx:
        def sb(name, shape, dt=F32):
            return ctx.enter_context(nc.sbuf_tensor(name, shape, dt))

        room = keep.OT[:].rearrange("p k t -> p (k t)")
        s, rest = (room[:, n * NHC * NK:(n + 1) * NHC * NK].rearrange("p (c n) -> p c n", n=NK) for n in range(2))
        top = sb("r_top", [P, NHC, TOPK])
        at = sb("r_at", [P, NHC, TOPK], U32)
        atf = sb("r_atf", [P, NHC, TOPK])
        sums = sb("r_sums", [P, PH, TOPK * TOPK])
        best = sb("r_best", [P, PH, TOPK])
        place = sb("r_place", [P, PH, TOPK], U32)
        part = sb("r_part", [P, 4, PH * TOPK], U32)
        partf = sb("r_partf", [P, 4, PH * TOPK])
        far = sb("r_far", [P, PH * TOPK])
        pick = sb("r_pick", [P, 3, PH * TOPK])
        den = sb("r_den", [P, PH])
        rden = sb("r_rden", [P, PH])
        pickT = sb("r_pickT", [P, 4, P])
        hot1 = sb("r_hot1", [P, SLOTS, GT, NK])
        hot2 = sb("r_hot2", [P, SLOTS, GT, NK])
        off = sb("r_off", [P, 2, SLOTS, NK])
        second = sb("r_second", [P, SLOTS, GT])
        G = sb("r_G", [P, 2, NK, HALF])
        pp = ctx.enter_context(nc.psum_tensor("r_pp", [P, 512], F32))
        pG = ctx.enter_context(nc.psum_tensor("r_pG", [P, SLOTS, GT, NK], F32))

        s_in = nc.alloc_semaphore("r_s_in")
        s_used = nc.alloc_semaphore("r_s_used")
        shifted = nc.alloc_semaphore("r_shifted")
        exp_done = nc.alloc_semaphore("r_exp_done")
        picked = nc.alloc_semaphore("r_picked")
        pick_turned = nc.alloc_semaphore("r_pick_turned")
        pick_out = nc.alloc_semaphore("r_pick_out")
        hot1_done = nc.alloc_semaphore("r_hot1_done")
        hot2_done = nc.alloc_semaphore("r_hot2_done")
        off_done = nc.alloc_semaphore("r_off_done")
        last_done = nc.alloc_semaphore("r_last_done")
        spread = nc.alloc_semaphore("r_spread")
        g_out = nc.alloc_semaphore("r_g_out")
        stored = [nc.alloc_semaphore(f"r_stored{n}") for n in range(2)]
        held = nc.alloc_semaphore("r_held")
        pool_held = nc.alloc_semaphore("r_pool_held")
        second_done = nc.alloc_semaphore("r_second_done")
        dve = Steps(nc, "r_dve")
        NGT = P // GT
        gview = io["s_g"].rearrange("i j t -> j i t")

        def halves(eng, w, body):
            for h in range(2 if w == P else 1):
                n = NGT // 2 if w == P else w // GT
                with eng.Fori(0, n // SLOTS) as r:
                    body(h, n // SLOTS * h + r, SLOTS * r)

        def each(eng, body):
            with eng.Fori(0, NT) as i:
                body(i, P)
            body(NT, TS)

        with nc.Block() as block:
            @block.sync
            def _(sp):
                for n in range(2):
                    sp.sem_inc(stored[n], 16)

                def store(i, w, t0):
                    for h in range(2 if w == P else 1):
                        sp.wait_ge(g_out, NGT * i + (NGT // 2 * (h + 1) if w == P else w // GT) + SLOTS)
                        m = min(w, HALF)
                        sp.dma_start(gview[:, :, ds(t0 + HALF * h, m)], G[:, h, :, 0:m]).then_inc(stored[h], 16)

                sp.dma_start(s, io["s_s"][0:P]).then_inc(s_in, 16)
                sp.wait_ge(s_used, 1)
                sp.dma_start(s, io["s_s"][P:2 * P]).then_inc(s_in, 16)
                with sp.Fori(2, NT) as i:
                    sp.wait_ge(s_used, i)
                    sp.dma_start(s, io["s_s"][ds(i * P, P)]).then_inc(s_in, 16)
                    store(i - 2, P, (i - 2) * P)
                sp.wait_ge(s_used, NT)
                sp.dma_start(s[0:TS], io["s_s"][TP:T]).then_inc(s_in, 16)
                store(NT - 2, P, TP - 2 * P)
                store(NT - 1, P, TP - P)
                store(NT, TS, TP)
                sp.wait_ge(stored[0], 16 * (NT + 1) + 16)
                sp.wait_ge(stored[1], 16 * NT + 16)

            @block.vector
            def _(v):
                def rows(i, g):
                    v.wait_ge(spread, NGT * i + g + 1)
                    for t in range(GT - 1):
                        col = slice(GT * g + t, GT * g + t + 1)
                        x = nc.vector.tensor_scalar(hot1[:, g % SLOTS, t], keep.iota[:], pickT[:, 0, col], pickT[:, 2, col],
                                                    ALU.is_equal, ALU.mult)
                    x.then_inc(hot1_done, 1)

                def search(i, w, between):
                    def two(ap, c):
                        return ap[0:w].rearrange("p (h c) k -> p h c k", c=2)[:, :, c]

                    v.wait_ge(s_in, 16 * i + 16)
                    hold(v, held)
                    for lo in (0, BEST):
                        src = s if lo == 0 else rest
                        for c in range(NHC):
                            x = nc.vector.max(top[0:w, c, lo:lo + BEST], src[0:w, c])
                            if c % 4 == 1:
                                between()
                        step(v, dve, x)
                        hold(v, held)
                        for c in range(NHC):
                            x = nc.vector.max_index(at[0:w, c, lo:lo + BEST], top[0:w, c, lo:lo + BEST], src[0:w, c])
                            if lo == 0:
                                x = nc.vector.match_replace(rest[0:w, c], top[0:w, c, 0:BEST], s[0:w, c], -3e38)
                            if c % 4 == 1:
                                between()
                        if lo == 0:
                            x.then_inc(s_used, 1)
                            v.wait_ge(s_used, i + 1)
                            hold(v, held)
                        else:
                            step(v, dve, x)
                    for a, b, lo, hi in ((slice(0, NEAR), TOPK, 0, NEAR * TOPK), (slice(NEAR, TOPK), FEW, NEAR * TOPK, CAND)):
                        na = a.stop - a.start
                        nc.vector.tensor_tensor(
                            sums[0:w, :, lo:hi].rearrange("p h (a b) -> p h a b", a=na),
                            two(top, 0)[:, :, a].unsqueeze(3).to_broadcast([w, PH, na, b]),
                            two(top, 1)[:, :, 0:b].unsqueeze(2).to_broadcast([w, PH, na, b]), ALU.add)
                    step(v, dve, nc.vector.tensor_copy(atf[0:w], at[0:w]))
                    between()
                    hold(v, held)
                    other = rest.rearrange("p c n -> p (c n)").rearrange("p (h n) -> p h n", h=PH)
                    for lo in (0, BEST):
                        src = sums if lo == 0 else other
                        for h in range(PH):
                            x = nc.vector.max(best[0:w, h, lo:lo + BEST], src[0:w, h, 0:CAND])
                            if h % 4 == 1:
                                between()
                        step(v, dve, x)
                        hold(v, held)
                        for h in range(PH):
                            x = nc.vector.max_index(place[0:w, h, lo:lo + BEST], best[0:w, h, lo:lo + BEST], src[0:w, h, 0:CAND])
                            if lo == 0:
                                x = nc.vector.match_replace(other[0:w, h, 0:CAND], best[0:w, h, 0:BEST],
                                                             sums[0:w, h, 0:CAND], -3e38)
                            if h % 4 == 1:
                                between()
                        step(v, dve, x)
                        hold(v, held)
                    flat = place[0:w].rearrange("p h k -> p (h k)")
                    wgt = pick[0:w, 2].rearrange("p (h k) -> p h k", h=PH)
                    nc.vector.tensor_tensor(wgt, best[0:w], best[0:w, :, 0:1].to_broadcast([w, PH, TOPK]),
                                            ALU.subtract).then_inc(shifted, 1)
                    nc.vector.tensor_scalar(part[0:w, 0], flat, 4, None, ALU.logical_shift_right)
                    nc.vector.tensor_scalar(part[0:w, 1], flat, TOPK - 1, None, ALU.bitwise_and)
                    nc.vector.tensor_scalar(part[0:w, 2], flat, 2, None, ALU.logical_shift_right)
                    step(v, dve, nc.vector.tensor_scalar(part[0:w, 3], flat, FEW - 1, None, ALU.bitwise_and))
                    step(v, dve, nc.vector.tensor_copy(partf[0:w], part[0:w]))
                    between()
                    nc.vector.tensor_scalar(far[0:w], partf[0:w, 0], float(NEAR), None, ALU.is_ge)
                    step(v, dve, nc.vector.tensor_tensor(partf[0:w, 2:4], partf[0:w, 2:4], partf[0:w, 0:2], ALU.subtract))
                    step(v, dve, nc.vector.tensor_tensor(partf[0:w, 2:4], partf[0:w, 2:4],
                                                         far[0:w].unsqueeze(1).to_broadcast([w, 2, PH * TOPK]), ALU.mult))
                    step(v, dve, nc.vector.tensor_tensor(partf[0:w, 0:2], partf[0:w, 0:2], partf[0:w, 2:4], ALU.add))
                    step(v, dve, nc.vector.scalar_tensor_tensor(
                        out=partf[0:w, 0], in0=far[0:w], scalar=float(NEAR - NEAR * TOPK // FEW), in1=partf[0:w, 0],
                        op0=ALU.mult, op1=ALU.add))
                    for c in range(2):
                        eq = (sums if c == 0 else other)[0:w].rearrange("p h (k a) -> p h k a", k=TOPK)
                        step(v, dve, nc.vector.tensor_tensor(
                            eq, keep.iota[0:w, 0:TOPK].unsqueeze(1).unsqueeze(1).to_broadcast([w, PH, TOPK, TOPK]),
                            partf[0:w, c].rearrange("p (h k) -> p h k", h=PH).unsqueeze(3)
                            .to_broadcast([w, PH, TOPK, TOPK]), ALU.is_equal))
                        between()
                        step(v, dve, nc.vector.tensor_tensor(
                            eq, eq, two(atf, c).unsqueeze(2).to_broadcast([w, PH, TOPK, TOPK]), ALU.mult))
                        between()
                        nc.vector.tensor_reduce(pick[0:w, c].rearrange("p (h k) -> p h k", h=PH), eq, AX.X, ALU.add)
                        between()

                def weights(i, w):
                    wgt = pick[0:w, 2].rearrange("p (h k) -> p h k", h=PH)
                    v.wait_ge(exp_done, i + 1)
                    step(v, dve, nc.vector.tensor_reduce(den[0:w], wgt, AX.X, ALU.add))
                    step(v, dve, nc.vector.reciprocal(rden[0:w], den[0:w]))
                    nc.vector.tensor_tensor(wgt, wgt, rden[0:w].unsqueeze(2).to_broadcast([w, PH, TOPK]),
                                            ALU.mult).then_inc(picked, 1)
                    v.wait_ge(pick_turned, i + 1)
                    v.wait_ge(spread, NGT * i + SLOTS)
                    nc.vector.tensor_copy(pickT[:, 0:3, 0:w], pp[:, 0:3 * P].rearrange("p (n t) -> p n t", n=3)[:, :, 0:w])
                    nc.vector.tensor_scalar(pickT[:, 3, 0:w], pp[:, 2 * P:2 * P + w], -1.0, None, ALU.mult
                                            ).then_inc(pick_out, 1)
                    v.wait_ge(pick_out, i + 1)
                    hold(v, held)

                def tile(i, w):
                    groups = iter(range(NGT))

                    def between():
                        g = next(groups, None)
                        if g is not None:
                            rows(i - 1, g)
                    search(i, w, between)
                    for g in groups:
                        rows(i - 1, g)
                    weights(i, w)

                PER = 20
                search(0, P, lambda: None)
                weights(0, P)
                with v.Fori(1, NT) as i:
                    dve.turn(i - 1, PER)
                    tile(i, P)
                dve.turned(NT - 1)
                tile(NT, TS)
                for g in range(TS // GT):
                    rows(NT, g)

            @block.scalar
            def _(act):
                act.sem_inc(g_out, SLOTS)
                act.sem_inc(last_done, SLOTS)

                def tile(i, w):
                    act.wait_ge(shifted, i + 1)
                    nc.scalar.activation(pick[0:w, 2], pick[0:w, 2], ACT.Exp).then_inc(exp_done, 1)
                    act.wait_ge(pick_out, i + 1)

                    def make(q, u):
                        g = SLOTS * q + u
                        col = ds(GT * g + GT - 1, 1)
                        act.wait_ge(last_done, NGT * i + g + 1)
                        for n in range(2):
                            x = nc.scalar.activation(off[:, n, u], keep.iota[:], ACT.Abs, scale=-1.0,
                                                     bias=pickT[:, n, col])
                        x.then_inc(off_done, 1)
                        act.wait_ge(off_done, NGT * i + g + 1)
                        act.wait_ge(spread, NGT * i + g + 1)
                        nc.scalar.activation(hot1[:, u, GT - 1], off[:, 0, u], ACT.Relu, scale=pickT[:, 3, col],
                                             bias=pickT[:, 2, col])
                        nc.scalar.activation(hot2[:, u, GT - 1], off[:, 1, u], ACT.Relu, scale=-1.0,
                                             bias=keep.ones[:, 0:1]).then_inc(last_done, 1)

                    def leave(h, q, u, r):
                        act.wait_ge(spread, NGT * i + SLOTS * q + u + SLOTS + 1)
                        act.wait_ge(stored[h], 16 * i + 16)
                        nc.scalar.activation(G[:, h, :, ds(GT * (SLOTS * r + u), GT)],
                                             pG[:, u].rearrange("p t i -> p i t"), ACT.Copy).then_inc(g_out, 1)

                    parts = 2 if w == P else 1
                    turns = w // parts // GT // SLOTS
                    for u in range(SLOTS):
                        make(0, u)
                    for h in range(parts):
                        with act.Fori(0, turns - 1) as r:
                            for u in range(SLOTS):
                                leave(h, turns * h + r, u, r)
                                make(turns * h + r + 1, u)
                        for u in range(SLOTS):
                            leave(h, turns * h + turns - 1, u, turns - 1)
                            if h + 1 < parts:
                                make(turns * (h + 1), u)
                each(act, tile)

            @block.gpsimd
            def _(pool):
                pool.sem_inc(hot2_done, 1)

                def tile(i, w):
                    pool.wait_ge(pick_out, i + 1)
                    hold(pool, pool_held)

                    def turn(h, q, r):
                        g = SLOTS * q
                        pool.wait_ge(hot2_done, NGT * i + g + 1)
                        hold(pool, pool_held)
                        nc.gpsimd.tensor_copy(second[:].rearrange("p s t -> p (s t)"),
                                              pickT[:, 1, ds(GT * g, GT * SLOTS)]).then_inc(second_done, 1)
                        pool.wait_ge(second_done, NGT // SLOTS * i + q + 1)
                        hold(pool, pool_held)
                        for u in range(SLOTS):
                            pool.wait_ge(spread, NGT * i + g + u + 1)
                            hold(pool, pool_held)
                            for t in range(GT - 1):
                                x = nc.gpsimd.tensor_scalar(hot2[:, u, t], keep.iota[:], second[:, u, t:t + 1], None,
                                                            ALU.is_equal)
                            x.then_inc(hot2_done, 1)
                    halves(pool, w, turn)
                each(pool, tile)

            @block.tensor
            def _(pe):
                pe.sem_inc(spread, SLOTS)

                def tile(i, w):
                    pe.wait_ge(picked, i + 1)
                    for n in range(3):
                        x = nc.tensor.transpose(pp[:, n * P:n * P + w], pick[0:w, n], keep.ident[0:w, 0:w])
                    x.then_inc(pick_turned, 1)

                    def turn(h, q, r):
                        g = SLOTS * q
                        for u in range(SLOTS):
                            pe.wait_ge(hot1_done, NGT * i + g + u + 1)
                            pe.wait_ge(hot2_done, NGT * i + g + u + 2)
                            pe.wait_ge(last_done, NGT * i + g + u + SLOTS + 1)
                            pe.wait_ge(g_out, NGT * i + g + u + 1)
                            for t in range(GT):
                                x = nc.tensor.matmul(pG[:, u, t], hot2[:, u, t], hot1[:, u, t], start=True, stop=True)
                            x.then_inc(spread, 1)
                    halves(pe, w, turn)
                each(pe, tile)


def peer_experts(nc, io, keep):
    with ExitStack() as ctx:
        def sb(name, shape, dt=F32):
            return ctx.enter_context(nc.sbuf_tensor(name, shape, dt))

        uu = sb("e_u", [P, 2, D])
        vv = sb("e_v", [P, 2, D])
        G = sb("e_G", [P, 2, T])
        uh = sb("e_uh", [P, 2, KC, P], F32R)
        ul = sb("e_ul", [P, 2, KC, P], F32R)
        vh = sb("e_vh", [P, 2, D], F32R)
        vl = sb("e_vl", [P, 2, D], F32R)
        act_out = sb("e_act", [P, NBK, W])
        ph = sb("e_ph", [P, 2, T], F32R)
        pl = sb("e_pl", [P, 2, T], F32R)
        pu = ctx.enter_context(nc.psum_tensor("e_pu", [P, 512], F32))
        pa = ctx.enter_context(nc.psum_tensor("e_pa", [P, NBK, 512], F32))
        po = ctx.enter_context(nc.psum_tensor("e_po", [P, 4, 512], F32))
        acc = keep.OT

        u_in = [nc.alloc_semaphore(f"e_u_in{u}") for u in range(2)]
        v_in = [nc.alloc_semaphore(f"e_v_in{u}") for u in range(2)]
        g_in = [nc.alloc_semaphore(f"e_g_in{u}") for u in range(2)]
        u_turned = nc.alloc_semaphore("e_u_turned")
        uh_done = nc.alloc_semaphore("e_uh_done")
        ul_done = nc.alloc_semaphore("e_ul_done")
        vh_done = nc.alloc_semaphore("e_vh_done")
        vl_done = nc.alloc_semaphore("e_vl_done")
        dotted = nc.alloc_semaphore("e_dotted")
        gelu_done = nc.alloc_semaphore("e_gelu_done")
        p_done = nc.alloc_semaphore("e_p_done")
        ph_done = nc.alloc_semaphore("e_ph_done")
        pl_done = nc.alloc_semaphore("e_pl_done")
        summed = nc.alloc_semaphore("e_summed")
        added = nc.alloc_semaphore("e_added")
        held = nc.alloc_semaphore("e_held")
        zeroed = nc.alloc_semaphore("e_zeroed")
        win_out = nc.alloc_semaphore("e_win_out")
        NP = NK // 2
        OUTS = KC * NBK
        SHARES = 28
        SHARE = (PAST - SQ) // SHARES
        assert SHARES * SHARE == PAST - SQ and 2 * SHARES < NP
        states = [io[n][0].rearrange("b r h e -> b r (h e)") for n in ("state_k_win", "state_v_win")]
        wins = [io[n][0].rearrange("b r h e -> b r (h e)") for n in ("k_win_sample", "v_win_sample")]
        uview = io["peer_u"][0].rearrange("(c e) d -> c e d", e=NK)
        vview = io["peer_v"][0].rearrange("(c e) d -> c e d", e=NK)

        def row(view, c):
            return view[ds(c, 1)].rearrange("a e d -> (a e) d")

        with nc.Block() as block:
            @block.sync
            def _(sp):
                for u in range(2):
                    sp.dma_start(uu[:, u], uview[u]).then_inc(u_in[u], 16)
                    sp.dma_start(G[:, u], io["s_g"][u]).then_inc(g_in[u], 16)
                    sp.dma_start(vv[:, u], vview[u]).then_inc(v_in[u], 16)

                def next_pair(i):
                    for u in range(2):
                        c = 2 * i + u
                        sp.wait_ge(u_turned, 2 * c + 2)
                        sp.dma_start(uu[:, u], row(uview, c + 2)).then_inc(u_in[u], 16)
                        sp.wait_ge(vl_done, c + 1)
                        sp.dma_start(vv[:, u], row(vview, c + 2)).then_inc(v_in[u], 16)
                    for u in range(2):
                        c = 2 * i + u
                        sp.wait_ge(p_done, NBK * c + NBK)
                        sp.dma_start(G[:, u], row(io["s_g"], c + 2)).then_inc(g_in[u], 16)

                with sp.Fori(0, SHARES) as j:
                    for t in range(2):
                        sp.dma_start(wins[t][:, ds(j * SHARE, SHARE)], states[t][:, ds(j * SHARE + SQ, SHARE)]
                                     ).then_inc(win_out, 16)
                        next_pair(2 * j + t)
                with sp.Fori(2 * SHARES, NP - 1) as i:
                    next_pair(i)
                sp.wait_ge(win_out, 16 * 2 * SHARES)

            @block.tensor
            def _(pe):
                pe.sem_inc(summed, 1)

                def turn_u(i, u, n):
                    c = 2 * i + u
                    pe.wait_ge(u_in[u], 16 * i + 16)
                    pe.wait_ge(ul_done, 2 * c + n + 1)
                    for k in range(4):
                        x = nc.tensor.transpose(pu[:, k * P:(k + 1) * P], uu[:, u, (4 * n + k) * P:(4 * n + k + 1) * P],
                                                keep.ident[:])
                    x.then_inc(u_turned, 1)

                def dot(i, u, blocks):
                    c = 2 * i + u
                    pe.wait_ge(ul_done, 2 * c + 3)
                    for b in blocks:
                        pe.wait_ge(gelu_done, NBK * c + b + 1)
                        cols = slice(b * W, (b + 1) * W)
                        for k in range(KC):
                            x = split_product(nc, pa[:, b, 0:W], uh[:, u, k], ul[:, u, k], keep.hi[:, k, cols],
                                              keep.lo[:, k, cols], k == 0, k == KC - 1)
                        x.then_inc(dotted, 1)

                def out(i, blocks):
                    pe.wait_ge(vl_done, 2 * i + 2)
                    n = KC * blocks[0]
                    for b in blocks:
                        cols = slice(b * W, (b + 1) * W)
                        pe.wait_ge(pl_done, NBK * (2 * i + 1) + b + 1 + NBK)
                        for k in range(KC):
                            pe.wait_ge(added, OUTS * i + n + 1)
                            for u in range(2):
                                x = split_product(nc, po[:, n % 4, 0:W], vh[:, u, k * P:(k + 1) * P],
                                                  vl[:, u, k * P:(k + 1) * P], ph[:, u, cols], pl[:, u, cols],
                                                  u == 0, u == 1)
                            x.then_inc(summed, 1)
                            n += 1

                ALL = range(NBK)
                for u in range(2):
                    for n in range(2):
                        turn_u(0, u, n)
                with pe.Fori(0, NP - 1) as i:
                    dot(i, 0, ALL)
                    turn_u(i + 1, 0, 0)
                    dot(i, 1, ALL[:1])
                    turn_u(i + 1, 0, 1)
                    dot(i, 1, ALL[1:])
                    turn_u(i + 1, 1, 0)
                    out(i, ALL[:1])
                    turn_u(i + 1, 1, 1)
                    out(i, ALL[1:])
                for u in range(2):
                    dot(NP - 1, u, ALL)
                out(NP - 1, ALL)

            @block.scalar
            def _(act):
                act.sem_inc(gelu_done, NBK)

                def copy_u(i, u, n):
                    act.wait_ge(u_turned, 2 * (2 * i + u) + n + 1)
                    nc.scalar.activation(uh[:, u, 4 * n:4 * n + 4], pu[:].rearrange("p (k e) -> p k e", k=4),
                                         ACT.Copy).then_inc(uh_done, 1)

                def gelus(i, u, blocks):
                    c = 2 * i + u
                    for b in blocks:
                        act.wait_ge(dotted, NBK * c + b + 1)
                        act.wait_ge(pl_done, NBK * c + b + 1)
                        nc.scalar.activation(act_out[:, b], pa[:, b, 0:W], ACT.Gelu).then_inc(gelu_done, 1)
                        act.wait_ge(p_done, NBK * c + b + 1)
                        nc.scalar.activation(ph[:, u, b * W:(b + 1) * W], act_out[:, b], ACT.Copy).then_inc(ph_done, 1)

                ALL = range(NBK)
                for u in range(2):
                    for n in range(2):
                        copy_u(0, u, n)
                with act.Fori(0, NP - 1) as i:
                    gelus(i, 0, ALL)
                    copy_u(i + 1, 0, 0)
                    gelus(i, 1, ALL[:1])
                    copy_u(i + 1, 0, 1)
                    gelus(i, 1, ALL[1:])
                    for n in range(2):
                        copy_u(i + 1, 1, n)
                for u in range(2):
                    gelus(NP - 1, u, ALL)

            @block.vector
            def _(v):
                v.sem_inc(ul_done, 1)
                v.sem_inc(pl_done, NBK)
                v.sem_inc(added, 4)

                def low_u(i, u, n):
                    v.wait_ge(uh_done, 2 * (2 * i + u) + n + 1)
                    part = slice(4 * n, 4 * n + 4)
                    nc.vector.tensor_tensor(ul[:, u, part], pu[:].rearrange("p (k e) -> p k e", k=4), uh[:, u, part],
                                            ALU.subtract).then_inc(ul_done, 1)

                def weigh(i, u, blocks):
                    c = 2 * i + u
                    v.wait_ge(g_in[u], 16 * i + 16)
                    for b in blocks:
                        cols = slice(b * W, (b + 1) * W)
                        v.wait_ge(gelu_done, NBK * c + b + 4)
                        nc.vector.tensor_tensor(act_out[:, b], act_out[:, b], G[:, u, cols], ALU.mult).then_inc(p_done, 1)
                        v.wait_ge(ph_done, NBK * c + b + 1)
                        nc.vector.tensor_tensor(pl[:, u, cols], act_out[:, b], ph[:, u, cols],
                                                ALU.subtract).then_inc(pl_done, 1)

                def add(i, blocks):
                    v.wait_ge(added, OUTS * i + 4)
                    n = KC * blocks[0]
                    for b in blocks:
                        cols = slice(b * W, (b + 1) * W)
                        for k in range(KC):
                            v.wait_ge(summed, OUTS * i + n + 2)
                            nc.vector.tensor_tensor(acc[:, k, cols], po[:, n % 4, 0:W], acc[:, k, cols],
                                                    ALU.add).then_inc(added, 1)
                            n += 1

                ALL = range(NBK)
                for u in range(2):
                    for n in range(2):
                        low_u(0, u, n)
                v.wait_ge(zeroed, 1)
                with v.Fori(0, NP - 1) as i:
                    weigh(i, 0, ALL)
                    low_u(i + 1, 0, 0)
                    weigh(i, 1, ALL[:1])
                    low_u(i + 1, 0, 1)
                    weigh(i, 1, ALL[1:])
                    low_u(i + 1, 1, 0)
                    add(i, ALL[:1])
                    low_u(i + 1, 1, 1)
                    add(i, ALL[1:])
                for u in range(2):
                    weigh(NP - 1, u, ALL)
                add(NP - 1, ALL)

            @block.gpsimd
            def _(pool):
                nc.gpsimd.memset(acc[:], 0.0).then_inc(zeroed, 1)
                with pool.Fori(0, NP) as i:
                    for u in range(2):
                        c = 2 * i + u
                        pool.wait_ge(v_in[u], 16 * i + 16)
                        pool.wait_ge(summed, OUTS * i + 1)
                        hold(pool, held)
                        nc.gpsimd.tensor_copy(vh[:, u], vv[:, u]).then_inc(vh_done, 1)
                        pool.wait_ge(vh_done, c + 1)
                        nc.gpsimd.tensor_tensor(vl[:, u], vv[:, u], vh[:, u], ALU.subtract).then_inc(vl_done, 1)


def finish(nc, io, keep):
    with ExitStack() as ctx:
        def sb(name, shape, dt=F32):
            return ctx.enter_context(nc.sbuf_tensor(name, shape, dt))

        xT = sb("f_xT", [P, KC, T])
        sq = sb("f_sq", [P, 2, T])
        rstd = sb("f_rstd", [P, T])
        y = sb("f_y", [P, 2, D])
        small = sb("f_small", [P, KC, TS])
        ps = ctx.enter_context(nc.psum_tensor("f_ps", [P, NBK, 512], F32))
        pt = ctx.enter_context(nc.psum_tensor("f_pt", [P, 2, 512], F32))
        x_in = nc.alloc_semaphore("f_x_in")
        added = nc.alloc_semaphore("f_added")
        squared = nc.alloc_semaphore("f_squared")
        summed = nc.alloc_semaphore("f_summed")
        mean_done = nc.alloc_semaphore("f_mean_done")
        rooted = nc.alloc_semaphore("f_rooted")
        normed = nc.alloc_semaphore("f_normed")
        turned = nc.alloc_semaphore("f_turned")
        y_out = [nc.alloc_semaphore(f"f_y_out{n}") for n in range(2)]
        stored = [nc.alloc_semaphore(f"f_stored{n}") for n in range(2)]
        dve = Steps(nc, "f_dve")
        GF = NMOD + 2 * KC

        def y_rows(i):
            return io["y_prompt"][0, i * P:(i + 1) * P, :] if i < NT else io["y_sample"].rearrange("b q d -> (b q) d")

        with nc.Block() as block:
            @block.sync
            def _(sp):
                sp.dma_start(xT[:], io["s_x"]).then_inc(x_in, 16)
                for i in range(NT + 1):
                    for n in range(2):
                        sp.wait_ge(y_out[n], i + 1)
                    sp.dma_start(y_rows(i), y[0:(P if i < NT else TS), i % 2]).then_inc(stored[i % 2], 16)
                for n in range(2):
                    sp.wait_ge(stored[n], 16 * ((NT + 2 - n) // 2))

            @block.vector
            def _(v):
                v.wait_ge(x_in, 16)
                for k in range(KC):
                    step(v, dve, nc.vector.tensor_tensor(by_seq(small[:, k]), by_seq(keep.OT[:, k, TP:T]),
                                                         seq_bcast(keep.mod[:, GATE2 * KC + k, 1:NCOND]), ALU.mult))
                    nc.vector.tensor_tensor(xT[:, k, TP:T], xT[:, k, TP:T], small[:, k], ALU.add)
                    nc.vector.scalar_tensor_tensor(out=xT[:, k, 0:TP], in0=keep.OT[:, k, 0:TP],
                                                   scalar=keep.mod[:, GATE2 * KC + k, 0:1], in1=xT[:, k, 0:TP],
                                                   op0=ALU.mult, op1=ALU.add).then_inc(added, 1)
                v.wait_ge(summed, KC)
                nc.vector.tensor_scalar(rstd[:].rearrange("p (b w) -> p b w", b=NBK), ps[:, :, 0:W], 1.0 / D, EPS,
                                        ALU.mult, ALU.add).then_inc(mean_done, 1)
                v.wait_ge(rooted, 1)
                step(v, dve, nc.vector.reciprocal(rstd[:], rstd[:]))
                for k in range(KC):
                    x = nc.vector.scalar_tensor_tensor(out=xT[:, k], in0=xT[:, k], scalar=keep.param[:, GF + k:GF + k + 1],
                                                       in1=rstd[:], op0=ALU.mult, op1=ALU.mult)
                    if k % 4 == 3:
                        x.then_inc(normed, 1)
                for i in range(NT + 1):
                    w = P if i < NT else TS
                    v.wait_ge(turned, 2 * i + 2)
                    if i >= 2:
                        v.wait_ge(stored[i % 2], 16 * (i // 2))
                    nc.vector.tensor_copy(y[0:w, i % 2, 512:D], pt[0:w, 1]).then_inc(y_out[1], 1)

            @block.scalar
            def _(act):
                for k in range(KC):
                    act.wait_ge(added, k + 1)
                    if k >= 2:
                        act.wait_ge(summed, k - 1)
                    nc.scalar.activation(sq[:, k % 2], xT[:, k], ACT.Square).then_inc(squared, 1)
                act.wait_ge(mean_done, 1)
                nc.scalar.activation(rstd[:], rstd[:], ACT.Sqrt).then_inc(rooted, 1)
                for i in range(NT + 1):
                    w = P if i < NT else TS
                    act.wait_ge(turned, 2 * i + 1)
                    if i >= 2:
                        act.wait_ge(stored[i % 2], 16 * (i // 2))
                    nc.scalar.activation(y[0:w, i % 2, 0:512], pt[0:w, 0], ACT.Copy).then_inc(y_out[0], 1)

            @block.tensor
            def _(pe):
                for k in range(KC):
                    pe.wait_ge(squared, k + 1)
                    for b in range(NBK):
                        x = nc.tensor.matmul(ps[:, b, 0:W], keep.ones[:], sq[:, k % 2, b * W:(b + 1) * W],
                                             start=(k == 0), stop=(k == KC - 1), skip_group_check=True)
                    x.then_inc(summed, 1)
                for i in range(NT + 1):
                    w = P if i < NT else TS
                    for n in range(2):
                        if i == 0:
                            pe.wait_ge(normed, n + 1)
                        else:
                            pe.wait_ge(y_out[n], i)
                        for k in range(4):
                            x = nc.tensor.transpose(pt[0:w, n, k * P:(k + 1) * P], xT[:, 4 * n + k, i * P:i * P + w],
                                                    keep.ident[:])
                        x.then_inc(turned, 1)


class Keep:
    pass


def run_stage(nc, io, keep, stage):
    before = nc.snapshot_sems()
    stage(nc, io, keep)
    nc.clear_and_free_semaphores(nc.allocated_since(before))
    nc.all_engine_barrier()


def build(nc, io):
    keep = Keep()
    with ExitStack() as ctx:
        def sb(name, shape, dt=F32):
            return ctx.enter_context(nc.sbuf_tensor(name, shape, dt))

        keep.ident = sb("k_ident", [P, P])
        keep.ones = sb("k_ones", [P, P])
        keep.iota = sb("k_iota", [P, NK])
        keep.param = sb("k_param", [P, NMOD + 3 * KC + 1])
        keep.mod = sb("k_mod", [P, NMOD, NCOND])
        keep.gs1 = sb("k_gs1", [P, KC, NCOND])
        keep.gs2 = sb("k_gs2", [P, KC, NCOND])
        keep.neglam = sb("k_neglam", [P, 1])
        keep.halves = sb("k_halves", [2 * CH * SQ, 2])
        keep.sign = sb("k_sign", [2 * CH * SQ, 2])
        with nc.sbuf_tensor("k_win", [P, KC, PROJ], F32) as keep.win:
            for stage in (modulation, project):
                run_stage(nc, io, keep, stage)
        keep.OT = sb("k_OT", [P, KC, T])
        for stage in (prompt_attn, sample_attn):
            run_stage(nc, io, keep, stage)
        keep.hi = sb("k_hi", [P, KC, T], F32R)
        keep.lo = sb("k_lo", [P, KC, T], F32R)
        for stage in (mix_out, peer_scores, peer_route, peer_experts, finish):
            run_stage(nc, io, keep, stage)


INPUTS = ["x_prompt", "x_sample", "cache_k_diff", "cache_v_diff", "state_k_win", "state_v_win", "page_table",
          "c_prompt", "c_sample", "ada_w", "ada_b", "norm_attn_g", "norm_ffn_g", "w_in", "w_o", "diff_lambda",
          "diff_subln_g", "peer_wq", "peer_keys", "peer_u", "peer_v", "final_norm_g"]
OUTPUTS = {
    "y_prompt": (1, TP, D), "y_sample": (NSEQ, SQ, D),
    "k_diff_prompt": (1, 1, TP, 4, 128), "v_diff_prompt": (1, 1, TP, 4, 128),
    "k_win_prompt": (1, 1, TP, 8, 64), "v_win_prompt": (1, 1, TP, 8, 64),
    "k_diff_sample": (1, NSEQ, SQ, 4, 128), "v_diff_sample": (1, NSEQ, SQ, 4, 128),
    "k_win_sample": (1, NSEQ, PAST, 8, 64), "v_win_sample": (1, NSEQ, PAST, 8, 64),
}
SCRATCH = {"s_proj": (T, PROJ), "s_x": (P, KC, T), "s_s": (T, NHC, NK), "s_g": (NK, NK, T)}


def kernel(**inputs):
    import concourse.bacc as bacc
    from concourse.bass_utils import run_bass_kernel_spmd

    nc = bacc.Bacc("TRN2", target_bir_lowering=False, num_devices=1)
    arrays = {name: np.ascontiguousarray(inputs[name]) for name in INPUTS} | host_tables()
    io = {name: nc.dram_tensor(name, a.shape, mybir.dt.from_np(a.dtype), kind="ExternalInput").ap()
          for name, a in arrays.items()}
    for name, shape in OUTPUTS.items():
        io[name] = nc.dram_tensor(name, shape, F32, kind="ExternalOutput").ap()
    for name, shape in SCRATCH.items():
        io[name] = nc.dram_tensor(name, shape, F32).ap()
    build(nc, io)
    got = run_bass_kernel_spmd(nc, [arrays], core_ids=[0]).results[0]
    return tuple(got[name] for name in OUTPUTS)
```
